# Optimizing a Trainium2 kernel written in Bass

```python
import jax, jax.numpy as jnp
from jax import lax
import numpy as np

D_MODEL = 1024
BATCH = 1
SEQ = 512
DEPTH = 2
DEC_BATCH = 8
DEC_SEQ = 4
PAST_LEN = 256
PAGE_SIZE = 128

N_A = DEPTH // 2
N_B = DEPTH - N_A
RWKV_HEAD_DIM = 64
RWKV_HEADS = D_MODEL // RWKV_HEAD_DIM
DECAY_LORA = 64
AAA_LORA = 64
MV_LORA = 32
GATE_LORA = 160
NSA_HEADS = 16
NSA_KV_HEADS = 4
NSA_HEAD_DIM = D_MODEL // NSA_HEADS
NSA_GROUP = NSA_HEADS // NSA_KV_HEADS
CMP_STRIDE = 16
CMP_LEN = 32
CMP_R = CMP_LEN // CMP_STRIDE
CMP_HIDDEN = 256
SEL_BLOCK = 64
SEL_TOP = 16
WINDOW = 512
Q_BLOCK = 64
N_GROUPS = 4
GROUP_EXPERTS = 4
N_EXPERTS = N_GROUPS * GROUP_EXPERTS
EXPERT_TOP = 2
EXPERT_FF = 512
NORM_EPS = 1e-6
LNX_EPS = 64e-5
NEG = -1e30

kernel_name = 'yoco_rwkv7_nsa_hmoe_step'

def rms_norm(x, g):
    xf = x.astype(jnp.float32)
    y = xf * lax.rsqrt(jnp.mean(xf * xf, axis=-1, keepdims=True) + NORM_EPS)
    return (y * g.astype(jnp.float32)).astype(x.dtype)

def modulate(h, shift, scale):
    return h * (1 + scale[:, None, :]) + shift[:, None, :]

def masked_softmax(s, mask):
    return jax.nn.softmax(jnp.where(mask, s, NEG), axis=-1) * mask

def alibi_slopes():
    h = jnp.arange(1, NSA_HEADS + 1, dtype=jnp.float32)
    return jnp.exp2(-8.0 * h / NSA_HEADS).reshape(NSA_KV_HEADS, NSA_GROUP)

def wkv7_scan(r, w, k, v, a, b, s0):
    def step(s, inp):
        r_t, w_t, k_t, v_t, a_t, b_t = inp
        sa = jnp.einsum('bhij,bhj->bhi', s, a_t)
        s = s * w_t[:, :, None, :] + sa[..., None] * b_t[:, :, None, :] + v_t[..., None] * k_t[:, :, None, :]
        return s, jnp.einsum('bhij,bhj->bhi', s, r_t)
    xs = tuple(jnp.moveaxis(z.astype(jnp.float32), 1, 0) for z in (r, w, k, v, a, b))
    s, ys = lax.scan(step, s0.astype(jnp.float32), xs)
    return jnp.moveaxis(ys, 0, 1), s

def rwkv7_time_mix(h, shift_prev, s0, v_first, P, l):
    B, T, C = h.shape
    heads = lambda z: z.reshape(B, T, RWKV_HEADS, RWKV_HEAD_DIM)
    xx = jnp.concatenate([shift_prev.astype(h.dtype)[:, None, :], h[:, :-1]], axis=1) - h
    xm = h[None] + xx[None] * P['rwkv_mix'][l][:, None, None, :]
    rkv = jnp.einsum('sbtc,scd->sbtd', xm[:3], P['rwkv_w_rkv'][l])
    r, k, v = rkv[0], rkv[1], rkv[2]
    w = -jax.nn.softplus(-(P['rwkv_w0'][l] + jnp.tanh(xm[3] @ P['rwkv_w1'][l]) @ P['rwkv_w2'][l])) - 0.5
    if v_first is None:
        v_first = v
    else:
        v = v + (v_first - v) * jax.nn.sigmoid(P['rwkv_v0'][l - 1] + (xm[2] @ P['rwkv_v1'][l - 1]) @ P['rwkv_v2'][l - 1])
    a = jax.nn.sigmoid(P['rwkv_a0'][l] + (xm[4] @ P['rwkv_a1'][l]) @ P['rwkv_a2'][l])
    g = jax.nn.sigmoid(xm[5] @ P['rwkv_g1'][l]) @ P['rwkv_g2'][l]
    kk = heads(k * P['rwkv_k_k'][l]).astype(jnp.float32)
    kk = kk * lax.rsqrt(jnp.maximum(jnp.sum(kk * kk, axis=-1, keepdims=True), 1e-24))
    k = k * (1 + (a - 1) * P['rwkv_k_a'][l])
    a_h = heads(a).astype(jnp.float32)
    decay = jnp.exp(-jnp.exp(heads(w).astype(jnp.float32)))
    y, s = wkv7_scan(heads(r), decay, heads(k), heads(v), -kk, kk * a_h, s0)
    mu = jnp.mean(y, axis=-1, keepdims=True)
    var = jnp.mean(jnp.square(y - mu), axis=-1, keepdims=True)
    yn = ((y - mu) * lax.rsqrt(var + LNX_EPS)).reshape(B, T, C) * P['rwkv_lnx_w'][l] + P['rwkv_lnx_b'][l]
    bonus = jnp.sum(heads(r).astype(jnp.float32) * heads(k).astype(jnp.float32) * P['rwkv_r_k'][l], axis=-1, keepdims=True) * heads(v).astype(jnp.float32)
    out = ((yn + bonus.reshape(B, T, C)).astype(h.dtype) * g) @ P['rwkv_w_o'][l]
    return out, v_first, h[:, -1], s.astype(s0.dtype)

def hier_moe(h, P, l):
    B, T, C = h.shape
    hf = h.reshape(B * T, C)
    grp_logits = (hf @ P['moe_w_grp'][l] + P['moe_b_grp'][l]).astype(jnp.float32)
    grp = jnp.argmax(grp_logits, axis=-1)
    p_grp = jnp.take_along_axis(jax.nn.softmax(grp_logits, axis=-1), grp[:, None], axis=-1)
    exp_logits = (hf @ P['moe_w_exp'][l] + P['moe_b_exp'][l]).astype(jnp.float32).reshape(-1, N_GROUPS, GROUP_EXPERTS)
    in_grp = jnp.take_along_axis(exp_logits, grp[:, None, None], axis=1)[:, 0]
    top_val, top_idx = lax.top_k(in_grp, EXPERT_TOP)
    w_top = jax.nn.softmax(top_val, axis=-1) * p_grp
    eid = grp[:, None] * GROUP_EXPERTS + top_idx
    combine = jnp.einsum('nk,nke->ne', w_top, jax.nn.one_hot(eid, N_EXPERTS, dtype=jnp.float32)).astype(h.dtype)
    out = jnp.zeros_like(hf)
    for e in range(N_EXPERTS):
        act = jax.nn.silu(hf @ P['moe_w_gate'][l, e]) * (hf @ P['moe_w_up'][l, e])
        out = out + combine[:, e:e + 1] * (act @ P['moe_w_down'][l, e])
    return out.reshape(B, T, C)

def shared_kv(x, c_act, P):
    B, T, _ = x.shape
    sh, sc = jnp.split(c_act @ P['kv_ada_w'] + P['kv_ada_b'], 2, axis=-1)
    hk = modulate(rms_norm(x, P['kv_norm_g']), sh, sc)
    return (hk @ P['w_kv']).reshape(B, T, 6, NSA_KV_HEADS, NSA_HEAD_DIM)

def compress(kc, vc, cmp_pos, cmp_w1, cmp_b1, cmp_w2):
    B, T = kc.shape[:2]
    n_ch = T // CMP_STRIDE
    nc = n_ch - CMP_R + 1
    kv = jnp.stack([kc, vc])[:, :, :n_ch * CMP_STRIDE]
    kv = kv.reshape(2, B, n_ch, CMP_STRIDE, NSA_KV_HEADS, NSA_HEAD_DIM)
    w1 = cmp_w1.reshape(2, CMP_R, CMP_STRIDE, NSA_HEAD_DIM, CMP_HIDDEN)
    part = jnp.einsum('zbnsgd,zrsdh->zrbngh', kv, w1)
    pos_term = jnp.einsum('zrsd,zrsdh->zh', cmp_pos.reshape(2, CMP_R, CMP_STRIDE, NSA_HEAD_DIM), w1) + cmp_b1
    hid = pos_term[:, None, None, None, :]
    for r in range(CMP_R):
        hid = hid + part[:, r, :, r:r + nc]
    out = jnp.einsum('zbngh,zhd->zbngd', jax.nn.gelu(hid), cmp_w2)
    return out[0], out[1]

def selection_blocks(ks, vs):
    B, T = ks.shape[:2]
    nb = -(-T // SEL_BLOCK)
    kv = jnp.pad(jnp.stack([ks, vs]), ((0, 0), (0, 0), (0, nb * SEL_BLOCK - T), (0, 0), (0, 0)))
    kv = kv.reshape(2, B, nb, SEL_BLOCK, NSA_KV_HEADS, NSA_HEAD_DIM).transpose(0, 1, 4, 2, 3, 5)
    return kv[0], kv[1]

def overlap_matrix(nc, nb):
    st = jnp.arange(nc, dtype=jnp.int32) * CMP_STRIDE
    bs = jnp.arange(nb, dtype=jnp.int32) * SEL_BLOCK
    ov = (st[:, None] <= bs[None, :] + SEL_BLOCK - 1) & (st[:, None] + CMP_LEN - 1 >= bs[None, :])
    return ov.astype(jnp.float32)

def branch_context(kv4, cmp_pos, cmp_w1, cmp_b1, cmp_w2):
    kc, vc = compress(kv4[:, :, 0], kv4[:, :, 1], cmp_pos, cmp_w1, cmp_b1, cmp_w2)
    nc = kc.shape[1]
    cmp_end = jnp.arange(nc, dtype=jnp.int32) * CMP_STRIDE + (CMP_LEN - 1)
    ksb, vsb = selection_blocks(kv4[:, :, 2], kv4[:, :, 3])
    return kc, vc, cmp_end, ksb, vsb, overlap_matrix(nc, ksb.shape[2])

def nsa_attend(q, gates, q_pos, kc, vc, cmp_end, ksb, vsb, overlap, kw, vw, w_pos):
    B, Tq = q.shape[:2]
    G, Hg, Dh = NSA_KV_HEADS, NSA_GROUP, NSA_HEAD_DIM
    qg = q.reshape(B, Tq, G, Hg, Dh).astype(jnp.float32) * (Dh ** -0.5)
    slope = alibi_slopes()[None, None, :, :, None]
    d_c = (q_pos[:, None] - cmp_end[None, :])[None, :, None, None, :]
    s_c = jnp.einsum('bqgpd,bngd->bqgpn', qg, kc.astype(jnp.float32)) - slope * d_c
    p_c = masked_softmax(s_c, d_c >= 0)
    o_c = jnp.einsum('bqgpn,bngd->bqgpd', p_c, vc.astype(jnp.float32))
    nb = ksb.shape[2]
    blk = jnp.arange(nb, dtype=jnp.int32)[None, :]
    cur = (q_pos // SEL_BLOCK)[:, None]
    valid = blk * SEL_BLOCK <= q_pos[:, None]
    forced = (blk == 0) | (blk == cur) | (blk == cur - 1)
    imp = jnp.einsum('bqgpn,nj->bqgj', p_c, overlap)
    score = jnp.where(valid[None, :, None, :], jnp.where(forced[None, :, None, :], -NEG, imp), NEG)
    n_top = min(SEL_TOP, nb)
    _, idx = lax.top_k(score, n_top)
    bi = jnp.arange(B)[:, None, None, None]
    gi = jnp.arange(G)[None, None, :, None]
    k_s = ksb[bi, gi, idx].reshape(B, Tq, G, n_top * SEL_BLOCK, Dh).astype(jnp.float32)
    v_s = vsb[bi, gi, idx].reshape(B, Tq, G, n_top * SEL_BLOCK, Dh).astype(jnp.float32)
    pos = (idx[..., None] * SEL_BLOCK + jnp.arange(SEL_BLOCK, dtype=jnp.int32)).reshape(B, Tq, G, n_top * SEL_BLOCK)
    d_s = (q_pos[None, :, None, None] - pos)[:, :, :, None, :]
    s_s = jnp.einsum('bqgpd,bqgkd->bqgpk', qg, k_s) - slope * d_s
    p_s = masked_softmax(s_s, d_s >= 0)
    o_s = jnp.einsum('bqgpk,bqgkd->bqgpd', p_s, v_s)
    d_w = q_pos[:, None] - w_pos[None, :]
    m_w = ((d_w >= 0) & (d_w < WINDOW) & (w_pos[None, :] >= 0))[None, :, None, None, :]
    s_w = jnp.einsum('bqgpd,bwgd->bqgpw', qg, kw.astype(jnp.float32)) - slope * d_w[None, :, None, None, :]
    p_w = masked_softmax(s_w, m_w)
    o_w = jnp.einsum('bqgpw,bwgd->bqgpd', p_w, vw.astype(jnp.float32))
    g = gates.reshape(B, Tq, G, Hg, 3).astype(jnp.float32)
    o = g[..., 0:1] * o_c + g[..., 1:2] * o_s + g[..., 2:3] * o_w
    return o.reshape(B, Tq, G * Hg * Dh).astype(q.dtype)

def prompt_attend(q, gates, ctx, kvw_pad):
    B, T = q.shape[:2]
    n_qb = T // Q_BLOCK
    span = WINDOW + Q_BLOCK
    qb = jnp.swapaxes(q.reshape(B, n_qb, Q_BLOCK, NSA_HEADS, NSA_HEAD_DIM), 0, 1)
    gb = jnp.swapaxes(gates.reshape(B, n_qb, Q_BLOCK, NSA_HEADS, 3), 0, 1)

    def one_block(args):
        i, q_i, g_i = args
        start = i * Q_BLOCK
        kvw = lax.dynamic_slice_in_dim(kvw_pad, start, span, axis=1)
        q_pos = start + jnp.arange(Q_BLOCK, dtype=jnp.int32)
        w_pos = start - WINDOW + jnp.arange(span, dtype=jnp.int32)
        return nsa_attend(q_i, g_i, q_pos, *ctx, kvw[:, :, 0], kvw[:, :, 1], w_pos)

    out = lax.map(one_block, (jnp.arange(n_qb, dtype=jnp.int32), qb, gb))
    return jnp.swapaxes(out, 0, 1).reshape(B, T, -1)

def nsa_mix(h, w_qg, w_o, attend):
    B, T, _ = h.shape
    qg = h @ w_qg
    q = qg[..., :NSA_HEADS * NSA_HEAD_DIM].reshape(B, T, NSA_HEADS, NSA_HEAD_DIM)
    gates = jax.nn.sigmoid(qg[..., NSA_HEADS * NSA_HEAD_DIM:].astype(jnp.float32)).reshape(B, T, NSA_HEADS, 3)
    return attend(q, gates) @ w_o

def run_trunk(x, c, shift0, wkv0, make_attend, P):
    c_act = jax.nn.silu(c)
    v_first, attend, kv = None, None, None
    shifts, states = [], []
    for l in range(DEPTH):
        sh1, sc1, gt1, sh2, sc2, gt2 = jnp.split(c_act @ P['ada_w'][l] + P['ada_b'][l], 6, axis=-1)
        h = modulate(rms_norm(x, P['norm_mix_g'][l]), sh1, sc1)
        if l < N_A:
            out, v_first, last_h, s = rwkv7_time_mix(h, shift0[l], wkv0[l], v_first, P, l)
            shifts.append(last_h)
            states.append(s)
        else:
            out = nsa_mix(h, P['nsa_w_qg'][l - N_A], P['nsa_w_o'][l - N_A], attend)
        x = x + gt1[:, None, :] * out
        h = modulate(rms_norm(x, P['norm_ffn_g'][l]), sh2, sc2)
        x = x + gt2[:, None, :] * hier_moe(h, P, l)
        if l == N_A - 1:
            kv = shared_kv(x, c_act, P)
            attend = make_attend(kv)
    return rms_norm(x, P['norm_f_g']), kv, jnp.stack(shifts), jnp.stack(states)

def setup_inputs(seed: int = 0) -> dict:
    key = jax.random.key(seed)
    keys = iter(jax.random.split(key, 64))

    def nrm(shape, scale, offset=0.0):
        return offset + scale * jax.random.normal(next(keys), shape, jnp.float32)

    D = D_MODEL
    G, Dh = NSA_KV_HEADS, NSA_HEAD_DIM
    H, N = RWKV_HEADS, RWKV_HEAD_DIM
    n_pages = PAST_LEN // PAGE_SIZE
    n_used = DEC_BATCH * n_pages
    n_pool = n_used + max(1, n_used // 4)
    page_table = jax.random.permutation(next(keys), n_pool)[:n_used].reshape(DEC_BATCH, n_pages).astype(jnp.int32)
    wb = min(WINDOW, PAST_LEN)
    return {
        'x_prompt': nrm((BATCH, SEQ, D), 1.0),
        'x_sample': nrm((DEC_BATCH, DEC_SEQ, D), 1.0),
        'cache_nsa_kv': nrm((n_pool, PAGE_SIZE, 4, G, Dh), 1.0),
        'cache_win_kv': nrm((DEC_BATCH, wb, 2, G, Dh), 1.0),
        'state_wkv': nrm((N_A, DEC_BATCH, H, N, N), 0.3),
        'state_shift': nrm((N_A, DEC_BATCH, D), 1.0),
        'page_table': page_table,
        'c_prompt': nrm((BATCH, D), 1.0),
        'c_sample': nrm((DEC_BATCH, D), 1.0),
        'ada_w': nrm((DEPTH, D, 6 * D), 0.5 * D ** -0.5),
        'ada_b': nrm((DEPTH, 6 * D), 0.02),
        'norm_mix_g': nrm((DEPTH, D), 0.02, 1.0),
        'norm_ffn_g': nrm((DEPTH, D), 0.02, 1.0),
        'norm_f_g': nrm((D,), 0.02, 1.0),
        'rwkv_mix': jax.random.uniform(next(keys), (N_A, 6, D), jnp.float32),
        'rwkv_w_rkv': nrm((N_A, 3, D, D), D ** -0.5),
        'rwkv_w0': nrm((N_A, D), 0.5, -1.0),
        'rwkv_w1': nrm((N_A, D, DECAY_LORA), D ** -0.5),
        'rwkv_w2': nrm((N_A, DECAY_LORA, D), 0.1 * DECAY_LORA ** -0.5),
        'rwkv_a0': nrm((N_A, D), 0.1),
        'rwkv_a1': nrm((N_A, D, AAA_LORA), D ** -0.5),
        'rwkv_a2': nrm((N_A, AAA_LORA, D), 0.1 * AAA_LORA ** -0.5),
        'rwkv_v0': nrm((N_A - 1, D), 0.5),
        'rwkv_v1': nrm((N_A - 1, D, MV_LORA), D ** -0.5),
        'rwkv_v2': nrm((N_A - 1, MV_LORA, D), 0.5 * MV_LORA ** -0.5),
        'rwkv_g1': nrm((N_A, D, GATE_LORA), D ** -0.5),
        'rwkv_g2': nrm((N_A, GATE_LORA, D), GATE_LORA ** -0.5),
        'rwkv_k_k': nrm((N_A, D), 0.05, 0.85),
        'rwkv_k_a': nrm((N_A, D), 0.05, 1.0),
        'rwkv_r_k': nrm((N_A, H, N), 0.1),
        'rwkv_lnx_w': nrm((N_A, D), 0.02, 1.0),
        'rwkv_lnx_b': nrm((N_A, D), 0.02),
        'rwkv_w_o': nrm((N_A, D, D), D ** -0.5),
        'kv_norm_g': nrm((D,), 0.02, 1.0),
        'kv_ada_w': nrm((D, 2 * D), 0.5 * D ** -0.5),
        'kv_ada_b': nrm((2 * D,), 0.02),
        'w_kv': nrm((D, 6 * G * Dh), D ** -0.5),
        'cmp_pos': nrm((2, CMP_LEN, Dh), 0.1),
        'cmp_w1': nrm((2, CMP_LEN * Dh, CMP_HIDDEN), (CMP_LEN * Dh) ** -0.5),
        'cmp_b1': nrm((2, CMP_HIDDEN), 0.02),
        'cmp_w2': nrm((2, CMP_HIDDEN, Dh), CMP_HIDDEN ** -0.5),
        'nsa_w_qg': nrm((N_B, D, NSA_HEADS * Dh + 3 * NSA_HEADS), D ** -0.5),
        'nsa_w_o': nrm((N_B, NSA_HEADS * Dh, D), (NSA_HEADS * Dh) ** -0.5),
        'moe_w_grp': nrm((DEPTH, D, N_GROUPS), D ** -0.5),
        'moe_b_grp': nrm((DEPTH, N_GROUPS), 0.01),
        'moe_w_exp': nrm((DEPTH, D, N_EXPERTS), D ** -0.5),
        'moe_b_exp': nrm((DEPTH, N_EXPERTS), 0.01),
        'moe_w_gate': nrm((DEPTH, N_EXPERTS, D, EXPERT_FF), D ** -0.5),
        'moe_w_up': nrm((DEPTH, N_EXPERTS, D, EXPERT_FF), D ** -0.5),
        'moe_w_down': nrm((DEPTH, N_EXPERTS, EXPERT_FF, D), EXPERT_FF ** -0.5),
    }

def reference(x_prompt, x_sample, cache_nsa_kv, cache_win_kv, state_wkv, state_shift, page_table, c_prompt, c_sample,
              ada_w, ada_b, norm_mix_g, norm_ffn_g, norm_f_g,
              rwkv_mix, rwkv_w_rkv, rwkv_w0, rwkv_w1, rwkv_w2, rwkv_a0, rwkv_a1, rwkv_a2, rwkv_v0, rwkv_v1, rwkv_v2,
              rwkv_g1, rwkv_g2, rwkv_k_k, rwkv_k_a, rwkv_r_k, rwkv_lnx_w, rwkv_lnx_b, rwkv_w_o,
              kv_norm_g, kv_ada_w, kv_ada_b, w_kv, cmp_pos, cmp_w1, cmp_b1, cmp_w2,
              nsa_w_qg, nsa_w_o,
              moe_w_grp, moe_b_grp, moe_w_exp, moe_b_exp, moe_w_gate, moe_w_up, moe_w_down):
    P = dict(ada_w=ada_w, ada_b=ada_b, norm_mix_g=norm_mix_g, norm_ffn_g=norm_ffn_g, norm_f_g=norm_f_g,
             rwkv_mix=rwkv_mix, rwkv_w_rkv=rwkv_w_rkv, rwkv_w0=rwkv_w0, rwkv_w1=rwkv_w1, rwkv_w2=rwkv_w2,
             rwkv_a0=rwkv_a0, rwkv_a1=rwkv_a1, rwkv_a2=rwkv_a2, rwkv_v0=rwkv_v0, rwkv_v1=rwkv_v1, rwkv_v2=rwkv_v2,
             rwkv_g1=rwkv_g1, rwkv_g2=rwkv_g2, rwkv_k_k=rwkv_k_k, rwkv_k_a=rwkv_k_a, rwkv_r_k=rwkv_r_k,
             rwkv_lnx_w=rwkv_lnx_w, rwkv_lnx_b=rwkv_lnx_b, rwkv_w_o=rwkv_w_o,
             kv_norm_g=kv_norm_g, kv_ada_w=kv_ada_w, kv_ada_b=kv_ada_b, w_kv=w_kv,
             nsa_w_qg=nsa_w_qg, nsa_w_o=nsa_w_o,
             moe_w_grp=moe_w_grp, moe_b_grp=moe_b_grp, moe_w_exp=moe_w_exp, moe_b_exp=moe_b_exp,
             moe_w_gate=moe_w_gate, moe_w_up=moe_w_up, moe_w_down=moe_w_down)

    def make_prompt_attend(kv):
        ctx = branch_context(kv[:, :, :4], cmp_pos, cmp_w1, cmp_b1, cmp_w2)
        kvw_pad = jnp.pad(kv[:, :, 4:], ((0, 0), (WINDOW, 0), (0, 0), (0, 0), (0, 0)))
        return lambda q, g: prompt_attend(q, g, ctx, kvw_pad)

    bp = x_prompt.shape[0]
    y_prompt, kv_p, shift_prompt, wkv_prompt = run_trunk(
        x_prompt, c_prompt,
        jnp.zeros((N_A, bp, D_MODEL), x_prompt.dtype),
        jnp.zeros((N_A, bp, RWKV_HEADS, RWKV_HEAD_DIM, RWKV_HEAD_DIM), x_prompt.dtype),
        make_prompt_attend, P)

    db, n_pages = page_table.shape
    past_len = n_pages * cache_nsa_kv.shape[1]
    past = cache_nsa_kv[page_table].reshape(db, past_len, 4, NSA_KV_HEADS, NSA_HEAD_DIM)
    wb = cache_win_kv.shape[1]

    def make_sample_attend(kv):
        S = kv.shape[1]
        ctx = branch_context(jnp.concatenate([past, kv[:, :, :4]], axis=1), cmp_pos, cmp_w1, cmp_b1, cmp_w2)
        kvw = jnp.concatenate([cache_win_kv, kv[:, :, 4:]], axis=1)
        q_pos = past_len + jnp.arange(S, dtype=jnp.int32)
        w_pos = past_len - wb + jnp.arange(wb + S, dtype=jnp.int32)
        return lambda q, g: nsa_attend(q, g, q_pos, *ctx, kvw[:, :, 0], kvw[:, :, 1], w_pos)

    y_sample, kv_s, shift_sample, wkv_sample = run_trunk(
        x_sample, c_sample, state_shift, state_wkv, make_sample_attend, P)

    kv_prompt = kv_p[:, :, :4]
    kv_sample = kv_s[:, :, :4]
    win_prompt = kv_p[:, -min(WINDOW, kv_p.shape[1]):, 4:]
    win_all = jnp.concatenate([cache_win_kv, kv_s[:, :, 4:]], axis=1)
    win_sample = win_all[:, -min(WINDOW, win_all.shape[1]):]
    return (y_prompt, y_sample, kv_prompt, kv_sample, win_prompt, win_sample, wkv_prompt, wkv_sample, shift_prompt, shift_sample)


_drawn_inputs = setup_inputs


def setup_inputs(seed=0):
    import zlib

    import numpy as np

    out = dict(_drawn_inputs(seed))
    spreads = {}
    factors = {'norm_ffn_g': 4.147,
     'norm_f_g': 2.743,
     'rwkv_w1': 4.007,
     'rwkv_w2': 4.036,
     'rwkv_k_k': 3.435,
     'rwkv_lnx_w': 8.0,
     'rwkv_lnx_b': 8.0,
     'kv_norm_g': 2.965,
     'cmp_pos': 5.067,
     'cmp_b1': 8.0,
     'moe_b_grp': 8.0,
     'moe_b_exp': 8.0}
    for name, (base, spread) in spreads.items():
        noise = np.random.default_rng([zlib.crc32(name.encode()), seed]).standard_normal(out[name].shape)
        drawn = base * np.exp(spread * noise) if base else spread * noise
        out[name] = __import__('jax').numpy.asarray(drawn.astype(out[name].dtype))
    for name, factor in factors.items():
        out[name] = (out[name] * factor).astype(out[name].dtype)
    return out
```

```python
import concourse.bass as bass
from concourse import mybir
from contextlib import ExitStack

F32 = mybir.dt.float32
I32 = mybir.dt.int32
ALU = mybir.AluOpType
ACT = mybir.ActivationFunctionType
AX = mybir.AxisListType

D = 1024
KT = D // 128
SEQ = 512
DB, DS = 8, 4
NS = DB * DS
T = SEQ + NS
HALF = T // 2
NC = 1 + DB
PAIRS = 8
CH = 128
NCH = SEQ // CH
G, HD, NH, HG = 4, 64, 16, 4
PAST, PAGE, NPOOL = 256, 128, 20
E_N, FF = 16, 512
WP = 3
NEG = -1.0e30
RMS_EPS, LNX_EPS = 1e-6, 64e-5

VEC = ["g_mix0", "g_mix1", "g_ffn0", "g_ffn1", "g_f", "g_kv", "mix0", "mix1", "mix2", "mix3", "mix4", "mix5",
       "w0", "a0", "k_k", "k_a", "r_k", "lnx_w", "lnx_b"]
VROW = {n: i for i, n in enumerate(VEC)}


class Bufs:
    pass


def allocate(nc, ctx, io):
    B = Bufs()

    def sb(stack, name, shape, dt=F32):
        return stack.enter_context(nc.sbuf_tensor(name, shape, dt))

    B.ident = sb(ctx, "ident", [128, 128])
    B.ones = sb(ctx, "ones", [128, 128])
    B.eps_rms = sb(ctx, "eps_rms", [128, 1])
    B.eps_lnx = sb(ctx, "eps_lnx", [128, 1])
    B.xT = sb(ctx, "xT", [128, KT, T])
    B.fT = sb(ctx, "fT", [128, KT, T])
    B.vT = sb(ctx, "vT", [128, 5, 128])
    B.modT = sb(ctx, "modT", [128, 112, NC])
    B.coef = sb(ctx, "coef", [128, KT, NC])
    B.rstd = sb(ctx, "rstd", [128, T])
    B.tmp_s = sb(ctx, "tmp_s", [128, 2, NS])

    rw = ExitStack()
    B.blk_ones = sb(rw, "blk_ones", [128, 128])
    B.blk_mean = sb(rw, "blk_mean", [128, 128])
    B.low = sb(rw, "low", [128, 128])
    B.up2 = sb(rw, "up2", [128, 2, 128])
    B.bm = {m: sb(rw, f"bm{m}", [128, 128]) for m in (16, 32, 64)}
    B.offl = {m: sb(rw, f"offl{m}", [128, 128]) for m in (16, 32, 64)}
    B.offu = {m: sb(rw, f"offu{m}", [128, 128]) for m in (16, 32, 64)}
    B.s_low = sb(rw, "s_low", [NS, NS])
    B.s_up2 = sb(rw, "s_up2", [NS, 2, NS])
    B.s_bm = sb(rw, "s_bm", [NS, NS])
    B.seg_start = sb(rw, "seg_start", [128, T])
    B.seg_sel = sb(rw, "seg_sel", [128, DB, NS])
    B.row_sel = sb(rw, "row_sel", [NS, DB])
    B.rkv = [sb(rw, f"rkv{i}", [128, KT, T]) for i in range(3)]
    B.hwa = sb(rw, "hwa", [128, T])
    B.hw, B.ha = B.hwa[0:64], B.hwa[64:128]
    B.hg = sb(rw, "hg", [128, T])
    B.hg2 = sb(rw, "hg2", [32, T])
    B.wa2 = sb(rw, "wa2", [128, D])
    B.w2, B.a2 = B.wa2[0:64], B.wa2[64:128]
    B.g2 = sb(rw, "g2", [128, D])
    B.g2b = sb(rw, "g2b", [32, D])

    st = ExitStack()
    B.xt = sb(st, "xt", [128, 5, D])
    B.vs = sb(st, "vs", [128, 5, 128])
    B.cact = sb(st, "cact", [128, NC, KT])
    B.adaw = [sb(st, f"adaw{i}", [128, KT, 512]) for i in range(3)]
    B.adas = [sb(st, f"adas{i}", [NC, 512]) for i in range(2)]
    st.close()
    st = ExitStack()
    B.xx = sb(st, "xx", [128, KT, T])
    B.xm = [sb(st, f"xm{i}", [128, KT, T]) for i in range(2)]
    B.wp = [sb(st, f"wp{i}", [128, KT, 128]) for i in range(WP)]
    B.w1 = sb(st, "w1", [128, KT, 64])
    B.a1 = sb(st, "a1", [128, KT, 64])
    B.g1 = sb(st, "g1", [128, KT, 160])
    B.lasth = sb(st, "lasth", [128, NC, KT])
    B.lasto = sb(st, "lasto", [NC * KT, 128])
    st.close()
    st = ExitStack()
    names = ("lw", "cum", "a", "g", "kk", "km", "t1", "t2", "e1", "e2", "bh", "kh", "bonus")
    B.p = {n: B.fT[:, i] if i < KT else sb(st, f"p_{n}", [128, T])[:] for i, n in enumerate(names)}
    B.ar = sb(st, "p_ar", [128, NCH, 2, CH])
    B.ars = sb(st, "p_ars", [128, 2, NS])
    B.mid = sb(st, "p_mid", [128, NCH])
    B.fac = sb(st, "p_fac", [128, NCH])
    B.facs = sb(st, "p_facs", [128, DB])
    B.axs = sb(st, "p_axs", [128, DB, NS])
    B.rxs = sb(st, "p_rxs", [128, DB, NS])
    B.tok = [sb(st, f"p_tok{i}", [128, NCH, CH]) for i in range(3)]
    B.toks = [sb(st, f"p_toks{i}", [NS, 128]) for i in range(3)]
    B.Lm = [sb(st, f"Lm{h}", [128, NCH, CH]) for h in range(2)]
    B.UR = [sb(st, f"UR{h}", [128, NCH, 2, CH]) for h in range(2)]
    B.KR = [sb(st, f"KR{h}", [128, NCH, 2, CH]) for h in range(2)]
    B.Lp = [sb(st, f"Lp{h}", [128, NCH, CH]) for h in range(2)]
    B.Up = [sb(st, f"Up{h}", [128, NCH, CH]) for h in range(2)]
    B.Ti = [sb(st, f"Ti{h}", [128, NCH, CH]) for h in range(2)]
    B.Tt = [sb(st, f"Tt{h}", [128, NCH, CH]) for h in range(2)]
    B.sL = [sb(st, f"sL{h}", [NS, NS]) for h in range(2)]
    B.sUR = [sb(st, f"sUR{h}", [NS, 2, NS]) for h in range(2)]
    B.sKR = [sb(st, f"sKR{h}", [NS, 2, NS]) for h in range(2)]
    B.sL2 = [sb(st, f"sL2{h}", [NS, NS]) for h in range(2)]
    B.sTt = [sb(st, f"sTt{h}", [NS, NS]) for h in range(2)]
    B.X = [sb(st, f"X{h}", [128, HD]) for h in range(2)]
    B.SA = [sb(st, f"SA{h}", [128, HD]) for h in range(2)]
    B.ST = sb(st, "ST", [128, HD])
    B.STs = sb(st, "STs", [128, DB, HD])
    B.stin = sb(st, "stin", [HD, DB, 2, HD])
    B.stout = sb(st, "stout", [HD, NC, 128])
    B.sax = [sb(st, f"sax{h}", [NS, DB, HD]) for h in range(2)]
    B.vx = sb(st, "vx", [NS, 2, DB, HD])
    st.close()
    rw.close()
    allocate_moe(nc, B, sb)
    allocate_nsa(nc, B, sb)
    B.bank = [ctx.enter_context(nc.psum_tensor(f"bank{i}", [128, 512], F32)) for i in range(8)]
    sems = {}

    def sem(name):
        if name not in sems:
            sems[name] = ctx.enter_context(nc.semaphore(name))
        return sems[name]

    B.sem = sem
    return B


def half(h):
    return slice(h * HALF, (h + 1) * HALF)


def vec(B, name):
    v = VROW[name]
    return B.vT[:, 2 + v // 16, (v % 16) * KT:(v % 16 + 1) * KT]


def mod(B, layer, which):
    at = layer * 48 + which * KT
    return B.modT[:, at:at + KT, :]


def program(nc, io, out):
    ctx = ExitStack()
    with ctx:
        B = allocate(nc, ctx, io)
        S = B.sem
        block = ctx.enter_context(nc.Block())
        ident, bank = B.ident, B.bank

        @block.gpsimd
        def _(pool):
            chain = [0]

            def link(ins):
                chain[0] += 1
                ins.then_inc(S("pool_chain"), 1)
                pool.wait_ge(S("pool_chain"), chain[0])

            def keep(tile, pattern, base, mult, op=ALU.is_ge, fill=0.0):
                link(pool.affine_select(out=tile, in_=tile, compare_op=op, fill=fill, base=base,
                                        pattern=pattern, channel_multiplier=mult))

            link(pool.memset(ident[:], 0.0))
            keep(ident[:], [[-1, 128]], 0, 1, ALU.not_equal, 1.0)
            pool.memset(B.ones[:], 1.0).then_inc(S("pool_ident"), 1)
            link(pool.memset(B.low[:], 1.0))
            keep(B.low[:], [[-1, 128]], -1, 1)
            link(pool.memset(B.up2[:], 1.0))
            keep(B.up2[:, 0, :], [[1, 128]], -1, -1)
            keep(B.up2[:, 1, :], [[1, 128]], 0, -1)
            for tile, m, n in [(B.bm[16], 16, 128), (B.bm[32], 32, 128), (B.bm[64], 64, 128), (B.s_bm, 4, NS)]:
                link(pool.memset(tile[:], 1.0))
                v = tile[:].rearrange("p (b c) -> p b c", c=m)
                keep(v, [[-m, n // m], [0, m]], 0, 1)
                keep(v, [[m, n // m], [0, m]], m - 1, -1)
            link(pool.memset(B.seg_sel[:], 1.0))
            keep(B.seg_sel[:], [[-DS, DB], [1, NS]], 0, 0)
            keep(B.seg_sel[:], [[DS, DB], [-1, NS]], DS - 1, 0)
            link(pool.memset(B.row_sel[:], 1.0))
            keep(B.row_sel[:], [[-DS, DB]], 0, 1)
            keep(B.row_sel[:], [[DS, DB]], DS - 1, -1)
            link(pool.memset(B.seg_start[:], 1.0))
            link(pool.memset(B.seg_start[:, 0:SEQ:CH], 0.0))
            link(pool.memset(B.seg_start[:, SEQ:T:DS], 0.0))
            pool.memset(B.eps_rms[:], RMS_EPS)
            pool.memset(B.eps_lnx[:], LNX_EPS).then_inc(S("pool_masks"), 1)

        @block.sync
        def _(sp):
            def row(g, r, n, src):
                sp.dma_start(B.vs[r:r + n, g, :], src).then_inc(S("vec_loaded"), 16)

            row(0, 0, 8, io["c_prompt"].rearrange("b (k p) -> (b k) p", p=128))
            row(0, 8, 64, io["c_sample"].rearrange("b (k p) -> (b k) p", p=128))
            row(1, 0, 64, io["state_shift"].rearrange("a b (k p) -> (a b k) p", p=128))
            row(2, 0, 16, io["norm_mix_g"].rearrange("l (k p) -> (l k) p", p=128))
            row(2, 16, 16, io["norm_ffn_g"].rearrange("l (k p) -> (l k) p", p=128))
            row(2, 32, 8, io["norm_f_g"].rearrange("(k p) -> k p", p=128))
            row(2, 40, 8, io["kv_norm_g"].rearrange("(k p) -> k p", p=128))
            row(2, 48, 48, io["rwkv_mix"].rearrange("l s (k p) -> (l s k) p", p=128))
            for n, name in enumerate(["rwkv_w0", "rwkv_a0", "rwkv_k_k", "rwkv_k_a"]):
                row(2, 96 + 8 * n, 8, io[name].rearrange("l (k p) -> (l k) p", p=128))
            row(3, 0, 8, io["rwkv_r_k"].rearrange("l (k h) n -> (l k) (h n)", h=2))
            row(3, 8, 8, io["rwkv_lnx_w"].rearrange("l (k p) -> (l k) p", p=128))
            row(3, 16, 8, io["rwkv_lnx_b"].rearrange("l (k p) -> (l k) p", p=128))
            row(4, 0, 96, io["ada_b"].rearrange("l (k p) -> (l k) p", p=128))
            row(4, 96, 16, io["kv_ada_b"].rearrange("(k p) -> k p", p=128))
            sp.dma_start(B.xt[:, 0:4, :], io["x_prompt"].rearrange("b (t p) d -> p (b t) d", p=128)).then_inc(S("x_loaded"), 16)
            sp.dma_start(B.xt[0:NS, 4, :], io["x_sample"].rearrange("b s d -> (b s) d")).then_inc(S("x_loaded"), 16)
            for j in range(28):
                if j >= 3:
                    sp.wait_ge(S("ada_mm"), j - 2)
                src = io["ada_w"][j // 12, :, (j % 12) * 512:(j % 12 + 1) * 512] if j < 24 else \
                    io["kv_ada_w"][:, (j - 24) * 512:(j - 23) * 512]
                sp.dma_start(B.adaw[j % 3][:], src.rearrange("(k p) n -> p k n", p=128)).then_inc(S(f"adaw_loaded{j % 3}"), 16)
            sp.dma_start(B.w2, io["rwkv_w2"][0]).then_inc(S("lora2_loaded"), 16)
            sp.dma_start(B.a2, io["rwkv_a2"][0]).then_inc(S("lora2_loaded"), 16)
            sp.dma_start(B.g2[:], io["rwkv_g2"][0, 0:128]).then_inc(S("lora2_loaded"), 16)
            sp.dma_start(B.g2b[:], io["rwkv_g2"][0, 128:160]).then_inc(S("lora2_loaded"), 16)
            sp.wait_ge(S("ada_tr"), 28)
            sp.wait_ge(S("in_ev"), 11)
            for tile, name in [(B.w1, "rwkv_w1"), (B.a1, "rwkv_a1"), (B.g1, "rwkv_g1")]:
                sp.dma_start(tile[:], io[name][0].rearrange("(k p) n -> p k n", p=128)).then_inc(S("lora1_loaded"), 16)
            for g in range(24):
                if g >= WP:
                    sp.wait_ge(S("rkv_mm"), 2 * (g - WP + 1))
                s, m = g // KT, g % KT
                sp.dma_start(B.wp[g % WP][:], io["rwkv_w_rkv"][0, s, :, m * 128:(m + 1) * 128].rearrange("(k p) n -> p k n", p=128))\
                  .then_inc(S(f"wp_loaded{g % WP}"), 16)
            sp.wait_ge(S("last_ev"), 1)
            sp.dma_start(out["shift_prompt"].rearrange("l b (k p) -> (l b k) p", p=128), B.lasto[0:8, :]).then_inc(S("stored"), 16)
            sp.dma_start(out["shift_sample"].rearrange("l b (k p) -> (l b k) p", p=128), B.lasto[8:72, :]).then_inc(S("stored"), 16)
            stored = 2
            for p in range(PAIRS):
                if p == 0:
                    sp.wait_ge(S("rkv_mm"), 48 + 8)
                    sp.wait_ge(S("xm_ready"), 6)
                    sp.wait_ge(S("stored"), 32)
                    sp.wait_ge(S("last_ev"), 1)
                if p >= 1:
                    sp.wait_ge(S("st_in"), p)
                for h in range(2):
                    sp.dma_start(B.stin[:, :, h, :], io["state_wkv"][0, :, 2 * p + h].rearrange("b i j -> i b j"))\
                      .then_inc(S("state_loaded"), 16)
                sp.wait_ge(S("st_out_ev"), p + 1)
                for h in range(2):
                    sp.dma_start(out["wkv_prompt"][0, 0, 2 * p + h], B.stout[:, 0, h * HD:(h + 1) * HD]).then_inc(S("state_stored"), 16)
                    sp.dma_start(out["wkv_sample"][0, :, 2 * p + h].rearrange("b i j -> i b j"),
                                 B.stout[:, 1:NC, h * HD:(h + 1) * HD]).then_inc(S("state_stored"), 16)
            sp_rest(nc, sp, B, io, out)

        @block.tensor
        def _(pe):
            pe.wait_ge(S("pool_ident"), 1)
            pe.wait_ge(S("vec_loaded"), 16 * 17)
            for g in range(4):
                rows = (72, 64, 128, 24)[g]
                mm = pe.transpose(bank[0][:, g * 128:g * 128 + rows], B.vs[0:rows, g, :], ident[0:rows, 0:rows])
            mm.then_inc(S("in_tr"), 1)
            pe.transpose(bank[1][:, 0:112], B.vs[0:112, 4, :], ident[0:112, 0:112]).then_inc(S("in_tr"), 1)
            pe.wait_ge(S("x_loaded"), 32)
            for g in range(2, 11):
                if g >= 8:
                    pe.wait_ge(S("in_ev"), g - 7)
                if g < 10:
                    t, h = (g - 2) // 2, (g - 2) % 2
                    for q in range(4):
                        k = 4 * h + q
                        mm = pe.transpose(bank[g % 8][:, q * 128:(q + 1) * 128], B.xt[:, t, k * 128:(k + 1) * 128], ident[:])
                else:
                    for k in range(KT):
                        mm = pe.transpose(bank[g % 8][:, k * NS:(k + 1) * NS], B.xt[0:NS, 4, k * 128:(k + 1) * 128],
                                          ident[0:NS, 0:NS])
                mm.then_inc(S("in_tr"), 1)
            pe.wait_ge(S("cact_ready"), 1)
            pe.wait_ge(S("in_ev"), 11)

            def ada_product(j):
                pe.wait_ge(S(f"adaw_loaded{j % 3}"), 16 * (j // 3 + 1))
                if j >= 2:
                    pe.wait_ge(S("ada_rows"), j - 1)
                for k in range(KT):
                    mm = pe.matmul(bank[j % 2][0:NC, :], B.cact[:, :, k], B.adaw[j % 3][:, k, :], start=k == 0, stop=k == KT - 1)
                mm.then_inc(S("ada_mm"), 1)

            def ada_turn(j):
                pe.wait_ge(S("ada_rows"), j + 1)
                if j >= 2:
                    pe.wait_ge(S("ada_ev"), j - 1)
                for q in range(4):
                    mm = pe.transpose(bank[2 + j % 2][:, q * NC:(q + 1) * NC], B.adas[j % 2][:, q * 128:(q + 1) * 128],
                                      ident[0:NC, 0:NC])
                mm.then_inc(S("ada_tr"), 1)

            for j in range(28):
                ada_product(j)
                if j >= 1:
                    ada_turn(j - 1)
            ada_turn(27)
            pe_norm_sum(pe, B, 0)
            for g in range(24):
                s = g // KT
                if g % KT == 0:
                    pe.wait_ge(S("xm_ready"), s + 1)
                pe.wait_ge(S(f"wp_loaded{g % WP}"), 16 * (g // WP + 1))
                for h in range(2):
                    n = 2 * g + h
                    if n >= 8:
                        pe.wait_ge(S("rkv_ev"), n - 7)
                    for k in range(KT):
                        mm = pe.matmul(bank[n % 8][:, 0:HALF], B.wp[g % WP][:, k, :], B.xm[s % 2][:, k, half(h)],
                                       start=k == 0, stop=k == KT - 1)
                    mm.then_inc(S("rkv_mm"), 1)
            pe.wait_ge(S("lora1_loaded"), 48)
            n = 48
            for s, w, c0, c1 in [(3, B.w1, 0, 64), (4, B.a1, 0, 64), (5, B.g1, 0, 128), (5, B.g1, 128, 160)]:
                pe.wait_ge(S("xm_ready"), s + 1)
                r0 = 64 if s == 4 else 0
                for h in range(2):
                    pe.wait_ge(S("rkv_ev"), n - 7)
                    for k in range(KT):
                        mm = pe.matmul(bank[n % 8][r0:r0 + c1 - c0, 0:HALF], w[:, k, c0:c1], B.xm[s % 2][:, k, half(h)],
                                       start=k == 0, stop=k == KT - 1)
                    mm.then_inc(S("rkv_mm"), 1)
                    n += 1
            pe.wait_ge(S("lasth_ready"), 1)
            pe.wait_ge(S("rkv_ev"), 56)
            pe.transpose(bank[0][0:72, 0:128], B.lasth[:].rearrange("p n k -> p (n k)"), ident[:]).then_inc(S("last_tr"), 1)
            pe.wait_ge(S("last_ev"), 1)
            for p in range(PAIRS):
                pe_pair(pe, B, p)
            pe_rest(nc, pe, B, io, out)

        @block.scalar
        def _(act):
            act.wait_ge(S("in_ev"), 1)
            act.activation(B.cact[:].rearrange("p n k -> p (n k)"), B.vT[:, 0, 0:72], ACT.Silu).then_inc(S("cact_ready"), 1)
            for j in range(28):
                act.wait_ge(S("ada_mm"), j + 1)
                if j >= 2:
                    act.wait_ge(S("ada_tr"), j - 1)
                act.activation(B.adas[j % 2][:], bank[j % 2][0:NC, :], ACT.Copy).then_inc(S("ada_rows"), 1)
            act_norm(act, B, 0)
            for n in range(56):
                act.wait_ge(S("rkv_mm"), n + 1)
                h = n % 2
                if n < 48:
                    s, m = n // 16, n % 16 // 2
                    ins = act.activation(B.rkv[s][:, m, half(h)], bank[n % 8][:, 0:HALF], ACT.Copy)
                else:
                    dst, fn = [(B.hw, ACT.Tanh), (B.ha, ACT.Copy), (B.hg, ACT.Sigmoid), (B.hg2, ACT.Sigmoid)][(n - 48) // 2]
                    r0 = 64 if (n - 48) // 2 == 1 else 0
                    ins = act.activation(dst[:, half(h)], bank[n % 8][r0:r0 + dst.shape[0], 0:HALF], fn)
                ins.then_inc(S("rkv_ev"), 1)
            act.drain()
            for p in range(PAIRS):
                act_pair(act, B, p)
            act_rest(nc, act, B, io, out)

        @block.vector
        def _(dve):
            for g in range(11):
                dve.wait_ge(S("in_tr"), g + 1)
                if g == 0:
                    for q in range(4):
                        rows = (72, 64, 128, 24)[q]
                        ins = dve.tensor_copy(B.vT[:, q, 0:rows], bank[0][:, q * 128:q * 128 + rows])
                elif g == 1:
                    ins = dve.tensor_copy(B.vT[:, 4, 0:112], bank[1][:, 0:112])
                elif g < 10:
                    t, h = (g - 2) // 2, (g - 2) % 2
                    ins = dve.tensor_copy(B.xT[:, 4 * h:4 * h + 4, t * 128:(t + 1) * 128],
                                          bank[g % 8][:].rearrange("p (k n) -> p k n", k=4))
                else:
                    ins = dve.tensor_copy(B.xT[:, :, SEQ:T], bank[g % 8][:, 0:KT * NS].rearrange("p (k n) -> p k n", k=KT))
                ins.then_inc(S("in_ev"), 1)
            dve.wait_ge(S("pool_masks"), 1)
            dve.tensor_scalar(B.blk_mean[:], B.bm[64][:], 1.0 / 64, None, ALU.mult)
            dve.tensor_copy(B.blk_ones[:], B.bm[64][:])
            dve.tensor_tensor(B.s_low[:], B.low[0:NS, 0:NS], B.s_bm[:], ALU.mult)
            for q in range(2):
                dve.tensor_tensor(B.s_up2[:, q, :], B.up2[0:NS, q, 0:NS], B.s_bm[:], ALU.mult)
            for m in (16, 32, 64):
                big = B.bm[2 * m] if m < 64 else B.ones
                dve.tensor_tensor(B.offl[m][:], big[:], B.bm[m][:], ALU.subtract)
                dve.tensor_tensor(B.offu[m][:], big[:], B.bm[m][:], ALU.subtract)
            dve.drain()
            for m in (16, 32, 64):
                dve.tensor_tensor(B.offl[m][:], B.offl[m][:], B.low[:], ALU.mult)
                dve.tensor_tensor(B.offu[m][:], B.offu[m][:], B.up2[:, 0, :], ALU.mult)
            dve.drain()
            for j in range(28):
                dve.wait_ge(S("ada_tr"), j + 1)
                bias = B.vT[:, 4, 4 * j:4 * j + 4].unsqueeze(2).to_broadcast([128, 4, NC])
                dve.tensor_tensor(B.modT[:, 4 * j:4 * j + 4, :], bank[2 + j % 2][:, 0:4 * NC].rearrange("p (q n) -> p q n", q=4),
                                  bias, ALU.add).then_inc(S("ada_ev"), 1)
            dve.drain()
            dve_norm(dve, B, 0, "g_mix0", mod(B, 0, 0), mod(B, 0, 1))
            dve.drain()
            h = B.fT
            dve.wait_ge(S("in_ev"), 11)
            dve.tensor_tensor(B.xx[:, :, 1:SEQ], h[:, :, 0:SEQ - 1], h[:, :, 1:SEQ], ALU.subtract)
            dve.tensor_scalar(B.xx[:, :, 0:1], h[:, :, 0:1], -1.0, None, ALU.mult)
            hs = h[:, :, SEQ:T].rearrange("p k (b s) -> p k b s", s=DS)
            xs = B.xx[:, :, SEQ:T].rearrange("p k (b s) -> p k b s", s=DS)
            dve.tensor_tensor(xs[:, :, :, 1:DS], hs[:, :, :, 0:DS - 1], hs[:, :, :, 1:DS], ALU.subtract)
            dve.tensor_tensor(xs[:, :, :, 0], B.vT[:, 1, 0:64].rearrange("p (b k) -> p k b", k=KT), hs[:, :, :, 0], ALU.subtract)
            dve.tensor_copy(B.lasth[:, 0, :], h[:, :, SEQ - 1])
            dve.tensor_copy(B.lasth[:, 1:NC, :].rearrange("p n k -> p k n"), hs[:, :, :, DS - 1]).then_inc(S("lasth_ready"), 1)
            dve.drain()
            for s in range(6):
                if s >= 2:
                    dve.wait_ge(S("rkv_mm"), {2: 16, 3: 32, 4: 48, 5: 50}[s])
                for k in range(KT):
                    ins = dve.scalar_tensor_tensor(out=B.xm[s % 2][:, k, :], in0=B.xx[:, k, :], scalar=vec(B, f"mix{s}")[:, k:k + 1],
                                                   in1=h[:, k, :], op0=ALU.mult, op1=ALU.add)
                ins.then_inc(S("xm_ready"), 1)
            dve.wait_ge(S("last_tr"), 1)
            dve.tensor_copy(B.lasto[:], bank[0][0:72, 0:128]).then_inc(S("last_ev"), 1)
            for p in range(PAIRS):
                dve_pair(dve, B, p)
            dve_rest(nc, dve, B, io, out)


def act_norm(act, B, n):
    S = B.sem
    act.wait_ge(S("x_ready"), n) if n else act.wait_ge(S("in_ev"), 11)
    act.activation(B.fT[:], B.xT[:], ACT.Square).then_inc(S("norm_sq"), 1)
    act.wait_ge(S("norm_mm"), n + 1)
    for h in range(2):
        ins = act.activation(B.rstd[:, half(h)], B.bank[h][:, 0:HALF], ACT.Sqrt, bias=B.eps_rms[:, 0:1], scale=1.0 / D)
    ins.then_inc(S("norm_rt"), 1)


def pe_norm_sum(pe, B, n):
    S = B.sem
    pe.wait_ge(S("norm_sq"), n + 1)
    for h in range(2):
        for k in range(KT):
            mm = pe.matmul(B.bank[h][:, 0:HALF], B.ones[:], B.fT[:, k, half(h)], start=k == 0, stop=k == KT - 1)
    mm.then_inc(S("norm_mm"), 1)


def dve_norm(dve, B, n, gain, shift, scale):
    S = B.sem
    g = vec(B, gain)
    if scale is not None:
        dve.scalar_tensor_tensor(out=B.coef[:], in0=scale, scalar=1.0, in1=g.unsqueeze(2).to_broadcast([128, KT, NC]),
                                 op0=ALU.add, op1=ALU.mult)
    if n is not None:
        dve.wait_ge(S("norm_rt"), n + 1)
        dve.reciprocal(B.rstd[:], B.rstd[:])
    dve.drain()
    dve.tensor_tensor(B.fT[:], B.xT[:], B.rstd[:].unsqueeze(1).to_broadcast([128, KT, T]), ALU.mult)
    dve.drain()
    for k in range(KT):
        if scale is None:
            ins = dve.tensor_scalar(B.fT[:, k, :], B.fT[:, k, :], g[:, k:k + 1], None, ALU.mult)
        else:
            dve.tensor_scalar(B.fT[:, k, 0:SEQ], B.fT[:, k, 0:SEQ], B.coef[:, k, 0:1], shift[:, k, 0:1], ALU.mult, ALU.add)
    if scale is not None:
        fs = B.fT[:, :, SEQ:T].rearrange("p k (b s) -> p k b s", s=DS)
        dve.tensor_tensor(fs, fs, B.coef[:, :, 1:NC].unsqueeze(3).to_broadcast([128, KT, DB, DS]), ALU.mult)
        dve.drain()
        ins = dve.tensor_tensor(fs, fs, shift[:, :, 1:NC].unsqueeze(3).to_broadcast([128, KT, DB, DS]), ALU.add)
    ins.then_inc(S("norm_done"), 1)


SQUARE, MERGES = (1, 2, 3), {5: 16, 7: 32, 9: 64}
STEPS = 14


def hs(h):
    return slice(h * HD, (h + 1) * HD)


def pe_pair(pe, B, p):
    S, bank, ident, P = B.sem, B.bank, B.ident, B.p
    pe.wait_ge(S("state_loaded"), 32 * (p + 1))
    if p >= 1:
        pe.wait_ge(S("pair_done"), p)
        pe.wait_ge(S("st_out_ev"), p)
    for b in range(DB):
        mm = pe.transpose(bank[6][:, b * HD:(b + 1) * HD], B.stin[:, b].rearrange("i h j -> i (h j)"), ident[0:HD, 0:HD])
    mm.then_inc(S("st_in_tr"), 1)
    pe.wait_ge(S("lora2_loaded"), 64)
    c = slice(p * 128, (p + 1) * 128)
    for i, (w, x) in enumerate([(B.w2, B.hw), (B.a2, B.ha)]):
        for h in range(2):
            mm = pe.matmul(bank[2 * i + h][:, 0:HALF], w[:, c], x[:, half(h)], start=True, stop=True)
        mm.then_inc(S("lora_mm"), 1)
    for h in range(2):
        pe.matmul(bank[4 + h][:, 0:HALF], B.g2[:, c], B.hg[:, half(h)], start=True, stop=False)
        mm = pe.matmul(bank[4 + h][:, 0:HALF], B.g2b[:, c], B.hg2[:, half(h)], start=False, stop=True)
    mm.then_inc(S("lora_mm"), 1)
    pe.wait_ge(S("st_in"), p + 1)
    pe.wait_ge(S("kksq_ready"), p + 1)
    for h in range(2):
        mm = pe.matmul(bank[6 + h][:, 0:HALF], B.blk_ones[:], P["t2"][:, half(h)], start=True, stop=True)
    mm.then_inc(S("head_sums"), 1)
    pe.wait_ge(S("rk_ready"), p + 1)
    for h in range(2):
        mm = pe.matmul(bank[h][:, 0:HALF], B.blk_ones[:], P["bonus"][:, half(h)], start=True, stop=True)
    mm.then_inc(S("head_sums"), 1)
    pe.wait_ge(S("grams_ready"), p + 1)
    pe.wait_ge(S("lora_ev"), 3 * (p + 1))
    src = [B.rkv[2][:, p, :], P["bh"], P["kh"]]
    for i in range(3):
        for q in range(NCH):
            mm = pe.transpose(bank[i][:, q * CH:(q + 1) * CH], src[i][:, q * CH:(q + 1) * CH], ident[:])
    for i in range(3):
        mm = pe.transpose(bank[3][0:NS, i * 128:(i + 1) * 128], src[i][:, SEQ:T], ident[:])
    mm.then_inc(S("tok_tr"), 1)
    pe.wait_ge(S("tok_ev"), p + 1)
    for s in range(STEPS):
        for h in range(2):
            pe_inverse(pe, B, p, s, h)
    for q in range(NCH + 1):
        pe_scan(pe, B, p, q)
    pe.wait_ge(S("y_ev"), p + 1)
    for h in range(2):
        mm = pe.matmul(bank[1 + 4 * h][:, 0:HALF], B.blk_mean[:], P["e1"][:, half(h)], start=True, stop=True)
    mm.then_inc(S("head_means"), 1)
    pe.wait_ge(S("seq_st0"), (NCH + 1) * (p + 1))
    pe.wait_ge(S("seq_st1"), (NCH + 1) * (p + 1))
    pe.transpose(bank[3][0:HD, 0:128], B.ST[:], ident[:])
    for b in range(DB):
        mm = pe.transpose(bank[7 if b < 4 else 2][0:HD, b % 4 * 128:b % 4 * 128 + 128], B.STs[:, b, :], ident[:])
    mm.then_inc(S("st_out_tr"), 1)
    pe.wait_ge(S("ysq_ready"), p + 1)
    for h in range(2):
        mm = pe.matmul(bank[1 + 4 * h][:, 0:HALF], B.blk_mean[:], P["t2"][:, half(h)], start=True, stop=True)
    mm.then_inc(S("head_means"), 1)


def pe_inverse(pe, B, p, s, h):
    S, bk = B.sem, B.bank[4 * h:4 * h + 4]
    r = hs(h)
    if s:
        pe.wait_ge(S(f"inv_dve{h}"), STEPS * p + s)
        if 2 <= s <= 4:
            pe.wait_ge(S(f"inv_act{h}"), 3 * p + s - 1)

    def four(b, lhsT, rhs):
        for c in range(NCH):
            mm = pe.matmul(bk[b][:, c * CH:(c + 1) * CH], lhsT(c), rhs(c), start=True, stop=True)
        return mm

    L, Lp, Up, Ti, Tt = (lambda t: (lambda c: t[:, c, :]))(B.Lm[h]), *[(lambda t: (lambda c: t[:, c, :]))(t) for t in
                                                                     (B.Lp[h], B.Up[h], B.Ti[h], B.Tt[h])]
    U = lambda c: B.UR[h][:, c, 0, :]
    bh = lambda c: B.p["bh"][r, c * CH:(c + 1) * CH]
    kh = lambda c: B.p["kh"][r, c * CH:(c + 1) * CH]
    both = lambda c: B.ar[r, c].rearrange("p q t -> p (q t)")
    if s == 0:
        four(0, lambda c: B.ar[r, c, 0, :], bh)
        for c in range(NCH):
            pe.matmul(bk[1 + c // 2][:, c % 2 * 256:c % 2 * 256 + 256], bh(c), both(c), start=True, stop=True)
        for c in range(2):
            mm = pe.matmul(bk[3][:, c * 256:c * 256 + 256], kh(c), both(c), start=True, stop=True)
    if s == 1:
        for c in range(2, 4):
            mm = pe.matmul(bk[0][:, c % 2 * 256:c % 2 * 256 + 256], kh(c), both(c), start=True, stop=True)
    if s in SQUARE:
        four(1, Up, Lp)
        mm = four(2, Lp, Up)
    if s in (2, 3, 4):
        four(3, Up, Ti)
        mm = four(0, Lp, Tt)
    if s in (5, 7):
        four(1, U, Ti)
    if s in (5, 7, 9):
        mm = four(2, L, Tt)
    if s in (6, 8):
        four(3, Tt, Lp)
    if s in (6, 8, 10):
        mm = four(0, Ti, Up)
    if s == 11:
        bs, ks, a = B.p["bh"][r, SEQ:T], B.p["kh"][r, SEQ:T], B.ars[r].rearrange("p q t -> p (q t)")
        pe.matmul(bk[1][0:NS, 0:NS], B.ars[r, 0, :], bs, start=True, stop=True)
        pe.matmul(bk[1][0:NS, 32:96], bs, a, start=True, stop=True)
        mm = pe.matmul(bk[1][0:NS, 96:160], ks, a, start=True, stop=True)
    if s == 12:
        mm = pe.matmul(bk[1][0:NS, 0:NS], B.sUR[h][:, 0, :], B.sL[h][:], start=True, stop=True)
    if s == 13:
        mm = pe.matmul(bk[1][0:NS, 0:NS], B.sL2[h][:], B.sTt[h][:], start=True, stop=True)
    mm.then_inc(S(f"inv_mm{h}"), 1)


def dve_inverse(dve, B, p, s, h):
    S, bk = B.sem, B.bank[4 * h:4 * h + 4]
    dve.wait_ge(S(f"inv_mm{h}"), STEPS * p + s + 1)
    quad = lambda b: bk[b][:].rearrange("p (c t) -> p c t", c=NCH)
    pairs = lambda b: bk[b][:].rearrange("p (c q t) -> p c q t", c=2, q=2)
    m4 = lambda m: m[:].unsqueeze(1).to_broadcast([128, NCH, CH])
    up = B.up2[:].unsqueeze(1).to_broadcast([128, 2, 2, CH])
    Lm, UR, KR, Lp, Up, Ti, Tt = B.Lm[h], B.UR[h], B.KR[h], B.Lp[h], B.Up[h], B.Ti[h], B.Tt[h]
    if s == 0:
        dve.tensor_tensor(Lm[:], quad(0), m4(B.low), ALU.mult)
        dve.tensor_tensor(UR[:, 0:2], pairs(1), up, ALU.mult)
        dve.tensor_tensor(UR[:, 2:4], pairs(2), up, ALU.mult)
        dve.tensor_tensor(KR[:, 0:2], pairs(3), up, ALU.mult)
        dve.drain()
        dve.tensor_tensor(Lp[:], Lm[:], m4(B.bm[16]), ALU.mult)
        dve.tensor_tensor(Up[:], UR[:, :, 0, :], m4(B.bm[16]), ALU.mult)
        dve.drain()
        dve.tensor_tensor(Ti[:], Lp[:], m4(B.ident), ALU.add)
        ins = dve.tensor_tensor(Tt[:], Up[:], m4(B.ident), ALU.add)
    if s == 1:
        ins = dve.tensor_tensor(KR[:, 2:4], pairs(0), up, ALU.mult)
    if s in (2, 3, 4, 6, 8):
        dve.tensor_tensor(Ti[:], quad(3), Ti[:], ALU.add)
    if s in (2, 3, 4, 6, 8, 10):
        ins = dve.tensor_tensor(Tt[:], quad(0), Tt[:], ALU.add)
    if s in (5, 7):
        dve.tensor_tensor(Lp[:], quad(1), m4(B.offl[MERGES[s]]), ALU.mult)
    if s in (5, 7, 9):
        ins = dve.tensor_tensor(Up[:], quad(2), m4(B.offu[MERGES[s]]), ALU.mult)
    if s == 11:
        dve.tensor_tensor(B.sL[h][:], bk[1][0:NS, 0:NS], B.s_low[:], ALU.mult)
        dve.tensor_tensor(B.sUR[h][:], bk[1][0:NS, 32:96].rearrange("p (q t) -> p q t", q=2), B.s_up2[:], ALU.mult)
        dve.tensor_tensor(B.sKR[h][:], bk[1][0:NS, 96:160].rearrange("p (q t) -> p q t", q=2), B.s_up2[:], ALU.mult)
        dve.drain()
        ins = dve.tensor_tensor(B.sTt[h][:], B.sUR[h][:, 0, :], B.ident[0:NS, 0:NS], ALU.add)
    if s == 12:
        ins = dve.tensor_copy(B.sL2[h][:], bk[1][0:NS, 0:NS])
    if s == 13:
        ins = dve.tensor_tensor(B.sTt[h][:], bk[1][0:NS, 0:NS], B.sTt[h][:], ALU.add)
    ins.then_inc(S(f"inv_dve{h}"), 1)


def pe_scan(pe, B, p, q):
    S = B.sem
    n = (NCH + 1) * p + q
    prompt = q < NCH
    for h in range(2):
        bk, r = B.bank[4 * h:4 * h + 4], hs(h)
        if q == 0:
            pe.wait_ge(S(f"inv_dve{h}"), STEPS * (p + 1))
        else:
            pe.wait_ge(S(f"seq_st{h}"), n)
        if prompt:
            if q:
                pe.matmul(bk[1][:, 0:HD], B.ar[r, q, 0, :], B.ST[r, :], start=True, stop=False)
            mm = pe.matmul(bk[1][:, 0:HD], B.KR[h][:, q, 0, :], B.tok[0][:, q, r], start=q == 0, stop=True)
        else:
            for b in range(DB):
                pe.matmul(bk[1][0:NS, 0:HD], B.axs[r, b, :], B.STs[r, b, :], start=b == 0, stop=False)
            mm = pe.matmul(bk[1][0:NS, 0:HD], B.sKR[h][:, 0, :], B.toks[0][:, r], start=False, stop=True)
        mm.then_inc(S(f"x_mm{h}"), 1)
    for h in range(2):
        bk = B.bank[4 * h:4 * h + 4]
        pe.wait_ge(S(f"x_ev{h}"), n + 1)
        if prompt:
            mm = pe.matmul(bk[2][:, 0:HD], B.Tt[h][:, q, :], B.X[h][:], start=True, stop=True)
        else:
            mm = pe.matmul(bk[2][0:NS, 0:HD], B.sTt[h][:], B.X[h][0:NS, :], start=True, stop=True)
        mm.then_inc(S(f"sa_mm{h}"), 1)
    for h in range(2):
        bk, r = B.bank[4 * h:4 * h + 4], hs(h)
        pe.wait_ge(S(f"sa_ev{h}"), n + 1)
        if prompt:
            pe.matmul(bk[3][r, 0:HD], B.tok[1][:, q, r], B.SA[h][:], start=True, stop=False)
            pe.matmul(bk[3][r, 0:HD], B.tok[2][:, q, r], B.tok[0][:, q, r], start=False, stop=True)
            y = bk[0][r, q * CH:(q + 1) * CH]
            if q:
                pe.matmul(y, B.ST[r, :], B.ar[r, q, 1, :], start=True, stop=False)
            pe.matmul(y, B.SA[h][:], B.UR[h][:, q, 1, :], start=q == 0, stop=False)
            mm = pe.matmul(y, B.tok[0][:, q, r], B.KR[h][:, q, 1, :], start=False, stop=True)
        else:
            pe.wait_ge(S(f"sax{h}"), p + 1)
            y = bk[2][r, 0:NS]
            pe.matmul(y, B.SA[h][0:NS, :], B.sUR[h][:, 1, :], start=True, stop=False)
            pe.matmul(y, B.toks[0][:, r], B.sKR[h][:, 1, :], start=False, stop=False)
            for b in range(DB):
                pe.matmul(y, B.STs[r, b, :], B.rxs[r, b, :], start=False, stop=b == DB - 1)
            pe.matmul(bk[3][r, :], B.toks[1][:, r], B.sax[h][:].rearrange("p b i -> p (b i)"), start=True, stop=False)
            mm = pe.matmul(bk[3][r, :], B.toks[2][:, r], B.vx[:, h].rearrange("p b i -> p (b i)"), start=False, stop=True)
        mm.then_inc(S(f"y_mm{h}"), 1)


def dve_scan(dve, B, p, q):
    S = B.sem
    n = (NCH + 1) * p + q
    for h in range(2):
        r = hs(h)
        if q == NCH:
            dve.wait_ge(S(f"sa_ev{h}"), n + 1)
            dve.tensor_tensor(B.sax[h][:], B.SA[h][0:NS, :].unsqueeze(1).to_broadcast([NS, DB, HD]),
                              B.row_sel[:].unsqueeze(2).to_broadcast([NS, DB, HD]), ALU.mult).then_inc(S(f"sax{h}"), 1)
    for h in range(2):
        r, d = hs(h), B.bank[4 * h + 3]
        dve.wait_ge(S(f"y_mm{h}"), n + 1)
        if q == NCH:
            dve.tensor_tensor(B.STs[r], d[r, :].rearrange("p (b i) -> p b i", b=DB), B.STs[r], ALU.add)
        elif q:
            dve.tensor_tensor(B.ST[r, :], d[r, 0:HD], B.ST[r, :], ALU.add)
        else:
            ins = dve.tensor_scalar(B.ST[r, :], d[r, 0:HD], B.fac[r, 0:1], None, ALU.mult)
        if q:
            dve.drain()
        if q == NCH:
            ins = dve.tensor_tensor(B.STs[r], B.STs[r], B.facs[r, :].unsqueeze(2).to_broadcast([HD, DB, HD]), ALU.mult)
        elif q:
            ins = dve.tensor_scalar(B.ST[r, :], B.ST[r, :], B.fac[r, q:q + 1], None, ALU.mult)
        ins.then_inc(S(f"seq_st{h}"), 1)


def act_pair(act, B, p):
    S, bank, P = B.sem, B.bank, B.p
    if p >= 1:
        act.wait_ge(S("pair_done"), p)
    act.wait_ge(S("st_in_tr"), p + 1)
    act.activation(B.STs[:].rearrange("p b i -> p (b i)"), bank[6][:], ACT.Copy).then_inc(S("st_in"), 1)
    for i, (dst, b) in enumerate([("lw", "w0"), ("a", "a0"), ("g", None)]):
        act.wait_ge(S("lora_mm"), 3 * p + i + 1)
        for h in range(2):
            if b:
                ins = act.activation(P[dst][:, half(h)], bank[2 * i + h][:, 0:HALF], ACT.Sigmoid, bias=vec(B, b)[:, p:p + 1])
            else:
                ins = act.activation(P[dst][:, half(h)], bank[2 * i + h][:, 0:HALF], ACT.Copy)
        ins.then_inc(S("lora_ev"), 1)
    act.wait_ge(S("cum_ready"), p + 1)
    act.activation(P["e1"][:], P["t1"][:], ACT.Exp)
    act.activation(P["e2"][:], P["cum"][:], ACT.Exp)
    act.activation(P["lw"][:], P["cum"][:], ACT.Exp, scale=-1.0)
    act.activation(B.fac[:], B.fac[:], ACT.Exp)
    act.activation(B.facs[:], P["cum"][:, SEQ + DS - 1:T:DS], ACT.Exp).then_inc(S("exps_ready"), 1)
    act.wait_ge(S("kkmax_ready"), p + 1)
    act.activation(P["t2"][:], P["t2"][:], ACT.Sqrt).then_inc(S("kk_rt"), 1)
    act.wait_ge(S("tok_tr"), p + 1)
    for i in range(3):
        act.activation(B.tok[i][:].rearrange("p c t -> p (c t)"), bank[i][:], ACT.Copy)
        ins = act.activation(B.toks[i][:], bank[3][0:NS, i * 128:(i + 1) * 128], ACT.Copy)
    ins.then_inc(S("tok_ev"), 1)
    for s in SQUARE:
        for h in range(2):
            act.wait_ge(S(f"inv_mm{h}"), STEPS * p + s + 1)
            act.activation(B.Lp[h][:].rearrange("p c t -> p (c t)"), bank[4 * h + 1][:], ACT.Copy)
            act.activation(B.Up[h][:].rearrange("p c t -> p (c t)"), bank[4 * h + 2][:], ACT.Copy).then_inc(S(f"inv_act{h}"), 1)
    for q in range(NCH + 1):
        n = (NCH + 1) * p + q
        rows = 128 if q < NCH else NS
        for h in range(2):
            act.wait_ge(S(f"x_mm{h}"), n + 1)
            if q:
                act.wait_ge(S(f"sa_mm{h}"), n)
            act.activation(B.X[h][0:rows, :], bank[4 * h + 1][0:rows, 0:HD], ACT.Copy).then_inc(S(f"x_ev{h}"), 1)
        for h in range(2):
            act.wait_ge(S(f"sa_mm{h}"), n + 1)
            if q:
                act.wait_ge(S(f"y_mm{h}"), n)
            act.activation(B.SA[h][0:rows, :], bank[4 * h + 2][0:rows, 0:HD], ACT.Copy).then_inc(S(f"sa_ev{h}"), 1)
    for h in range(2):
        act.wait_ge(S(f"y_mm{h}"), (NCH + 1) * (p + 1))
        act.activation(P["e1"][hs(h), 0:SEQ], bank[4 * h][hs(h), :], ACT.Copy)
        ins = act.activation(P["e1"][hs(h), SEQ:T], bank[4 * h + 2][hs(h), 0:NS], ACT.Copy)
    ins.then_inc(S("y_ev"), 1)
    act.wait_ge(S("st_out_tr"), p + 1)
    if p >= 1:
        act.wait_ge(S("state_stored"), 64 * p)
    act.activation(B.stout[:, 0, :], bank[3][0:HD, 0:128], ACT.Copy)
    act.activation(B.stout[:, 1:5, :].rearrange("p b j -> p (b j)"), bank[7][0:HD, :], ACT.Copy)
    act.activation(B.stout[:, 5:9, :].rearrange("p b j -> p (b j)"), bank[2][0:HD, :], ACT.Copy).then_inc(S("st_out_ev"), 1)
    act.wait_ge(S("head_means"), 2 * p + 2)
    for h in range(2):
        ins = act.activation(P["t1"][:, half(h)], bank[1 + 4 * h][:, 0:HALF], ACT.Sqrt, bias=B.eps_lnx[:, 0:1])
    ins.then_inc(S("var_rt"), 1)


def dve_pair(dve, B, p):
    S, bank, P = B.sem, B.bank, B.p
    r, k, v = (B.rkv[i][:, p, :] for i in range(3))
    col = lambda name: vec(B, name)[:, p:p + 1]
    if p == 0:
        dve.wait_ge(S("rkv_ev"), 56)
    dve.tensor_scalar(P["kk"][:], k, col("k_k"), None, ALU.mult)
    dve.wait_ge(S("lora_ev"), 3 * p + 1)
    dve.tensor_scalar(P["lw"][:], P["lw"][:], -float(2.718281828459045 ** -0.5), None, ALU.mult)
    dve.drain()
    dve.tensor_tensor(P["t2"][:], P["kk"][:], P["kk"][:], ALU.mult).then_inc(S("kksq_ready"), 1)
    dve.tensor_tensor_scan(P["cum"][:], B.seg_start[:], P["lw"][:], 0.0, ALU.mult, ALU.add)
    dve.drain()
    dve.tensor_copy(B.mid[:], P["cum"][:, CH // 2 - 1:SEQ:CH])
    dve.drain()
    pc = P["cum"][:, 0:SEQ].rearrange("p (c t) -> p c t", c=NCH)
    dve.tensor_tensor(pc, pc, B.mid[:].unsqueeze(2).to_broadcast([128, NCH, CH]), ALU.subtract)
    dve.drain()
    dve.tensor_tensor(B.fac[:, 0:NCH - 1], P["cum"][:, CH - 1:SEQ - CH:CH], B.mid[:, 1:NCH], ALU.add)
    dve.tensor_copy(B.fac[:, NCH - 1:NCH], P["cum"][:, SEQ - 1:SEQ])
    dve.tensor_tensor(P["t1"][:], P["cum"][:], P["lw"][:], ALU.subtract).then_inc(S("cum_ready"), 1)
    dve.wait_ge(S("lora_ev"), 3 * p + 2)
    dve.tensor_scalar(P["km"][:], P["a"][:], -1.0, col("k_a"), ALU.add, ALU.mult)
    dve.drain()
    dve.scalar_tensor_tensor(out=P["km"][:], in0=P["km"][:], scalar=1.0, in1=k, op0=ALU.add, op1=ALU.mult)
    dve.drain()
    dve.scalar_tensor_tensor(out=P["bonus"][:], in0=r, scalar=col("r_k"), in1=P["km"][:], op0=ALU.mult, op1=ALU.mult)\
       .then_inc(S("rk_ready"), 1)
    dve.wait_ge(S("head_sums"), 2 * p + 1)
    for h in range(2):
        ins = dve.tensor_scalar(P["t2"][:, half(h)], bank[6 + h][:, 0:HALF], 1e-24, None, ALU.max)
    ins.then_inc(S("kkmax_ready"), 1)
    dve.wait_ge(S("head_sums"), 2 * p + 2)
    for h in range(2):
        dve.tensor_tensor(P["bonus"][:, half(h)], bank[h][:, 0:HALF], v[:, half(h)], ALU.mult)
    dve.wait_ge(S("exps_ready"), p + 1)
    dve.tensor_tensor(B.ar[:, :, 1, :], r[:, 0:SEQ].rearrange("p (c t) -> p c t", c=NCH),
                      P["e2"][:, 0:SEQ].rearrange("p (c t) -> p c t", c=NCH), ALU.mult)
    dve.tensor_tensor(B.ars[:, 1, :], r[:, SEQ:T], P["e2"][:, SEQ:T], ALU.mult)
    dve.tensor_tensor(P["kh"][:], P["km"][:], P["lw"][:], ALU.mult)
    dve.wait_ge(S("kk_rt"), p + 1)
    dve.reciprocal(P["t2"][:], P["t2"][:])
    dve.drain()
    dve.tensor_tensor(P["kk"][:], P["kk"][:], P["t2"][:], ALU.mult)
    dve.drain()
    dve.scalar_tensor_tensor(out=B.ar[:, :, 0, :], in0=P["kk"][:, 0:SEQ].rearrange("p (c t) -> p c t", c=NCH), scalar=-1.0,
                             in1=P["e1"][:, 0:SEQ].rearrange("p (c t) -> p c t", c=NCH), op0=ALU.mult, op1=ALU.mult)
    dve.scalar_tensor_tensor(out=B.ars[:, 0, :], in0=P["kk"][:, SEQ:T], scalar=-1.0, in1=P["e1"][:, SEQ:T],
                             op0=ALU.mult, op1=ALU.mult)
    dve.tensor_tensor(P["bh"][:], P["kk"][:], P["a"][:], ALU.mult)
    dve.drain()
    dve.tensor_tensor(B.axs[:], B.seg_sel[:], B.ars[:, 0, :].unsqueeze(1).to_broadcast([128, DB, NS]), ALU.mult)
    dve.tensor_tensor(B.rxs[:], B.seg_sel[:], B.ars[:, 1, :].unsqueeze(1).to_broadcast([128, DB, NS]), ALU.mult)
    dve.tensor_tensor(P["bh"][:], P["bh"][:], P["lw"][:], ALU.mult).then_inc(S("grams_ready"), 1)
    dve.wait_ge(S("tok_ev"), p + 1)
    for h in range(2):
        dve.tensor_tensor(B.vx[:, h], B.toks[0][:, hs(h)].unsqueeze(1).to_broadcast([NS, DB, HD]),
                          B.row_sel[:].unsqueeze(2).to_broadcast([NS, DB, HD]), ALU.mult)
    for s in range(STEPS):
        for h in range(2):
            dve_inverse(dve, B, p, s, h)
    for q in range(NCH + 1):
        dve_scan(dve, B, p, q)
    y = P["e1"]
    dve.wait_ge(S("head_means"), 2 * p + 1)
    for h in range(2):
        dve.tensor_tensor(y[:, half(h)], y[:, half(h)], bank[1 + 4 * h][:, 0:HALF], ALU.subtract)
    dve.drain()
    dve.tensor_tensor(P["t2"][:], y[:], y[:], ALU.mult).then_inc(S("ysq_ready"), 1)
    dve.wait_ge(S("var_rt"), p + 1)
    dve.reciprocal(P["t1"][:], P["t1"][:])
    dve.drain()
    dve.tensor_tensor(y[:], y[:], P["t1"][:], ALU.mult)
    dve.drain()
    dve.tensor_scalar(y[:], y[:], col("lnx_w"), col("lnx_b"), ALU.mult, ALU.add)
    dve.drain()
    dve.tensor_tensor(y[:], y[:], P["bonus"][:], ALU.add)
    dve.drain()
    dve.tensor_tensor(r, y[:], P["g"][:], ALU.mult).then_inc(S("pair_done"), 1)


TT = [(i, 128 if i < 4 else NS) for i in range(5)]


def cols(i):
    return slice(i * 128, min((i + 1) * 128, T))


def allocate_moe(nc, B, sb):
    st = ExitStack()
    B.wr = sb(st, "wr", [128, KT, 20])
    B.br = sb(st, "br", [128, 20])
    B.lg = sb(st, "lg", [128, 5, 20])
    B.rt = {n: sb(st, f"rt_{n}", [128, 5, w]) for n, w in
            dict(gmax=1, eg=4, sum=1, rem=1, gm=4, sel=16, ing=4, v1=1, v2=1, o1=4, o2=4, in2=4, ew=1, w1=1, w2=1, eqt=4).items()}
    B.comb = sb(st, "comb", [128, 5, 16])
    B.combT = sb(st, "combT", [16, T])
    B.esel = [sb(st, f"esel{i}", [16, 128]) for i in range(2)]
    B.cb = [sb(st, f"cb{i}", [128, T]) for i in range(2)]
    B.act = sb(st, "act", [128, 4, T])
    B.acc = sb(st, "acc", [128, KT, T])
    B.wg = [sb(st, f"wg{i}", [128, KT, FF]) for i in range(2)]
    B.wu = [sb(st, f"wu{i}", [128, KT, FF]) for i in range(2)]
    B.wd = [sb(st, f"wd{i}", [128, 4, D]) for i in range(2)]
    B.wo = [sb(st, f"wo{i}", [128, KT, 128]) for i in range(4)]
    st.close()


def sp_out_proj(sp, B, n, src):
    S = B.sem
    for m in range(KT):
        g = n * KT + m
        if g >= 4:
            sp.wait_ge(S("out_mm"), 2 * (g - 3))
        for part, rows in src(m):
            sp.dma_start(B.wo[g % 4][part] if part else B.wo[g % 4][:], rows).then_inc(S(f"wo_loaded{g % 4}"), 16)


def pe_out_proj(pe, B, n, x, dmas):
    S = B.sem
    for m in range(KT):
        g = n * KT + m
        pe.wait_ge(S(f"wo_loaded{g % 4}"), dmas[g])
        for h in range(2):
            q = 2 * g + h
            if q % 16 >= 8:
                pe.wait_ge(S("out_ev"), q - 7)
            for k in range(KT):
                mm = pe.matmul(B.bank[q % 8][:, 0:HALF], B.wo[g % 4][:, k, :], x[:, k, half(h)], start=k == 0, stop=k == KT - 1)
            mm.then_inc(S("out_mm"), 1)


def add_gated(dve, B, ps, h, gate, m):
    dst = B.xT[:, m, half(h)]
    w = HALF if h == 0 else HALF - NS
    if h:
        dve.tensor_tensor(B.tmp_s[:, m % 2].rearrange("p (b s) -> p b s", s=DS), ps[:, w:HALF].rearrange("p (b s) -> p b s", s=DS),
                          gate[:, m, 1:NC].unsqueeze(2).to_broadcast([128, DB, DS]), ALU.mult)
        dve.drain()
        dve.tensor_tensor(dst[:, w:HALF], dst[:, w:HALF], B.tmp_s[:, m % 2], ALU.add)
    return dve.scalar_tensor_tensor(out=dst[:, 0:w], in0=ps[:, 0:w], scalar=gate[:, m, 0:1], in1=dst[:, 0:w], op0=ALU.mult, op1=ALU.add)


def dve_out_proj(dve, B, n, gate):
    S = B.sem
    for q in range(16 * n, 16 * n + 16):
        dve.wait_ge(S("out_mm"), q + 1)
        add_gated(dve, B, B.bank[q % 8], q % 2, gate, q % 16 // 2).then_inc(S("out_ev"), 1)


def sp_moe(sp, B, io, l):
    S = B.sem
    sp.wait_ge(S("out_mm"), 16 * (l + 1))
    for src, n, w in [("moe_w_grp", 0, 4), ("moe_w_exp", 4, 16)]:
        sp.dma_start(B.wr[:, :, n:n + w], io[src][l].rearrange("(k p) n -> p k n", p=128)).then_inc(S("router_loaded"), 16)
    for src, n, w in [("moe_b_grp", 0, 4), ("moe_b_exp", 4, 16)]:
        sp.dma_start(B.br[:, n:n + w], io[src][l].rearrange("(a n) -> a n", a=1).to_broadcast([128, w])).then_inc(S("router_loaded"), 16)

    def load(t, i, first=False):
        done = 2 * t + i - 2 + 16 * l
        pick = lambda name: io[name][l, bass.ds(2 * t + i, 1)].rearrange("e (k p) n -> p (e k) n", p=128)
        if not first:
            sp.wait_ge(S("up_mm"), done * 8 + 8)
        sp.dma_start(B.wg[i][:], pick("moe_w_gate")).then_inc(S(f"wgu_loaded{i}"), 16)
        sp.dma_start(B.wu[i][:], pick("moe_w_up")).then_inc(S(f"wgu_loaded{i}"), 16)
        if not first:
            sp.wait_ge(S("down_mm"), done * 16 + 16)
        sp.dma_start(B.wd[i][:], pick("moe_w_down")).then_inc(S(f"wd_loaded{i}"), 16)

    load(0, 0, True)
    load(0, 1, True)
    with sp.Fori(1, E_N // 2) as t:
        for i in range(2):
            load(t, i)


def pe_moe(pe, B, l):
    S, bank = B.sem, B.bank
    pe.wait_ge(S("router_loaded"), 64 * (l + 1))
    pe.wait_ge(S("norm_done"), 2 + 3 * l)
    for t, rows in TT:
        for k in range(KT):
            mm = pe.matmul(bank[2][0:rows, t * 20:(t + 1) * 20], B.fT[:, k, cols(t)], B.wr[:, k, :], start=k == 0, stop=k == KT - 1)
    mm.then_inc(S("router_mm"), 1)
    pe.wait_ge(S("comb_ready"), l + 1)
    for t, rows in TT:
        b = bank[3] if t < 4 else bank[4]
        mm = pe.transpose(b[0:16, t % 4 * 128:t % 4 * 128 + rows], B.comb[0:rows, t, :], B.ident[0:rows, 0:rows])
    mm.then_inc(S("comb_tr"), 1)
    pe.wait_ge(S("comb_ev"), l + 1)
    with pe.Fori(0, E_N // 2) as t:
        for i in range(2):
            pe_expert(pe, B, i, 2 * t + (16 * l + i))


def pe_expert(pe, B, i, e):
    S, bank = B.sem, B.bank
    pe.wait_ge(S("esel_ready"), e + 1)
    for h in range(2):
        mm = pe.matmul(bank[6 + h][:, 0:HALF], B.esel[i][:], B.combT[:, half(h)], start=True, stop=True)
    mm.then_inc(S("cb_mm"), 1)
    pe.wait_ge(S(f"wgu_loaded{i}"), (e - i) * 16 + 32)
    for s in range(8):
        m, h = s // 2, s % 2
        if s == 3:
            pe.wait_ge(S("cb_ev"), e + 1)
        if s >= 4:
            pe.wait_ge(S("act_ready"), e * 8 + (s - 3))
        for w, b, done in [(B.wg[i], bank[2 * s % 8], "gate_mm"), (B.wu[i], bank[(2 * s + 1) % 8], "up_mm")]:
            for k in range(KT):
                mm = pe.matmul(b[:, 0:HALF], w[:, k, m * 128:(m + 1) * 128], B.fT[:, k, half(h)], start=k == 0, stop=k == KT - 1)
            mm.then_inc(S(done), 1)
    pe.wait_ge(S("act_ready"), e * 8 + 8)
    pe.wait_ge(S(f"wd_loaded{i}"), (e - i) * 8 + 16)
    for q in range(16):
        m, h = q // 2, q % 2
        if q >= 8:
            pe.wait_ge(S("acc_ev"), e * 16 + (q - 7))
        for k in range(4):
            mm = pe.matmul(bank[q % 8][:, 0:HALF], B.wd[i][:, k, m * 128:(m + 1) * 128], B.act[:, k, half(h)], start=k == 0, stop=k == 3)
        mm.then_inc(S("down_mm"), 1)


def act_moe(act, B, l):
    S, bank, R = B.sem, B.bank, B.rt
    act.wait_ge(S("route_exp"), 2 * l + 1)
    act.activation(R["eg"][:], R["eg"][:], ACT.Exp).then_inc(S("route_exped"), 1)
    act.wait_ge(S("route_exp"), 2 * l + 2)
    act.activation(R["ew"][:], R["ew"][:], ACT.Exp).then_inc(S("route_exped"), 1)
    act.wait_ge(S("comb_tr"), l + 1)
    act.activation(B.combT[:, 0:SEQ], bank[3][0:16, :], ACT.Copy)
    act.activation(B.combT[:, SEQ:T], bank[4][0:16, 0:NS], ACT.Copy).then_inc(S("comb_ev"), 1)
    with act.Fori(0, E_N // 2) as t:
        for i in range(2):
            e = 2 * t + (16 * l + i)
            act.wait_ge(S("cb_mm"), e + 1)
            for h in range(2):
                ins = act.activation(B.cb[i][:, half(h)], bank[6 + h][:, 0:HALF], ACT.Copy)
            ins.then_inc(S("cb_ev"), 1)
            for s in range(8):
                act.wait_ge(S("gate_mm"), e * 8 + (s + 1))
                act.activation(B.act[:, s // 2, half(s % 2)], bank[2 * s % 8][:, 0:HALF], ACT.Silu).then_inc(S("silu_done"), 1)


def first_max(dve, R, value, top, out, n):
    dve.tensor_tensor(R["eqt"][:, :, 0:n], value, top[:].to_broadcast([128, 5, n]), ALU.is_equal)
    dve.memset(R["rem"][:], 1.0)
    dve.drain()
    for j in range(n):
        dve.tensor_tensor(out[:, :, j:j + 1], R["eqt"][:, :, j:j + 1], R["rem"][:], ALU.mult)
        dve.drain()
        dve.tensor_tensor(R["rem"][:], R["rem"][:], out[:, :, j:j + 1], ALU.subtract)
        dve.drain()


def dve_moe(dve, B, l):
    S, bank, R = B.sem, B.bank, B.rt
    dve.wait_ge(S("router_loaded"), 64 * (l + 1))
    dve.memset(B.lg[:], 0.0)
    dve.drain()
    dve.wait_ge(S("router_mm"), l + 1)
    dve.tensor_tensor(B.lg[:, 0:4], bank[2][:, 0:80].rearrange("p (t c) -> p t c", t=4), B.br[:].unsqueeze(1).to_broadcast([128, 4, 20]), ALU.add)
    dve.tensor_tensor(B.lg[0:NS, 4], bank[2][0:NS, 80:100], B.br[0:NS], ALU.add)
    dve.drain()
    dve.tensor_reduce(R["gmax"][:], B.lg[:, :, 0:4], AX.X, ALU.max)
    dve.drain()
    dve.tensor_tensor(R["eg"][:], B.lg[:, :, 0:4], R["gmax"][:].to_broadcast([128, 5, 4]), ALU.subtract).then_inc(S("route_exp"), 1)
    first_max(dve, R, B.lg[:, :, 0:4], R["gmax"], R["gm"], 4)
    dve.wait_ge(S("route_exped"), 2 * l + 1)
    dve.tensor_reduce(R["sum"][:], R["eg"][:], AX.X, ALU.add)
    dve.tensor_tensor(R["sel"][:].rearrange("p t (g e) -> p t g e", g=4), B.lg[:, :, 4:20].rearrange("p t (g e) -> p t g e", g=4),
                      R["gm"][:].unsqueeze(3).to_broadcast([128, 5, 4, 4]), ALU.mult)
    dve.drain()
    dve.tensor_reduce(R["ing"][:], R["sel"][:].rearrange("p t (g e) -> p t e g", g=4), AX.X, ALU.add)
    dve.reciprocal(R["sum"][:], R["sum"][:])
    dve.drain()
    dve.tensor_reduce(R["v1"][:], R["ing"][:], AX.X, ALU.max)
    dve.drain()
    first_max(dve, R, R["ing"][:], R["v1"], R["o1"], 4)
    dve.scalar_tensor_tensor(out=R["in2"][:], in0=R["o1"][:], scalar=NEG, in1=R["ing"][:], op0=ALU.mult, op1=ALU.add)
    dve.drain()
    dve.tensor_reduce(R["v2"][:], R["in2"][:], AX.X, ALU.max)
    dve.drain()
    dve.tensor_tensor(R["ew"][:], R["v2"][:], R["v1"][:], ALU.subtract).then_inc(S("route_exp"), 1)
    first_max(dve, R, R["in2"][:], R["v2"], R["o2"], 4)
    dve.wait_ge(S("route_exped"), 2 * l + 2)
    dve.tensor_scalar(R["w1"][:], R["ew"][:], 1.0, None, ALU.add)
    dve.drain()
    dve.reciprocal(R["w1"][:], R["w1"][:])
    dve.drain()
    dve.tensor_tensor(R["w1"][:], R["w1"][:], R["sum"][:], ALU.mult)
    dve.drain()
    dve.tensor_tensor(R["w2"][:], R["w1"][:], R["ew"][:], ALU.mult)
    dve.tensor_tensor(R["o1"][:], R["o1"][:], R["w1"][:].to_broadcast([128, 5, 4]), ALU.mult)
    dve.drain()
    dve.tensor_tensor(R["o2"][:], R["o2"][:], R["w2"][:].to_broadcast([128, 5, 4]), ALU.mult)
    dve.drain()
    dve.tensor_tensor(R["o1"][:], R["o1"][:], R["o2"][:], ALU.add)
    dve.drain()
    dve.tensor_tensor(B.comb[:].rearrange("p t (g e) -> p t g e", g=4), R["gm"][:].unsqueeze(3).to_broadcast([128, 5, 4, 4]),
                      R["o1"][:].unsqueeze(2).to_broadcast([128, 5, 4, 4]), ALU.mult).then_inc(S("comb_ready"), 1)
    dve.memset(B.acc[:], 0.0)
    with dve.Fori(0, E_N // 2) as t:
        for i in range(2):
            e = 2 * t + (16 * l + i)
            dve.tensor_copy(B.esel[i][:], B.ident[0:16, bass.ds(2 * t + i, 1)].to_broadcast([16, 128])).then_inc(S("esel_ready"), 1)
            dve.wait_ge(S("cb_ev"), e + 1)
            for s in range(8):
                a = B.act[:, s // 2, half(s % 2)]
                dve.wait_ge(S("silu_done"), e * 8 + (s + 1))
                dve.wait_ge(S("up_mm"), e * 8 + (s + 1))
                dve.tensor_tensor(a, bank[(2 * s + 1) % 8][:, 0:HALF], a, ALU.mult)
                dve.drain()
                dve.tensor_tensor(a, a, B.cb[i][:, half(s % 2)], ALU.mult).then_inc(S("act_ready"), 1)
            for q in range(16):
                dve.wait_ge(S("down_mm"), e * 16 + (q + 1))
                acc = B.acc[:, q // 2, half(q % 2)]
                dve.tensor_tensor(acc, bank[q % 8][:, 0:HALF], acc, ALU.add).then_inc(S("acc_ev"), 1)
    dve.drain()
    gate = mod(B, l, 5)
    for m in range(KT):
        for h in range(2):
            ins = add_gated(dve, B, B.acc[:, m, half(h)], h, gate, m)
    dve.drain()
    dve.nop().then_inc(S("x_ready"), 1)


NCP, NCS = 31, 15
NCK = DB * NCS
CK = 4 * NCK + 4 * NCP
SK = PAST + NS
TABLE = {}
_at = 0
for _n, _w in [("dist_p", 512), ("dist_c", 4 * NCP), ("row_valid", 4), ("dist_s", 2 * SK), ("dist_cs", 2 * NCK), ("spread", 256),
               ("head_sel", 4), ("slope", 4)]:
    TABLE[_n] = (_at, _at + _w)
    _at += _w
TABLE_W = _at
FAR = 1.0e32


def slope_of(h):
    return 2.0 ** (-8.0 * (h + 1) / NH)


def shape_table():
    import numpy as np
    tab = np.zeros((128, TABLE_W), np.float32)
    p = np.arange(128)

    def put(name, value):
        a, b = TABLE[name]
        tab[:value.shape[0], a:b] = value.reshape(value.shape[0], -1)

    d = p[:, None] - np.arange(512)[None] + 384
    put("dist_p", np.where(d >= 0, d, FAR))
    q = np.arange(4)[None, :, None] * 128 + p[:, None, None]
    d = q - (16 * np.arange(NCP)[None, None] + 31)
    put("dist_c", np.where(d >= 0, d, FAR))
    put("row_valid", (q[:, :, 0] >= 31).astype(np.float32))
    b4, hg, t = p // 32, p % 16 // 4, p % 4
    bq = np.arange(2)[None, :, None]
    past = (PAST + t)[:, None, None] - np.arange(PAST)[None, None] + 0 * bq
    new = np.arange(NS)[None, None]
    own = (new // DS == 4 * bq + b4[:, None, None]) & (new % DS <= t[:, None, None])
    put("dist_s", np.concatenate([past, np.where(own, t[:, None, None] - new % DS, FAR)], 2))
    c = np.arange(NCK)[None, None]
    d = (PAST + t)[:, None, None] - (16 * (c % NCS) + 31)
    put("dist_cs", np.where(c // NCS == 4 * bq + b4[:, None, None], d, FAR))
    tok = np.arange(NS)[:, None, None]
    put("spread", (tok == (4 * bq[0][None] + b4[None, None]) * DS + t[None, None]).astype(np.float32))
    put("head_sel", (hg[:, None] == np.arange(HG)[None]).astype(np.float32))
    put("slope", np.stack([-2.0 ** (-8.0 * (HG * g + hg + 1) / NH) for g in range(G)], 1))
    return tab


def allocate_nsa(nc, B, sb):
    kv = ExitStack()
    B.kvtok = sb(kv, "kvtok", [128, 5, 1536])
    B.kT = sb(kv, "kT", [128, 2, 2, T])
    B.kcT = sb(kv, "kcT", [128, 2, NCK + NCP])
    B.vcs = sb(kv, "vcs", [NCK, G, HD])
    B.vcp = sb(kv, "vcp", [NCP, G, HD])
    B.tab = sb(kv, "tab", [128, TABLE_W])
    B.pages = sb(kv, "pages", [1, 16], I32)
    B.pbr = sb(kv, "pbr", [36, 128])
    B.pbT = sb(kv, "pbT", [128, 36])
    B.posb = sb(kv, "posb", [128, 4])
    B.cw2 = sb(kv, "cw2", [128, 2, 2, HD])
    st = ExitStack()
    B.wkv = sb(st, "wkv", [128, KT, 1536])
    st.close()
    st = ExitStack()
    B.cs = sb(st, "cs", [128, 8, 16, HD])
    B.cp = sb(st, "cp", [64, G, 16, HD])
    B.kvT = sb(st, "kvT", [128, G, 8, 160])
    B.cw1 = sb(st, "cw1", [128, 16, 256])
    B.hid = sb(st, "hid", [128, 2, CK])
    st.close()
    B.kTs = sb(kv, "kTs", [128, 2, 2, DB, PAST])
    B.vp = sb(kv, "vp", [128, 2, 16, 256])
    B.qT = sb(kv, "qT", [128, KT, T])
    B.gates = sb(kv, "gates", [128, 5, 48])
    B.gs = sb(kv, "gs", [128, 2, G, 3])
    B.gtmp = sb(kv, "gtmp", [128, 2, 48])
    B.qs = sb(kv, "qs", [128, 2, DB, 32])
    st = ExitStack()
    B.kp = sb(st, "kp", [128, 16, 256])
    B.wq = [sb(st, f"wq{i}", [128, KT, 128]) for i in range(2)]
    B.wgt = sb(st, "wgt", [128, KT, 48])
    st.close()
    st = ExitStack()
    B.sc = [sb(st, f"sc{i}", [128, 2, 512]) for i in range(2)]
    B.PT = [sb(st, f"PT{i}", [128, 2, 512]) for i in range(2)]
    B.nm = [sb(st, f"nm{i}", [128, 3]) for i in range(2)]
    B.sm = [sb(st, f"sm{i}", [128, 3]) for i in range(2)]
    B.scc = [sb(st, f"scc{i}", [128, 4, NCP]) for i in range(2)]
    B.nmc = sb(st, "nmc", [128, 4])
    B.smc = sb(st, "smc", [128, 4])
    B.PTc = [sb(st, f"PTc{i}", [NCP, 512]) for i in range(2)]
    st.close()
    kv.close()
    st = ExitStack()
    B.ytok = sb(st, "ytok", [128, 5, D])
    st.close()


def table(B, name, rows=128):
    a, b = TABLE[name]
    return B.tab[0:rows, a:b]


def gslice(g):
    return slice(64 * (g % 2), 64 * (g % 2) + 64), g // 2


def sp_kv(nc, sp, B, io, out):
    S = B.sem
    sp.wait_ge(S("x_ready"), 2)
    for c in range(3):
        sp.dma_start(B.wkv[:, :, c * 512:(c + 1) * 512], io["w_kv"][:, c * 512:(c + 1) * 512].rearrange("(k p) n -> p k n", p=128))\
          .then_inc(S("wkv_loaded"), 16)
    sp.dma_start(B.tab[:], io["table"]).then_inc(S("small_loaded"), 16)
    sp.dma_start(B.pages[:], io["page_table"].rearrange("b n -> (b n)").rearrange("(a n) -> a n", a=1)).then_inc(S("pages_loaded"), 16)
    sp.dma_start(B.pbr[0:32], io["cmp_pos"].rearrange("z (c l) d -> (z c) (l d)", l=2)).then_inc(S("small_loaded"), 16)
    sp.dma_start(B.pbr[32:36], io["cmp_b1"].rearrange("z (m p) -> (z m) p", p=128)).then_inc(S("small_loaded"), 16)
    sp.dma_start(B.cw2[:], io["cmp_w2"].rearrange("z (m p) d -> p z m d", p=128)).then_inc(S("small_loaded"), 16)
    for src, dst in [(io["cache_win_kv"], out["win_sample"][:, 0:PAST])]:
        sp.dma_start(dst.rearrange("b t s g d -> b t (s g d)"), src.rearrange("b t s g d -> b t (s g d)")).then_inc(S("kv_stored"), 16)
    sp.wait_ge(S("kv_ev"), 15)
    sp.dma_start(out["kv_prompt"].rearrange("b (t p) s g d -> p (b t) (s g d)", p=128), B.kvtok[:, 0:4, 0:1024]).then_inc(S("kvp_stored"), 16)
    sp.dma_start(out["win_prompt"].rearrange("b (t p) s g d -> p (b t) (s g d)", p=128), B.kvtok[:, 0:4, 1024:1536]).then_inc(S("kv_stored"), 16)
    sp.dma_start(out["kv_sample"].rearrange("b t s g d -> (b t) (s g d)"), B.kvtok[0:NS, 4, 0:1024]).then_inc(S("kv_stored"), 16)
    for b in range(DB):
        sp.dma_start(out["win_sample"][b, PAST:PAST + DS].rearrange("t s g d -> t (s g d)"), B.kvtok[b * DS:(b + 1) * DS, 4, 1024:1536])\
          .then_inc(S("kv_stored"), 16)
    sp.dma_start(B.cw1[:], io["cmp_w1"][0].rearrange("(c p) h -> p c h", p=128)).then_inc(S("cw1_loaded"), 16)
    sp.wait_ge(S("pages_loaded"), 16)
    for q in range(16):
        page = sp.value_load(B.pages[0:1, q:q + 1], min_val=0, max_val=NPOOL - 1)
        rows = io["cache_nsa_kv"][bass.ds(page, 1)].rearrange("a (n l) s g d -> (a n) l (s g) d", l=16)
        for c in range(8):
            sp.dma_start(B.cs[8 * q:8 * q + 8, c], rows[:, :, c, :]).then_inc(S("cs_loaded"), 16)
    sp.wait_ge(S("kvp_stored"), 16)
    rows = out["kv_prompt"].rearrange("b (n l) s g d -> (b n) l s g d", l=16)
    for z in range(2):
        for g in range(G):
            sp.dma_start(B.cp[32 * z:32 * z + 32, g], rows[:, :, z, g, :]).then_inc(S("cs_loaded"), 16)
    sp.wait_ge(S("hid_mm"), 1)
    sp.dma_start(B.cw1[:], io["cmp_w1"][1].rearrange("(c p) h -> p c h", p=128)).then_inc(S("cw1_loaded"), 16)
    sp.wait_ge(S("cmp_done"), 1)
    for br in range(2):
        if br:
            sp.wait_ge(S("kts_tr"), 8)
        for q in range(16):
            if br:
                row = lambda s: io["cache_win_kv"][q // 2:q // 2 + 1, q % 2 * 128:q % 2 * 128 + 128, s]
            else:
                page = sp.value_load(B.pages[0:1, q:q + 1], min_val=0, max_val=NPOOL - 1)
                row = lambda s: io["cache_nsa_kv"][bass.ds(page, 1), :, 2 + s]
            sp.dma_start(B.kp[:, q, :], row(0).rearrange("a t g d -> t (a g d)")).then_inc(S("kp_loaded"), 16)
            sp.dma_start(B.vp[:, br, q, :], row(1).rearrange("a t g d -> t (a g d)")).then_inc(S("vp_loaded"), 16)
    sp.dma_start(B.wgt[:], io["nsa_w_qg"][0, :, D:D + 48].rearrange("(k p) n -> p k n", p=128)).then_inc(S("wgt_loaded"), 16)
    w_q = io["nsa_w_qg"][0, :, 0:D].rearrange("(k p) (gp g2 hg d) -> p k gp g2 hg d", p=128, gp=2, g2=2, hg=HG)
    for j in range(KT):
        if j >= 2:
            sp.wait_ge(S("q_mm"), 2 * (j - 1))
        for g2 in range(2):
            sp.dma_start(B.wq[j % 2][:, :, g2 * HD:(g2 + 1) * HD], w_q[:, :, j // 4, g2, j % 4, :]).then_inc(S(f"wq_loaded{j % 2}"), 16)


def pe_kv(pe, B):
    S, bank, ident = B.sem, B.bank, B.ident
    pe.wait_ge(S("wkv_loaded"), 48)
    pe.wait_ge(S("norm_done"), 3)
    for n in range(15):
        t, c = n // 3, n % 3
        rows = TT[t][1]
        if n >= 8:
            pe.wait_ge(S("kv_ev"), n - 7)
        for k in range(KT):
            mm = pe.matmul(bank[n % 8][0:rows, :], B.fT[:, k, cols(t)], B.wkv[:, k, c * 512:(c + 1) * 512], start=k == 0, stop=k == KT - 1)
        mm.then_inc(S("kv_mm"), 1)
    pe.wait_ge(S("kv_ev"), 15)
    for n in range(4):
        br, gp = n // 2, n % 2
        at = (2 + 2 * br) * 256 + gp * 128
        for t in range(4):
            mm = pe.transpose(bank[n][:, t * 128:(t + 1) * 128], B.kvtok[:, t, at:at + 128], ident[:])
        mm.then_inc(S("kt_tr"), 1)
    for n in range(4):
        at = (2 + 2 * (n // 2)) * 256 + n % 2 * 128
        pe.transpose(bank[4][:, n * NS:(n + 1) * NS], B.kvtok[0:NS, 4, at:at + 128], ident[0:NS, 0:NS])
    pe.wait_ge(S("small_loaded"), 64)
    pe.transpose(bank[4][:, 128:164], B.pbr[:], ident[0:36, 0:36]).then_inc(S("kt_tr"), 1)
    pe.wait_ge(S("kt_ev"), 5)
    pe.wait_ge(S("cs_loaded"), 16 * 136)
    for z in range(2):
        for n in range(16):
            a = 16 * z + n
            if a >= 8:
                pe.wait_ge(S("kvt_ev"), a - 7)
            if z and n == 0:
                pe.wait_ge(S("cmp_ev"), 1)
                pe.wait_ge(S("hid_ev"), 4)
            for q in range(2):
                g, lp = (2 * n + q) // 8, (2 * n + q) % 8
                cz = slice(32 * z, 32 * z + 32)
                pe.transpose(bank[n % 8][:, q * 160:q * 160 + 128], B.cs[:, 4 * z + g, 2 * lp:2 * lp + 2].rearrange("p l d -> p (l d)"), ident[:])
                mm = pe.transpose(bank[n % 8][:, q * 160 + 128:q * 160 + 160], B.cp[cz, g, 2 * lp:2 * lp + 2].rearrange("p l d -> p (l d)"),
                                  ident[cz, cz])
            mm.then_inc(S("kvt_tr"), 1)
        pe.wait_ge(S("kvt_ev"), 16 * (z + 1))
        pe.wait_ge(S("cw1_loaded"), 16 * (z + 1))
        for m in range(2):
            for c in range(16):
                mm = pe.matmul(bank[4][:, m:m + 1], B.cw1[:, c, m * 128:(m + 1) * 128], B.pbT[:, z * 16 + c:z * 16 + c + 1],
                               start=c == 0, stop=c == 15)
        mm.then_inc(S("pos_mm"), 1)
        for m in range(2):
            for part in range(2):
                for c in range(16):
                    r, lp = c // 8, c % 8
                    v = B.kvT[:, :, lp, 0:128].rearrange("p g (b n) -> p g b n", b=DB)[:, :, :, r:r + NCS] if part == 0 else \
                        B.kvT[:, :, lp, 128 + r:128 + r + NCP]
                    o = bank[2 * m + part][:, 0:4 * NCK].rearrange("p (g b n) -> p g b n", g=G, b=DB) if part == 0 else \
                        bank[2 * m + part][:, 0:4 * NCP].rearrange("p (g n) -> p g n", g=G)
                    mm = pe.matmul(o, B.cw1[:, c, m * 128:(m + 1) * 128], v, start=c == 0, stop=c == 15)
        mm.then_inc(S("hid_mm"), 1)
        pe.wait_ge(S("hid_ev"), 4 * (z + 1))
        for g in range(G):
            r, gp = gslice(g)
            for part, w in [(0, NCK), (1, NCP)]:
                at = g * NCK if part == 0 else 4 * NCK + g * NCP
                for m in range(2):
                    if z == 0:
                        o = bank[5][r, gp * 151 + part * NCK:gp * 151 + part * NCK + w]
                        mm = pe.matmul(o, B.cw2[:, z, m, :], B.hid[:, m, at:at + w], start=m == 0, stop=m == 1)
                    else:
                        mm = pe.matmul(bank[5 + part][0:w, g * HD:(g + 1) * HD], B.hid[:, m, at:at + w], B.cw2[:, z, m, :],
                                       start=m == 0, stop=m == 1)
        mm.then_inc(S("cmp_mm"), 1)
    pe.wait_ge(S("cmp_ev"), 2)
    for br in range(2):
        pe.wait_ge(S("kp_loaded"), 256 * (br + 1))
        for n in range(8):
            gp, bp = n // 4, n % 4
            if 8 * br + n >= 8:
                pe.wait_ge(S("kts_ev"), 8 * br + n - 7)
            for q in range(4):
                mm = pe.transpose(bank[n][:, q * 128:(q + 1) * 128], B.kp[:, 4 * bp + q, gp * 128:(gp + 1) * 128], ident[:])
            mm.then_inc(S("kts_tr"), 1)
    pe.wait_ge(S("norm_done"), 4)
    for j in range(KT):
        pe.wait_ge(S(f"wq_loaded{j % 2}"), 32 * (j // 2 + 1))
        for h in range(2):
            n = 2 * j + h
            if n >= 8:
                pe.wait_ge(S("q_ev"), n - 7)
            else:
                pe.wait_ge(S("kts_ev"), 9 + n)
            for k in range(KT):
                mm = pe.matmul(bank[n % 8][:, 0:HALF], B.wq[j % 2][:, k, :], B.fT[:, k, half(h)], start=k == 0, stop=k == KT - 1)
            mm.then_inc(S("q_mm"), 1)
    pe.wait_ge(S("wgt_loaded"), 16)
    pe.wait_ge(S("q_ev"), 16)
    for t, rows in TT:
        for k in range(KT):
            mm = pe.matmul(bank[0][0:rows, t * 48:(t + 1) * 48], B.fT[:, k, cols(t)], B.wgt[:, k, :], start=k == 0, stop=k == KT - 1)
    mm.then_inc(S("gate_mm1"), 1)
    pe.wait_ge(S("gates_ready"), 1)
    for bq in range(2):
        a = TABLE["spread"][0] + bq * 128
        mm = pe.matmul(bank[1][:, bq * 48:(bq + 1) * 48], B.tab[0:NS, a:a + 128], B.gates[0:NS, 4, :], start=True, stop=True)
    mm.then_inc(S("gspread_mm"), 1)
    pe_attend(pe, B)


UNITS = [(h, i) for h in range(NH) for i in range(4)]
SUNITS = [(bq, g) for bq in range(2) for g in range(G)]

NU = len(UNITS)


def unit(h):
    g = h // HG
    r, gp = gslice(g)
    return g, r, gp, gp * 4 + h % HG


def pe_attend(pe, B):
    S, bank, ident = B.sem, B.bank, B.ident
    U = len(UNITS)
    pe.wait_ge(S("gs_ready"), 1)

    def scores(u):
        h, i = UNITS[u]
        g, r, gp, j = unit(h)
        if u >= 2:
            pe.wait_ge(S("sc_ready"), u - 1)
        for br in range(2):
            mm = pe.matmul(bank[2 * (u % 2) + br][:, 0:128 * (i + 1)], B.qT[r, j, i * 128:(i + 1) * 128], B.kT[r, br, gp, 0:128 * (i + 1)],
                           start=True, stop=True)
        mm.then_inc(S("sc_mm"), 1)

    def cmp_scores(h):
        g, r, gp, j = unit(h)
        if h >= 1:
            pe.wait_ge(S("ptc_ev"), h)
        for i in range(4):
            mm = pe.matmul(bank[6][:, i * NCP:(i + 1) * NCP], B.qT[r, j, i * 128:(i + 1) * 128], B.kcT[r, gp, NCK:NCK + NCP],
                           start=True, stop=True)
        mm.then_inc(S("scc_mm"), 1)

    def cmp_turn(h):
        pe.wait_ge(S("pc_ready"), h + 1)
        for i in range(4):
            mm = pe.transpose(bank[6][0:NCP, i * 128:(i + 1) * 128], B.scc[h % 2][:, i, :], ident[:])
        mm.then_inc(S("ptc_tr"), 1)

    def turn(u):
        h, i = UNITS[u]
        pe.wait_ge(S("p_ready"), u + 1)
        if u >= 1:
            pe.wait_ge(S("pt_ev"), u)
        for br in range(2):
            for kt in range(i + 1):
                mm = pe.transpose(bank[4 + br][:, kt * 128:(kt + 1) * 128], B.sc[u % 2][:, br, kt * 128:(kt + 1) * 128], ident[:])
        mm.then_inc(S("pt_tr"), 1)

    def values(u):
        h, i = UNITS[u]
        g, r, gp, j = unit(h)
        pe.wait_ge(S("pt_ev"), u + 1)
        if i == 0:
            pe.wait_ge(S("ptc_ev"), h + 1)
            if h >= 1:
                pe.wait_ge(S("o_ev"), h)
        o = bank[7][r, i * 128:(i + 1) * 128]
        pe.matmul(o, B.vcp[:, g, :], B.PTc[h % 2][:, i * 128:(i + 1) * 128], start=True, stop=False)
        for br in range(2):
            for kt in range(i + 1):
                v = (3 + 2 * br) * 256 + g * HD
                mm = pe.matmul(o, B.kvtok[:, kt, v:v + HD], B.PT[u % 2][:, br, kt * 128:(kt + 1) * 128], start=False,
                               stop=br == 1 and kt == i)
        mm.then_inc(S("pv_mm"), 1)

    for s in range(U + 2):
        if s < U:
            scores(s)
            if UNITS[s][1] == 0:
                cmp_scores(UNITS[s][0])
        if s >= 1 and s - 1 < U:
            turn(s - 1)
            if UNITS[s - 1][1] == 0:
                cmp_turn(UNITS[s - 1][0])
        if s >= 2:
            values(s - 2)
    pe.wait_ge(S("o_ev"), NH)
    pe.wait_ge(S("vp_loaded"), 512)

    def s_scores(u):
        bq, g = SUNITS[u]
        r, gp = gslice(g)
        if u >= 1:
            pe.wait_ge(S("sc_ready"), NU + u)
        for br in range(2):
            b_ = bank[2 * (u % 2) + br]
            for b in range(4):
                pe.matmul(b_[32 * b:32 * b + 32, 0:PAST], B.qs[r, gp, 4 * bq + b, :], B.kTs[r, br, gp, 4 * bq + b, :], start=True, stop=True)
            qall = B.qs[r, gp, 4 * bq:4 * bq + 4, :].rearrange("p b c -> p (b c)")
            pe.matmul(b_[:, PAST:SK], qall, B.kT[r, br, gp, SEQ:T], start=True, stop=True)
        pe.matmul(bank[6][:, 0:NCK], qall, B.kcT[r, gp, 0:NCK], start=True, stop=True).then_inc(S("sc_mm"), 1)

    def s_turn(u):
        pe.wait_ge(S("p_ready"), NU + u + 1)
        if u >= 1:
            pe.wait_ge(S("pt_ev"), NU + u)
        P = s_probs(B, u)
        for br in range(2):
            for kt in range(2):
                pe.transpose(bank[4 + br][:, kt * 128:(kt + 1) * 128], P[br][:, kt * 128:(kt + 1) * 128], ident[:])
            mm = pe.transpose(bank[4 + br][0:NS, 256:384], P[br][:, PAST:SK], ident[:])
        mm = pe.transpose(bank[4][0:NCK, 384:512], P[2], ident[:])
        mm.then_inc(S("pt_tr"), 1)

    def s_values(u):
        bq, g = SUNITS[u]
        r, gp = gslice(g)
        pe.wait_ge(S("pt_ev"), NU + u + 1)
        if u >= 1:
            pe.wait_ge(S("so_ev"), u)
        PT = B.PT[u % 2]
        for b in range(4):
            c = slice(32 * b, 32 * b + 32)
            o = bank[7][r, c]
            pe.matmul(o, B.vcs[:, g, :], PT[0:NCK, 0, 384:512][:, c], start=True, stop=False)
            for br in range(2):
                for kt in range(2):
                    pe.matmul(o, B.vp[:, br, 2 * (4 * bq + b) + kt, g * HD:(g + 1) * HD], PT[:, br, kt * 128:(kt + 1) * 128][:, c],
                              start=False, stop=False)
                v = (3 + 2 * br) * 256 + g * HD
                mm = pe.matmul(o, B.kvtok[0:NS, 4, v:v + HD], PT[0:NS, br, 256:384][:, c], start=False, stop=br == 1)
        mm.then_inc(S("pv_mm"), 1)

    U = len(SUNITS)
    for s in range(U + 2):
        if s < U:
            s_scores(s)
        if s >= 1 and s - 1 < U:
            s_turn(s - 1)
        if s >= 2:
            s_values(s - 2)


def s_probs(B, u):
    v = B.sc[u % 2][:].rearrange("p a b -> p (a b)")
    return [v[:, 0:SK], v[:, SK:2 * SK], v[:, 2 * SK:2 * SK + NCK]]


def act_kv(act, B):
    S, bank = B.sem, B.bank
    for n in range(15):
        act.wait_ge(S("kv_mm"), n + 1)
        rows = TT[n // 3][1]
        act.activation(B.kvtok[0:rows, n // 3, n % 3 * 512:n % 3 * 512 + 512], bank[n % 8][0:rows, :], ACT.Copy).then_inc(S("kv_ev"), 1)
    for z in range(2):
        act.wait_ge(S("hid_mm"), z + 1)
        act.wait_ge(S("posb_ready"), z + 1)
        if z:
            act.wait_ge(S("cmp_mm"), 1)
        for m in range(2):
            bias = B.posb[:, 2 * z + m:2 * z + m + 1]
            act.activation(B.hid[:, m, 0:4 * NCK], bank[2 * m][:, 0:4 * NCK], ACT.Gelu_apprx_tanh, bias=bias).then_inc(S("hid_ev"), 1)
            act.activation(B.hid[:, m, 4 * NCK:CK], bank[2 * m + 1][:, 0:4 * NCP], ACT.Gelu_apprx_tanh, bias=bias).then_inc(S("hid_ev"), 1)
    for n in range(16):
        act.wait_ge(S("q_mm"), n + 1)
        if n == 0:
            act.wait_ge(S("cmp_done"), 1)
        act.activation(B.qT[:, n // 2, half(n % 2)], bank[n % 8][:, 0:HALF], ACT.Copy, scale=HD ** -0.5).then_inc(S("q_ev"), 1)
    act.wait_ge(S("gate_mm1"), 1)
    act.activation(B.gates[:, 0:4].rearrange("p t c -> p (t c)"), bank[0][:, 0:192], ACT.Sigmoid)
    act.activation(B.gates[0:NS, 4], bank[0][0:NS, 192:240], ACT.Sigmoid).then_inc(S("gates_ready"), 1)
    U = len(UNITS)
    for s in range(U + 1):
        if s < U:
            h, i = UNITS[s]
            x = s % 2
            act.wait_ge(S("sc_ready"), s + 1)
            for br in range(2):
                v = B.sc[x][:, br, 0:128 * (i + 1)]
                ins = act.activation(v, v, ACT.Exp, bias=B.nm[x][:, br:br + 1], accum_out=B.sm[x][:, br:br + 1])
            ins.then_inc(S("exp_done"), 1)
            if i == 0:
                act.wait_ge(S("scc_ready"), h + 1)
                act.activation(B.scc[h % 2][:], B.scc[h % 2][:], ACT.Exp).then_inc(S("expc_done"), 1)
        if s >= 1:
            h, i = UNITS[s - 1]
            x = (s - 1) % 2
            act.wait_ge(S("pt_tr"), s)
            if s >= 3:
                act.wait_ge(S("pv_mm"), s - 2)
            for br in range(2):
                ins = act.activation(B.PT[x][:, br, 0:128 * (i + 1)], bank[4 + br][:, 0:128 * (i + 1)], ACT.Copy)
            ins.then_inc(S("pt_ev"), 1)
            if i == 0:
                act.wait_ge(S("ptc_tr"), h + 1)
                act.activation(B.PTc[h % 2][:], bank[6][0:NCP, :], ACT.Copy).then_inc(S("ptc_ev"), 1)
            if s >= 4 and i == 1:
                act_store_head(act, B, h - 1)
    act_store_head(act, B, NH - 1)
    U = len(SUNITS)
    for s in range(U + 1):
        if s < U:
            x = s % 2
            act.wait_ge(S("sc_ready"), NU + s + 1)
            for q, col in [(0, 1), (1, 2), (2, 0)]:
                v = s_probs(B, s)[q]
                ins = act.activation(v, v, ACT.Exp, bias=B.nm[x][:, col:col + 1], accum_out=B.sm[x][:, col:col + 1])
            ins.then_inc(S("exp_done"), 1)
        if s >= 1:
            act.wait_ge(S("pt_tr"), NU + s)
            if s >= 3:
                act.wait_ge(S("pv_mm"), NU + s - 2)
            PT = B.PT[(s - 1) % 2]
            for br in range(2):
                act.activation(PT[:, br, 0:256], bank[4 + br][:, 0:256], ACT.Copy)
                ins = act.activation(PT[0:NS, br, 256:384], bank[4 + br][0:NS, 256:384], ACT.Copy)
            act.activation(PT[0:NCK, 0, 384:512], bank[4][0:NCK, 384:512], ACT.Copy).then_inc(S("pt_ev"), 1)


def act_store_head(act, B, h):
    S = B.sem
    g, r, gp, j = unit(h)
    act.wait_ge(S("pv_mm"), 4 * (h + 1))
    act.activation(B.fT[r, j, 0:SEQ], B.bank[7][r, :], ACT.Copy).then_inc(S("o_ev"), 1)


def dve_kv(dve, B):
    S, bank = B.sem, B.bank
    for n in range(5):
        dve.wait_ge(S("kt_tr"), n + 1)
        if n < 4:
            ins = dve.tensor_copy(B.kT[:, n // 2, n % 2, 0:SEQ], bank[n][:])
        else:
            dve.tensor_copy(B.kT[:, :, :, SEQ:T], bank[4][:, 0:128].rearrange("p (a b n) -> p a b n", a=2, b=2))
            ins = dve.tensor_copy(B.pbT[:], bank[4][:, 128:164])
        ins.then_inc(S("kt_ev"), 1)
    dve.drain()
    dve_norm(dve, B, None, "g_mix1", mod(B, 1, 0), mod(B, 1, 1))
    for z in range(2):
        for n in range(16):
            dve.wait_ge(S("kvt_tr"), 16 * z + n + 1)
            if z and n == 0:
                dve.wait_ge(S("hid_mm"), 1)
            g, lp = 2 * n // 8, 2 * n % 8
            dve.tensor_copy(B.kvT[:, g, lp:lp + 2, :], bank[n % 8][:, 0:320].rearrange("p (q c) -> p q c", q=2)).then_inc(S("kvt_ev"), 1)
        dve.wait_ge(S("pos_mm"), z + 1)
        dve.tensor_tensor(B.posb[:, 2 * z:2 * z + 2], bank[4][:, 0:2], B.pbT[:, 32 + 2 * z:34 + 2 * z], ALU.add).then_inc(S("posb_ready"), 1)
        dve.wait_ge(S("cmp_mm"), z + 1)
        if z == 0:
            ins = dve.tensor_copy(B.kcT[:].rearrange("p a c -> p (a c)"), bank[5][:, 0:302])
        else:
            dve.tensor_copy(B.vcs[:].rearrange("p g d -> p (g d)"), bank[5][0:NCK, 0:256])
            ins = dve.tensor_copy(B.vcp[:].rearrange("p g d -> p (g d)"), bank[6][0:NCP, 0:256])
        ins.then_inc(S("cmp_ev"), 1)
    dve.drain()
    dve.nop().then_inc(S("cmp_done"), 1)
    for n in range(16):
        dve.wait_ge(S("kts_tr"), n + 1)
        gp, bp = n % 8 // 4, n % 4
        dve.tensor_copy(B.kTs[:, n // 8, gp, 2 * bp:2 * bp + 2, :].rearrange("p b t -> p (b t)"), bank[n % 8][:]).then_inc(S("kts_ev"), 1)
    dve.memset(B.qs[:], 0.0)
    dve.drain()
    dve.wait_ge(S("q_ev"), 16)
    for gp in range(2):
        dve.tensor_copy(B.qs[:, gp, :, 0:16].rearrange("p b (h t) -> p b h t", h=HG),
                        B.qT[:, 4 * gp:4 * gp + 4, SEQ:T].rearrange("p h (b t) -> p b h t", b=DB))
    dve.wait_ge(S("gspread_mm"), 1)
    sel = table(B, "head_sel").unsqueeze(1).unsqueeze(3).to_broadcast([128, G, HG, 3])
    for bq in range(2):
        dve.tensor_tensor(B.gtmp[:, bq].rearrange("p (g h c) -> p g h c", g=G, h=HG),
                          bank[1][:, bq * 48:(bq + 1) * 48].rearrange("p (g h c) -> p g h c", g=G, h=HG), sel, ALU.mult)
    dve.drain()
    for bq in range(2):
        ins = dve.tensor_reduce(B.gs[:, bq], B.gtmp[:, bq].rearrange("p (g h c) -> p g c h", g=G, h=HG), AX.X, ALU.add)
    ins.then_inc(S("gs_ready"), 1)
    dve_attend(dve, B)


def dve_attend(dve, B):
    S, bank = B.sem, B.bank
    U = len(UNITS)
    a0 = TABLE["dist_p"][0]
    for s in range(U + 1):
        if s < U:
            h, i = UNITS[s]
            x, nk = s % 2, 128 * (i + 1)
            dve.wait_ge(S("sc_mm"), s + 1)
            if s >= 2:
                dve.wait_ge(S("pt_tr"), s - 1)
            for br in range(2):
                dve.scalar_tensor_tensor(out=B.sc[x][:, br, 0:nk], in0=B.tab[:, a0 + 384 - 128 * i:a0 + 512], scalar=-slope_of(h),
                                         in1=bank[2 * x + br][:, 0:nk], op0=ALU.mult, op1=ALU.add)
            dve.drain()
            dve.tensor_reduce(B.nm[x][:, 0:2], B.sc[x][:, :, 0:nk], AX.X, ALU.max, negate=True).then_inc(S("sc_ready"), 1)
            if i == 0:
                C = B.scc[h % 2]
                dve.wait_ge(S("scc_mm"), h + 1)
                if h >= 2:
                    dve.wait_ge(S("ptc_tr"), h - 1)
                dve.scalar_tensor_tensor(out=C[:], in0=table(B, "dist_c").rearrange("p (i n) -> p i n", i=4), scalar=-slope_of(h),
                                         in1=bank[6][:, 0:4 * NCP].rearrange("p (i n) -> p i n", i=4), op0=ALU.mult, op1=ALU.add)
                dve.drain()
                dve.tensor_reduce(B.nmc[:], C[:], AX.X, ALU.max)
                dve.drain()
                dve.tensor_tensor(C[:], C[:], B.nmc[:].unsqueeze(2).to_broadcast([128, 4, NCP]), ALU.subtract).then_inc(S("scc_ready"), 1)
        if s >= 1:
            h, i = UNITS[s - 1]
            x, nk = (s - 1) % 2, 128 * (i + 1)
            dve.wait_ge(S("exp_done"), s)
            dve.reciprocal(B.sm[x][:, 0:2], B.sm[x][:, 0:2])
            dve.drain()
            dve.tensor_tensor(B.sm[x][:, 0:2], B.sm[x][:, 0:2], B.gates[:, i, 3 * h + 1:3 * h + 3], ALU.mult)
            dve.drain()
            for br in range(2):
                v = B.sc[x][:, br, 0:nk]
                ins = dve.tensor_scalar(v, v, B.sm[x][:, br:br + 1], None, ALU.mult)
            ins.then_inc(S("p_ready"), 1)
            if i == 0:
                C = B.scc[h % 2]
                dve.wait_ge(S("expc_done"), h + 1)
                dve.tensor_reduce(B.smc[:], C[:], AX.X, ALU.add)
                dve.drain()
                dve.reciprocal(B.smc[:], B.smc[:])
                dve.drain()
                dve.tensor_tensor(B.smc[:], B.smc[:], table(B, "row_valid"), ALU.mult)
                dve.drain()
                dve.tensor_tensor(B.smc[:], B.smc[:], B.gates[:, 0:4, 3 * h], ALU.mult)
                dve.drain()
                dve.tensor_tensor(C[:], C[:], B.smc[:].unsqueeze(2).to_broadcast([128, 4, NCP]), ALU.mult).then_inc(S("pc_ready"), 1)
    U = len(SUNITS)
    ds = table(B, "dist_s").rearrange("p (q k) -> p q k", q=2)
    dcs = table(B, "dist_cs").rearrange("p (q k) -> p q k", q=2)
    dve.wait_ge(S("pt_tr"), len(UNITS))
    for s in range(U + 2):
        if s < U:
            bq, g = SUNITS[s]
            x = s % 2
            sl = table(B, "slope")[:, g:g + 1]
            P = s_probs(B, s)
            dve.wait_ge(S("sc_mm"), NU + s + 1)
            if s >= 2:
                dve.wait_ge(S("pt_tr"), NU + s - 1)
            for q, d, src in [(0, ds, bank[2 * x]), (1, ds, bank[2 * x + 1]), (2, dcs, bank[6])]:
                w = SK if q < 2 else NCK
                dve.scalar_tensor_tensor(out=P[q], in0=d[:, bq], scalar=sl, in1=src[:, 0:w], op0=ALU.mult, op1=ALU.add)
            dve.drain()
            for q, col in [(0, 1), (1, 2), (2, 0)]:
                ins = dve.tensor_reduce(B.nm[x][:, col:col + 1], P[q], AX.X, ALU.max, negate=True)
            ins.then_inc(S("sc_ready"), 1)
        if s >= 1 and s - 1 < U:
            bq, g = SUNITS[s - 1]
            x = (s - 1) % 2
            dve.wait_ge(S("exp_done"), NU + s)
            dve.reciprocal(B.sm[x][:], B.sm[x][:])
            dve.drain()
            dve.tensor_tensor(B.sm[x][:], B.sm[x][:], B.gs[:, bq, g, :], ALU.mult)
            dve.drain()
            for q, col in [(0, 1), (1, 2), (2, 0)]:
                v = s_probs(B, s - 1)[q]
                ins = dve.tensor_scalar(v, v, B.sm[x][:, col:col + 1], None, ALU.mult)
            ins.then_inc(S("p_ready"), 1)
        if s >= 2:
            bq, g = SUNITS[s - 2]
            r, gp = gslice(g)
            dve.wait_ge(S("pv_mm"), NU + s - 1)
            dst = B.fT[r, 4 * gp:4 * gp + 4, SEQ + 16 * bq:SEQ + 16 * bq + 16].rearrange("p h (b t) -> p b h t", b=4)
            src = bank[7][r, 0:128].rearrange("p (b c) -> p b c", b=4)[:, :, 0:16].rearrange("p b (h t) -> p b h t", h=HG)
            dve.tensor_copy(dst, src).then_inc(S("so_ev"), 1)


def sp_rest(nc, sp, B, io, out):
    S = B.sem
    sp.wait_ge(S("pair_done"), PAIRS)
    sp.wait_ge(S("state_stored"), 64 * PAIRS)
    sp.wait_ge(S("stored"), 32)
    w_o = io["rwkv_w_o"][0].rearrange("(k p) n -> p k n", p=128)
    sp_out_proj(sp, B, 0, lambda m: [(None, w_o[:, :, m * 128:(m + 1) * 128])])
    sp_moe(sp, B, io, 0)
    sp_kv(nc, sp, B, io, out)
    sp.wait_ge(S("so_ev"), len(SUNITS))
    sp.wait_ge(S("kv_stored"), 16 * 11)
    w_o1 = io["nsa_w_o"][0].rearrange("(gp g2 hg d) n -> g2 d gp hg n", gp=2, g2=2, hg=HG)

    def rows(m):
        for g2 in range(2):
            for gp in range(2):
                yield (slice(64 * g2, 64 * g2 + 64), slice(4 * gp, 4 * gp + 4)), w_o1[g2, :, gp, :, m * 128:(m + 1) * 128]

    sp_out_proj(sp, B, 1, rows)
    sp_moe(sp, B, io, 1)
    sp.wait_ge(S("y_ev_out"), 10)
    sp.dma_start(out["y_prompt"].rearrange("b (t p) d -> p (b t) d", p=128), B.ytok[:, 0:4, :]).then_inc(S("y_stored"), 16)
    sp.dma_start(out["y_sample"].rearrange("b s d -> (b s) d"), B.ytok[0:NS, 4, :]).then_inc(S("y_stored"), 16)
    sp.wait_ge(S("y_stored"), 32)


def pe_rest(nc, pe, B, io, out):
    S = B.sem
    pe.wait_ge(S("pair_done"), PAIRS)
    pe_out_proj(pe, B, 0, B.rkv[0], [16 * (m // 4 + 1) for m in range(KT)])
    pe_norm_sum(pe, B, 1)
    pe_moe(pe, B, 0)
    pe_norm_sum(pe, B, 2)
    pe_kv(pe, B)
    pe.wait_ge(S("so_ev"), len(SUNITS))
    pe.wait_ge(S("o_ev"), NH)
    pe_out_proj(pe, B, 1, B.fT, [0] * KT + [32 + 64 * (m // 4 + 1) for m in range(KT)])
    pe_norm_sum(pe, B, 3)
    pe_moe(pe, B, 1)
    pe_norm_sum(pe, B, 4)
    pe.wait_ge(S("norm_done"), 6)
    for n in range(10):
        t, h = n // 2, n % 2
        rows = TT[t][1]
        if n >= 8:
            pe.wait_ge(S("y_ev_out"), n - 7)
        for q in range(4):
            mm = pe.transpose(B.bank[n % 8][0:rows, q * 128:(q + 1) * 128], B.fT[:, 4 * h + q, cols(t)], B.ident[:])
        mm.then_inc(S("y_tr"), 1)


def act_rest(nc, act, B, io, out):
    S = B.sem
    act_norm(act, B, 1)
    act_moe(act, B, 0)
    act_norm(act, B, 2)
    act_kv(act, B)
    act_norm(act, B, 3)
    act_moe(act, B, 1)
    act_norm(act, B, 4)
    for n in range(10):
        act.wait_ge(S("y_tr"), n + 1)
        rows = TT[n // 2][1]
        act.activation(B.ytok[0:rows, n // 2, n % 2 * 512:n % 2 * 512 + 512], B.bank[n % 8][0:rows, :], ACT.Copy).then_inc(S("y_ev_out"), 1)


def dve_rest(nc, dve, B, io, out):
    S = B.sem
    dve.drain()
    dve_out_proj(dve, B, 0, mod(B, 0, 2))
    dve.drain()
    dve.nop().then_inc(S("x_ready"), 1)
    dve_norm(dve, B, 1, "g_ffn0", mod(B, 0, 3), mod(B, 0, 4))
    dve_moe(dve, B, 0)
    dve_norm(dve, B, 2, "g_kv", mod(B, 2, 0), mod(B, 2, 1))
    dve_kv(dve, B)
    dve.drain()
    dve_out_proj(dve, B, 1, mod(B, 1, 2))
    dve.drain()
    dve.nop().then_inc(S("x_ready"), 1)
    dve_norm(dve, B, 3, "g_ffn1", mod(B, 1, 3), mod(B, 1, 4))
    dve_moe(dve, B, 1)
    dve_norm(dve, B, 4, "g_f", None, None)


_OUTS = [("y_prompt", (1, SEQ, D)), ("y_sample", (DB, DS, D)), ("kv_prompt", (1, SEQ, 4, G, HD)), ("kv_sample", (DB, DS, 4, G, HD)),
         ("win_prompt", (1, SEQ, 2, G, HD)), ("win_sample", (DB, PAST + DS, 2, G, HD)), ("wkv_prompt", (1, 1, NH, HD, HD)),
         ("wkv_sample", (1, DB, NH, HD, HD)), ("shift_prompt", (1, 1, D)), ("shift_sample", (1, DB, D))]
_UNUSED = ("rwkv_v0", "rwkv_v1", "rwkv_v2")


def kernel(**inputs):
    import numpy as _np
    import concourse.bacc as _bacc
    from concourse import mybir as _mybir
    from concourse.bass_utils import run_bass_kernel_spmd as _run

    nc = _bacc.Bacc("TRN2", target_bir_lowering=False, num_devices=1)
    arrays, io, out = {}, {}, {}
    for name, value in inputs.items():
        if name in _UNUSED:
            continue
        a = _np.ascontiguousarray(value)
        arrays[f"in_{name}_dram"] = a
        io[name] = nc.dram_tensor(f"in_{name}_dram", a.shape, _mybir.dt.from_np(a.dtype), kind="ExternalInput").ap()
    arrays["in_table_dram"] = shape_table()
    io["table"] = nc.dram_tensor("in_table_dram", (128, TABLE_W), _mybir.dt.float32, kind="ExternalInput").ap()
    for name, shape in _OUTS:
        out[name] = nc.dram_tensor(f"out_{name}_dram", shape, _mybir.dt.float32, kind="ExternalOutput").ap()
    program(nc, io, out)
    r = _run(nc, [arrays], core_ids=[0])
    return tuple(r.results[0][f"out_{name}_dram"] for name, _ in _OUTS)
```

```python
import concourse.bass as bass
from concourse import mybir
from contextlib import ExitStack

F32 = mybir.dt.float32
I32 = mybir.dt.int32
ALU = mybir.AluOpType
ACT = mybir.ActivationFunctionType
AX = mybir.AxisListType

D = 1024
KT = D // 128
SEQ = 512
DB, DS = 8, 4
NS = DB * DS
T = SEQ + NS
HALF = T // 2
NC = 1 + DB
PAIRS = 8
CH = 128
NCH = SEQ // CH
G, HD, NH, HG = 4, 64, 16, 4
PAST, PAGE, NPOOL = 256, 128, 20
E_N, FF = 16, 512
WP = 3
NEG = -1.0e30
RMS_EPS, LNX_EPS = 1e-6, 64e-5

VEC = ["g_mix0", "g_mix1", "g_ffn0", "g_ffn1", "g_f", "g_kv", "mix0", "mix1", "mix2", "mix3", "mix4", "mix5",
       "w0", "a0", "k_k", "k_a", "r_k", "lnx_w", "lnx_b"]
VROW = {n: i for i, n in enumerate(VEC)}


class Bufs:
    pass


def allocate(nc, ctx, io):
    B = Bufs()

    def sb(stack, name, shape, dt=F32):
        return stack.enter_context(nc.sbuf_tensor(name, shape, dt))

    B.ident = sb(ctx, "ident", [128, 128])
    B.ones = sb(ctx, "ones", [128, 128])
    B.upper = sb(ctx, "upper", [128, 128])
    B.zeros = sb(ctx, "zeros", [128, 256])
    B.idx = sb(ctx, "idx", [128, 16])
    B.pairs = [sb(ctx, f"pairs{l}", [128, 1], I32) for l in range(2)]
    B.eps_rms = sb(ctx, "eps_rms", [128, 1])
    B.eps_lnx = sb(ctx, "eps_lnx", [128, 1])
    B.xT = sb(ctx, "xT", [128, KT, T])
    B.fT = sb(ctx, "fT", [128, KT, T])
    B.vT = sb(ctx, "vT", [128, 5, 128])
    B.modT = sb(ctx, "modT", [128, 112, NC])
    B.coef = sb(ctx, "coef", [128, KT, NC])
    B.rstd = sb(ctx, "rstd", [128, T])
    B.tmp_s = sb(ctx, "tmp_s", [128, 2, NS])

    rw = ExitStack()
    B.blk_ones = sb(rw, "blk_ones", [128, 128])
    B.blk_mean = sb(rw, "blk_mean", [128, 128])
    B.low = sb(rw, "low", [128, 128])
    B.up2 = sb(rw, "up2", [128, 2, 128])
    B.bm = {m: sb(rw, f"bm{m}", [128, 128]) for m in (16, 32, 64)}
    B.offu = {m: sb(rw, f"offu{m}", [128, 128]) for m in (16, 32, 64)}
    B.s_low = sb(rw, "s_low", [NS, NS])
    B.s_up2 = sb(rw, "s_up2", [NS, 2, NS])
    B.s_bm = sb(rw, "s_bm", [NS, NS])
    B.seg_start = sb(rw, "seg_start", [128, T])
    B.seg_sel = sb(rw, "seg_sel", [128, DB, NS])
    B.row_sel = sb(rw, "row_sel", [NS, DB])
    B.rkv = [sb(rw, f"rkv{i}", [128, KT, T]) for i in range(3)]
    B.hwa = sb(rw, "hwa", [128, T])
    B.hw, B.ha = B.hwa[0:64], B.hwa[64:128]
    B.hg = sb(rw, "hg", [128, T])
    B.hg2 = sb(rw, "hg2", [32, T])
    B.wa2 = sb(rw, "wa2", [128, D])
    B.w2, B.a2 = B.wa2[0:64], B.wa2[64:128]
    B.g2 = sb(rw, "g2", [128, D])
    B.g2b = sb(rw, "g2b", [32, D])

    st = ExitStack()
    B.xt = sb(st, "xt", [128, 5, D])
    B.vs = sb(st, "vs", [128, 5, 128])
    B.cact = sb(st, "cact", [128, NC, KT])
    B.adaw = [sb(st, f"adaw{i}", [128, KT, 512]) for i in range(3)]
    B.adas = [sb(st, f"adas{i}", [NC, 512]) for i in range(2)]
    st.close()
    st = ExitStack()
    B.xx = sb(st, "xx", [128, KT, T])
    B.xm = [sb(st, f"xm{i}", [128, KT, T]) for i in range(2)]
    B.wp = [sb(st, f"wp{i}", [128, KT, 128]) for i in range(WP)]
    B.w1 = sb(st, "w1", [128, KT, 64])
    B.a1 = sb(st, "a1", [128, KT, 64])
    B.g1 = sb(st, "g1", [128, KT, 160])
    B.lasth = sb(st, "lasth", [128, NC, KT])
    B.lasto = sb(st, "lasto", [NC * KT, 128])
    st.close()
    st = ExitStack()
    names = ("lw", "cum", "a", "g", "kk", "km", "t1", "t2", "e1", "e2", "bh", "kh", "bonus")
    B.p = {n: B.fT[:, i] if i < KT else sb(st, f"p_{n}", [128, T])[:] for i, n in enumerate(names)}
    B.ar = sb(st, "p_ar", [128, NCH, 2, CH])
    B.ars = sb(st, "p_ars", [128, 2, NS])
    B.mid = sb(st, "p_mid", [128, NCH])
    B.fac = sb(st, "p_fac", [128, NCH])
    B.facs = sb(st, "p_facs", [128, DB])
    B.axs = sb(st, "p_axs", [128, DB, NS])
    B.rxs = sb(st, "p_rxs", [128, DB, NS])
    B.tok = [sb(st, f"p_tok{i}", [128, NCH, CH]) for i in range(3)]
    B.toks = [sb(st, f"p_toks{i}", [NS, 128]) for i in range(3)]
    B.Lm = [sb(st, f"Lm{h}", [128, NCH, CH]) for h in range(2)]
    B.UR = [sb(st, f"UR{h}", [128, NCH, 2, CH]) for h in range(2)]
    B.KR = [sb(st, f"KR{h}", [128, NCH, 2, CH]) for h in range(2)]
    B.Lp = [sb(st, f"Lp{h}", [128, NCH, CH]) for h in range(2)]
    B.Up = [sb(st, f"Up{h}", [128, NCH, CH]) for h in range(2)]
    B.Ti = [sb(st, f"Ti{h}", [128, NCH, CH]) for h in range(2)]
    B.Tt = [sb(st, f"Tt{h}", [128, NCH, CH]) for h in range(2)]
    B.sL = [sb(st, f"sL{h}", [NS, NS]) for h in range(2)]
    B.sUR = [sb(st, f"sUR{h}", [NS, 2, NS]) for h in range(2)]
    B.sKR = [sb(st, f"sKR{h}", [NS, 2, NS]) for h in range(2)]
    B.sL2 = [sb(st, f"sL2{h}", [NS, NS]) for h in range(2)]
    B.sTt = [sb(st, f"sTt{h}", [NS, NS]) for h in range(2)]
    B.X = [sb(st, f"X{h}", [128, HD]) for h in range(2)]
    B.SA = [sb(st, f"SA{h}", [128, HD]) for h in range(2)]
    B.ST = sb(st, "ST", [128, HD])
    B.STs = sb(st, "STs", [128, DB, HD])
    B.stin = sb(st, "stin", [HD, DB, 2, HD])
    B.stout = sb(st, "stout", [HD, NC, 128])
    B.sax = [sb(st, f"sax{h}", [NS, DB, HD]) for h in range(2)]
    B.vx = sb(st, "vx", [NS, 2, DB, HD])
    st.close()
    rw.close()
    allocate_moe(nc, B, sb)
    allocate_nsa(nc, B, sb)
    B.bank = [ctx.enter_context(nc.psum_tensor(f"bank{i}", [128, 512], F32)) for i in range(8)]
    sems = {}

    def sem(name):
        if name not in sems:
            sems[name] = ctx.enter_context(nc.semaphore(name))
        return sems[name]

    B.sem = sem
    return B


def half(h):
    return slice(h * HALF, (h + 1) * HALF)


def vec(B, name):
    v = VROW[name]
    return B.vT[:, 2 + v // 16, (v % 16) * KT:(v % 16 + 1) * KT]


def mod(B, layer, which):
    at = layer * 48 + which * KT
    return B.modT[:, at:at + KT, :]


def program(nc, io, out):
    ctx = ExitStack()
    with ctx:
        B = allocate(nc, ctx, io)
        S = B.sem
        block = ctx.enter_context(nc.Block())
        ident, bank = B.ident, B.bank

        @block.gpsimd
        def _(pool):
            chain = [0]

            def link(ins):
                chain[0] += 1
                ins.then_inc(S("pool_chain"), 1)
                pool.wait_ge(S("pool_chain"), chain[0])

            def keep(tile, pattern, base, mult, op=ALU.is_ge, fill=0.0):
                link(pool.affine_select(out=tile, in_=tile, compare_op=op, fill=fill, base=base,
                                        pattern=pattern, channel_multiplier=mult))

            link(pool.memset(ident[:], 0.0))
            keep(ident[:], [[-1, 128]], 0, 1, ALU.not_equal, 1.0)
            pool.memset(B.ones[:], 1.0).then_inc(S("pool_ident"), 1)
            link(pool.memset(B.low[:], 1.0))
            keep(B.low[:], [[-1, 128]], -1, 1)
            link(pool.memset(B.up2[:], 1.0))
            keep(B.up2[:, 0, :], [[1, 128]], -1, -1)
            keep(B.up2[:, 1, :], [[1, 128]], 0, -1)
            link(pool.memset(B.upper[:], 1.0))
            keep(B.upper[:], [[1, 128]], -1, -1)
            for e in range(16):
                pool.memset(B.idx[:, e:e + 1], float(e))
            link(pool.memset(B.zeros[:], 0.0))
            for tile, m, n in [(B.bm[16], 16, 128), (B.bm[32], 32, 128), (B.bm[64], 64, 128), (B.s_bm, 4, NS)]:
                link(pool.memset(tile[:], 1.0))
                v = tile[:].rearrange("p (b c) -> p b c", c=m)
                keep(v, [[-m, n // m], [0, m]], 0, 1)
                keep(v, [[m, n // m], [0, m]], m - 1, -1)
            link(pool.memset(B.seg_sel[:], 1.0))
            keep(B.seg_sel[:], [[-DS, DB], [1, NS]], 0, 0)
            keep(B.seg_sel[:], [[DS, DB], [-1, NS]], DS - 1, 0)
            link(pool.memset(B.row_sel[:], 1.0))
            keep(B.row_sel[:], [[-DS, DB]], 0, 1)
            keep(B.row_sel[:], [[DS, DB]], DS - 1, -1)
            link(pool.memset(B.seg_start[:], 1.0))
            link(pool.memset(B.seg_start[:, 0:SEQ:CH], 0.0))
            link(pool.memset(B.seg_start[:, SEQ:T:DS], 0.0))
            pool.memset(B.eps_rms[:], RMS_EPS)
            pool.memset(B.eps_lnx[:], LNX_EPS).then_inc(S("pool_masks"), 1)
            pool_zero_slots(pool, B)
            regs = []
            pool_moe(pool, B, 0, regs)
            pool_moe(pool, B, 1, regs)

        @block.sync
        def _(sp):
            def row(g, r, n, src):
                sp.dma_start(B.vs[r:r + n, g, :], src).then_inc(S("vec_loaded"), 16)

            row(0, 0, 8, io["c_prompt"].rearrange("b (k p) -> (b k) p", p=128))
            row(0, 8, 64, io["c_sample"].rearrange("b (k p) -> (b k) p", p=128))
            row(1, 0, 64, io["state_shift"].rearrange("a b (k p) -> (a b k) p", p=128))
            row(2, 0, 16, io["norm_mix_g"].rearrange("l (k p) -> (l k) p", p=128))
            row(2, 16, 16, io["norm_ffn_g"].rearrange("l (k p) -> (l k) p", p=128))
            row(2, 32, 8, io["norm_f_g"].rearrange("(k p) -> k p", p=128))
            row(2, 40, 8, io["kv_norm_g"].rearrange("(k p) -> k p", p=128))
            row(2, 48, 48, io["rwkv_mix"].rearrange("l s (k p) -> (l s k) p", p=128))
            for n, name in enumerate(["rwkv_w0", "rwkv_a0", "rwkv_k_k", "rwkv_k_a"]):
                row(2, 96 + 8 * n, 8, io[name].rearrange("l (k p) -> (l k) p", p=128))
            row(3, 0, 8, io["rwkv_r_k"].rearrange("l (k h) n -> (l k) (h n)", h=2))
            row(3, 8, 8, io["rwkv_lnx_w"].rearrange("l (k p) -> (l k) p", p=128))
            row(3, 16, 8, io["rwkv_lnx_b"].rearrange("l (k p) -> (l k) p", p=128))
            row(4, 0, 96, io["ada_b"].rearrange("l (k p) -> (l k) p", p=128))
            row(4, 96, 16, io["kv_ada_b"].rearrange("(k p) -> k p", p=128))
            sp.dma_start(B.xt[:, 0:4, :], io["x_prompt"].rearrange("b (t p) d -> p (b t) d", p=128)).then_inc(S("x_loaded"), 16)
            sp.dma_start(B.xt[0:NS, 4, :], io["x_sample"].rearrange("b s d -> (b s) d")).then_inc(S("x_loaded"), 16)
            for j in range(28):
                if j >= 3:
                    sp.wait_ge(S("ada_mm"), j - 2)
                src = io["ada_w"][j // 12, :, (j % 12) * 512:(j % 12 + 1) * 512] if j < 24 else \
                    io["kv_ada_w"][:, (j - 24) * 512:(j - 23) * 512]
                sp.dma_start(B.adaw[j % 3][:], src.rearrange("(k p) n -> p k n", p=128)).then_inc(S(f"w_loaded{j % 3}"), 16)
            sp.dma_start(B.w2, io["rwkv_w2"][0]).then_inc(S("lora2_loaded"), 16)
            sp.dma_start(B.a2, io["rwkv_a2"][0]).then_inc(S("lora2_loaded"), 16)
            sp.dma_start(B.g2[:], io["rwkv_g2"][0, 0:128]).then_inc(S("lora2_loaded"), 16)
            sp.dma_start(B.g2b[:], io["rwkv_g2"][0, 128:160]).then_inc(S("lora2_loaded"), 16)
            sp.wait_ge(S("ada_tr"), 28)
            sp.wait_ge(S("in_ev"), 11)
            for tile, name in [(B.w1, "rwkv_w1"), (B.a1, "rwkv_a1"), (B.g1, "rwkv_g1")]:
                sp.dma_start(tile[:], io[name][0].rearrange("(k p) n -> p k n", p=128)).then_inc(S("lora1_loaded"), 16)
            for g in range(24):
                if g >= WP:
                    sp.wait_ge(S("rkv_mm"), 2 * (g - WP + 1))
                s, m = g // KT, g % KT
                sp.dma_start(B.wp[g % WP][:], io["rwkv_w_rkv"][0, s, :, m * 128:(m + 1) * 128].rearrange("(k p) n -> p k n", p=128))\
                  .then_inc(S(f"w_loaded{g % WP}"), 16)
            sp.wait_ge(S("last_ev"), 1)
            sp.dma_start(out["shift_prompt"].rearrange("l b (k p) -> (l b k) p", p=128), B.lasto[0:8, :]).then_inc(S("stored"), 16)
            sp.dma_start(out["shift_sample"].rearrange("l b (k p) -> (l b k) p", p=128), B.lasto[8:72, :]).then_inc(S("stored"), 16)
            stored = 2
            for p in range(PAIRS):
                if p == 0:
                    sp.wait_ge(S("rkv_mm"), 48 + 8)
                    sp.wait_ge(S("xm_ready"), 6)
                    sp.wait_ge(S("stored"), 32)
                    sp.wait_ge(S("last_ev"), 1)
                if p >= 1:
                    sp.wait_ge(S("st_in"), p)
                for h in range(2):
                    sp.dma_start(B.stin[:, :, h, :], io["state_wkv"][0, :, 2 * p + h].rearrange("b i j -> i b j"))\
                      .then_inc(S("state_loaded"), 16)
                sp.wait_ge(S("st_out_ev"), p + 1)
                for h in range(2):
                    sp.dma_start(out["wkv_prompt"][0, 0, 2 * p + h], B.stout[:, 0, h * HD:(h + 1) * HD]).then_inc(S("state_stored"), 16)
                    sp.dma_start(out["wkv_sample"][0, :, 2 * p + h].rearrange("b i j -> i b j"),
                                 B.stout[:, 1:NC, h * HD:(h + 1) * HD]).then_inc(S("state_stored"), 16)
            sp_rest(nc, sp, B, io, out)

        @block.tensor
        def _(pe):
            pe.wait_ge(S("pool_ident"), 1)
            pe.wait_ge(S("vec_loaded"), 16 * 17)
            for g in range(4):
                rows = (72, 64, 128, 24)[g]
                mm = pe.transpose(bank[0][:, g * 128:g * 128 + rows], B.vs[0:rows, g, :], ident[0:rows, 0:rows])
            mm.then_inc(S("in_tr"), 1)
            pe.transpose(bank[1][:, 0:112], B.vs[0:112, 4, :], ident[0:112, 0:112]).then_inc(S("in_tr"), 1)
            pe.wait_ge(S("x_loaded"), 32)
            for g in range(2, 11):
                if g >= 8:
                    pe.wait_ge(S("in_ev"), g - 7)
                if g < 10:
                    t, h = (g - 2) // 2, (g - 2) % 2
                    for q in range(4):
                        k = 4 * h + q
                        mm = pe.transpose(bank[g % 8][:, q * 128:(q + 1) * 128], B.xt[:, t, k * 128:(k + 1) * 128], ident[:])
                else:
                    for k in range(KT):
                        mm = pe.transpose(bank[g % 8][:, k * NS:(k + 1) * NS], B.xt[0:NS, 4, k * 128:(k + 1) * 128],
                                          ident[0:NS, 0:NS])
                mm.then_inc(S("in_tr"), 1)
            pe.wait_ge(S("cact_ready"), 1)
            pe.wait_ge(S("in_ev"), 11)

            def ada_product(j):
                pe.wait_ge(S(f"w_loaded{j % 3}"), 16 * (j // 3 + 1))
                if j >= 2:
                    pe.wait_ge(S("ada_rows"), j - 1)
                for k in range(KT):
                    mm = pe.matmul(bank[j % 2][0:NC, :], B.cact[:, :, k], B.adaw[j % 3][:, k, :], start=k == 0, stop=k == KT - 1)
                mm.then_inc(S("ada_mm"), 1)

            def ada_turn(j):
                pe.wait_ge(S("ada_rows"), j + 1)
                if j >= 2:
                    pe.wait_ge(S("ada_ev"), j - 1)
                for q in range(4):
                    mm = pe.transpose(bank[2 + j % 2][:, q * NC:(q + 1) * NC], B.adas[j % 2][:, q * 128:(q + 1) * 128],
                                      ident[0:NC, 0:NC])
                mm.then_inc(S("ada_tr"), 1)

            for j in range(28):
                ada_product(j)
                if j >= 1:
                    ada_turn(j - 1)
            ada_turn(27)
            pe_norm_sum(pe, B, 0)
            for g in range(24):
                s = g // KT
                if g % KT == 0:
                    pe.wait_ge(S("xm_ready"), s + 1)
                pe.wait_ge(S(f"w_loaded{g % WP}"), 16 * ((10, 9, 9)[g % WP] + g // WP + 1))
                for h in range(2):
                    n = 2 * g + h
                    if n >= 8:
                        pe.wait_ge(S("rkv_ev"), n - 7)
                    for k in range(KT):
                        mm = pe.matmul(bank[n % 8][:, 0:HALF], B.wp[g % WP][:, k, :], B.xm[s % 2][:, k, half(h)],
                                       start=k == 0, stop=k == KT - 1)
                    mm.then_inc(S("rkv_mm"), 1)
            pe.wait_ge(S("lora1_loaded"), 48)
            n = 48
            for s, w, c0, c1 in [(3, B.w1, 0, 64), (4, B.a1, 0, 64), (5, B.g1, 0, 128), (5, B.g1, 128, 160)]:
                pe.wait_ge(S("xm_ready"), s + 1)
                r0 = 64 if s == 4 else 0
                for h in range(2):
                    pe.wait_ge(S("rkv_ev"), n - 7)
                    for k in range(KT):
                        mm = pe.matmul(bank[n % 8][r0:r0 + c1 - c0, 0:HALF], w[:, k, c0:c1], B.xm[s % 2][:, k, half(h)],
                                       start=k == 0, stop=k == KT - 1)
                    mm.then_inc(S("rkv_mm"), 1)
                    n += 1
            pe.wait_ge(S("lasth_ready"), 1)
            pe.wait_ge(S("rkv_ev"), 56)
            pe.transpose(bank[0][0:72, 0:128], B.lasth[:].rearrange("p n k -> p (n k)"), ident[:]).then_inc(S("last_tr"), 1)
            pe.wait_ge(S("last_ev"), 1)
            for p in range(PAIRS):
                pe_pair(pe, B, p)
            pe_rest(nc, pe, B, io, out)

        @block.scalar
        def _(act):
            act.wait_ge(S("in_ev"), 1)
            act.activation(B.cact[:].rearrange("p n k -> p (n k)"), B.vT[:, 0, 0:72], ACT.Silu).then_inc(S("cact_ready"), 1)
            for j in range(28):
                act.wait_ge(S("ada_mm"), j + 1)
                if j >= 2:
                    act.wait_ge(S("ada_tr"), j - 1)
                act.activation(B.adas[j % 2][:], bank[j % 2][0:NC, :], ACT.Copy).then_inc(S("ada_rows"), 1)
            act_norm(act, B, 0)
            act_scale(act, B, 0, mod(B, 0, 0))
            for n in range(56):
                act.wait_ge(S("rkv_mm"), n + 1)
                h = n % 2
                if n < 48:
                    s, m = n // 16, n % 16 // 2
                    ins = act.activation(B.rkv[s][:, m, half(h)], bank[n % 8][:, 0:HALF], ACT.Copy)
                else:
                    dst, fn = [(B.hw, ACT.Tanh), (B.ha, ACT.Copy), (B.hg, ACT.Sigmoid), (B.hg2, ACT.Sigmoid)][(n - 48) // 2]
                    r0 = 64 if (n - 48) // 2 == 1 else 0
                    ins = act.activation(dst[:, half(h)], bank[n % 8][r0:r0 + dst.shape[0], 0:HALF], fn)
                ins.then_inc(S("rkv_ev"), 1)
            act.drain()
            for p in range(PAIRS):
                act_pair(act, B, p)
            act_rest(nc, act, B, io, out)

        @block.vector
        def _(dve):
            for g in range(11):
                dve.wait_ge(S("in_tr"), g + 1)
                if g == 0:
                    for q in range(4):
                        rows = (72, 64, 128, 24)[q]
                        ins = dve.tensor_copy(B.vT[:, q, 0:rows], bank[0][:, q * 128:q * 128 + rows])
                elif g == 1:
                    ins = dve.tensor_copy(B.vT[:, 4, 0:112], bank[1][:, 0:112])
                elif g < 10:
                    t, h = (g - 2) // 2, (g - 2) % 2
                    ins = dve.tensor_copy(B.xT[:, 4 * h:4 * h + 4, t * 128:(t + 1) * 128],
                                          bank[g % 8][:].rearrange("p (k n) -> p k n", k=4))
                else:
                    ins = dve.tensor_copy(B.xT[:, :, SEQ:T], bank[g % 8][:, 0:KT * NS].rearrange("p (k n) -> p k n", k=KT))
                ins.then_inc(S("in_ev"), 1)
            dve.wait_ge(S("pool_masks"), 1)
            dve.tensor_scalar(B.blk_mean[:], B.bm[64][:], 1.0 / 64, None, ALU.mult)
            dve.tensor_copy(B.blk_ones[:], B.bm[64][:])
            dve.tensor_tensor(B.s_low[:], B.low[0:NS, 0:NS], B.s_bm[:], ALU.mult)
            for q in range(2):
                dve.tensor_tensor(B.s_up2[:, q, :], B.up2[0:NS, q, 0:NS], B.s_bm[:], ALU.mult)
            for m in (16, 32, 64):
                big = B.bm[2 * m] if m < 64 else B.ones
                dve.tensor_tensor(B.offu[m][:], big[:], B.bm[m][:], ALU.subtract)
            dve.drain()
            for m in (16, 32, 64):
                dve.tensor_tensor(B.offu[m][:], B.offu[m][:], B.up2[:, 0, :], ALU.mult)
            dve.drain()
            for j in range(28):
                dve.wait_ge(S("ada_tr"), j + 1)
                bias = B.vT[:, 4, 4 * j:4 * j + 4].unsqueeze(2).to_broadcast([128, 4, NC])
                dve.tensor_tensor(B.modT[:, 4 * j:4 * j + 4, :], bank[2 + j % 2][:, 0:4 * NC].rearrange("p (q n) -> p q n", q=4),
                                  bias, ALU.add).then_inc(S("ada_ev"), 1)
            dve.drain()
            dve_norm(dve, B, 0, 0, "g_mix0", mod(B, 0, 0), mod(B, 0, 1))
            dve.drain()
            h = B.fT
            dve.wait_ge(S("in_ev"), 11)
            dve.tensor_tensor(B.xx[:, :, 1:SEQ], h[:, :, 0:SEQ - 1], h[:, :, 1:SEQ], ALU.subtract)
            dve.tensor_scalar(B.xx[:, :, 0:1], h[:, :, 0:1], -1.0, None, ALU.mult)
            hs = h[:, :, SEQ:T].rearrange("p k (b s) -> p k b s", s=DS)
            xs = B.xx[:, :, SEQ:T].rearrange("p k (b s) -> p k b s", s=DS)
            dve.tensor_tensor(xs[:, :, :, 1:DS], hs[:, :, :, 0:DS - 1], hs[:, :, :, 1:DS], ALU.subtract)
            dve.tensor_tensor(xs[:, :, :, 0], B.vT[:, 1, 0:64].rearrange("p (b k) -> p k b", k=KT), hs[:, :, :, 0], ALU.subtract)
            dve.tensor_copy(B.lasth[:, 0, :], h[:, :, SEQ - 1])
            dve.tensor_copy(B.lasth[:, 1:NC, :].rearrange("p n k -> p k n"), hs[:, :, :, DS - 1]).then_inc(S("lasth_ready"), 1)
            dve.drain()
            for s in range(6):
                if s >= 2:
                    dve.wait_ge(S("rkv_mm"), {2: 16, 3: 32, 4: 48, 5: 50}[s])
                for k in range(KT):
                    ins = dve.scalar_tensor_tensor(out=B.xm[s % 2][:, k, :], in0=B.xx[:, k, :], scalar=vec(B, f"mix{s}")[:, k:k + 1],
                                                   in1=h[:, k, :], op0=ALU.mult, op1=ALU.add)
                ins.then_inc(S("xm_ready"), 1)
            dve.wait_ge(S("last_tr"), 1)
            dve.tensor_copy(B.lasto[:], bank[0][0:72, 0:128]).then_inc(S("last_ev"), 1)
            for p in range(PAIRS):
                dve_pair(dve, B, p)
            dve_rest(nc, dve, B, io, out)


ROOT_AT, SCALED_AT = (1, 3, 5, 8, 10), (2, 4, 6, 7, 9)


def act_norm(act, B, n):
    S = B.sem
    act.wait_ge(S("x_ready"), n) if n else act.wait_ge(S("in_ev"), 11)
    for k in range(KT):
        act.activation(B.fT[:, k], B.xT[:, k], ACT.Square).then_inc(S("norm_sq"), 1)
    act.wait_ge(S("norm_mm"), n + 1)
    for h in range(2):
        ins = act.activation(B.rstd[:, half(h)], B.bank[h][:, 0:HALF], ACT.Sqrt, bias=B.eps_rms[:, 0:1], scale=1.0 / D)
    ins.then_inc(S("norm_rt"), 1)


def act_scale(act, B, i, shift):
    S = B.sem
    for k in range(KT):
        act.wait_ge(S("norm_x"), KT * i + k + 1)
        x = B.fT[:, k, 0:SEQ]
        ins = act.activation(x, x, ACT.Identity, bias=shift[:, k, 0:1], scale=B.coef[:, k, 0:1])
    ins.then_inc(S("norm_rt"), 1)


def pe_norm_sum(pe, B, n):
    S = B.sem
    for k in range(KT):
        pe.wait_ge(S("norm_sq"), KT * n + k + 1)
        for h in range(2):
            mm = pe.matmul(B.bank[h][:, 0:HALF], B.ones[:], B.fT[:, k, half(h)], start=k == 0, stop=k == KT - 1)
    mm.then_inc(S("norm_mm"), 1)


def dve_norm(dve, B, n, i, gain, shift, scale):
    S = B.sem
    g = vec(B, gain)
    if scale is not None:
        dve.scalar_tensor_tensor(out=B.coef[:], in0=scale, scalar=1.0, in1=g.unsqueeze(2).to_broadcast([128, KT, NC]),
                                 op0=ALU.add, op1=ALU.mult)
    if n is not None:
        dve.wait_ge(S("norm_rt"), ROOT_AT[n])
        dve.reciprocal(B.rstd[:], B.rstd[:])
    dve.drain()
    if scale is None:
        for k in range(KT):
            ins = dve.scalar_tensor_tensor(out=B.fT[:, k], in0=B.xT[:, k], scalar=g[:, k:k + 1], in1=B.rstd[:], op0=ALU.mult, op1=ALU.mult)
        ins.then_inc(S("norm_done"), 1)
        return
    for k in range(KT):
        dve.tensor_tensor(B.fT[:, k], B.xT[:, k], B.rstd[:], ALU.mult).then_inc(S("norm_x"), 1)
    dve.drain()
    fs = B.fT[:, :, SEQ:T].rearrange("p k (b s) -> p k b s", s=DS)
    dve.tensor_tensor(fs, fs, B.coef[:, :, 1:NC].unsqueeze(3).to_broadcast([128, KT, DB, DS]), ALU.mult)
    dve.drain()
    dve.tensor_tensor(fs, fs, shift[:, :, 1:NC].unsqueeze(3).to_broadcast([128, KT, DB, DS]), ALU.add)
    dve.wait_ge(S("norm_rt"), SCALED_AT[i])
    dve.drain()
    dve.nop().then_inc(S("norm_done"), 1)


SQUARE, MERGES = (1, 2, 3), {5: 16, 7: 32, 9: 64}
STEPS = 14


def hs(h):
    return slice(h * HD, (h + 1) * HD)


def pe_pair(pe, B, p):
    S, bank, ident, P = B.sem, B.bank, B.ident, B.p
    pe.wait_ge(S("state_loaded"), 32 * (p + 1))
    if p >= 1:
        pe.wait_ge(S("var_rt"), p)
        pe.wait_ge(S("st_out_ev"), p)
    for b in range(DB):
        mm = pe.transpose(bank[6][:, b * HD:(b + 1) * HD], B.stin[:, b].rearrange("i h j -> i (h j)"), ident[0:HD, 0:HD])
    mm.then_inc(S("st_in_tr"), 1)
    pe.wait_ge(S("lora2_loaded"), 64)
    c = slice(p * 128, (p + 1) * 128)
    for i, (w, x) in enumerate([(B.w2, B.hw), (B.a2, B.ha)]):
        for h in range(2):
            mm = pe.matmul(bank[2 * i + h][:, 0:HALF], w[:, c], x[:, half(h)], start=True, stop=True)
        mm.then_inc(S("lora_mm"), 1)
    for h in range(2):
        pe.matmul(bank[4 + h][:, 0:HALF], B.g2[:, c], B.hg[:, half(h)], start=True, stop=False)
        mm = pe.matmul(bank[4 + h][:, 0:HALF], B.g2b[:, c], B.hg2[:, half(h)], start=False, stop=True)
    mm.then_inc(S("lora_mm"), 1)
    pe.wait_ge(S("st_in"), p + 1)
    pe.wait_ge(S("kksq_ready"), p + 1)
    for h in range(2):
        mm = pe.matmul(bank[6 + h][:, 0:HALF], B.blk_ones[:], P["t2"][:, half(h)], start=True, stop=True)
    mm.then_inc(S("head_sums"), 1)
    pe.wait_ge(S("rk_ready"), p + 1)
    for h in range(2):
        mm = pe.matmul(bank[h][:, 0:HALF], B.blk_ones[:], P["bonus"][:, half(h)], start=True, stop=True)
    mm.then_inc(S("head_sums"), 1)
    pe.wait_ge(S("grams_ready"), p + 1)
    pe.wait_ge(S("lora_ev"), 3 * (p + 1))
    src = [B.rkv[2][:, p, :], P["bh"], P["kh"]]
    for i in range(3):
        for q in range(NCH):
            mm = pe.transpose(bank[i][:, q * CH:(q + 1) * CH], src[i][:, q * CH:(q + 1) * CH], ident[:])
    for i in range(3):
        mm = pe.transpose(bank[3][0:NS, i * 128:(i + 1) * 128], src[i][:, SEQ:T], ident[:])
    mm.then_inc(S("tok_tr"), 1)
    pe.wait_ge(S("tok_ev"), p + 1)
    for s in range(STEPS):
        for h in range(2):
            pe_inverse(pe, B, p, s, h)
    for q in range(NCH + 1):
        pe_scan(pe, B, p, q)
    pe.wait_ge(S("y_ev"), p + 1)
    for h in range(2):
        mm = pe.matmul(bank[1 + 4 * h][:, 0:HALF], B.blk_mean[:], P["e1"][:, half(h)], start=True, stop=True)
    mm.then_inc(S("head_means"), 1)
    pe.wait_ge(S("seq_st0"), (NCH + 1) * (p + 1))
    pe.wait_ge(S("seq_st1"), (NCH + 1) * (p + 1))
    pe.transpose(bank[3][0:HD, 0:128], B.ST[:], ident[:])
    for b in range(DB):
        mm = pe.transpose(bank[7 if b < 4 else 2][0:HD, b % 4 * 128:b % 4 * 128 + 128], B.STs[:, b, :], ident[:])
    mm.then_inc(S("st_out_tr"), 1)
    pe.wait_ge(S("ysq_ready"), p + 1)
    for h in range(2):
        mm = pe.matmul(bank[1 + 4 * h][:, 0:HALF], B.blk_mean[:], P["t2"][:, half(h)], start=True, stop=True)
    mm.then_inc(S("head_means"), 1)


def products(p, s):
    return (STEPS + 3) * p + s + 1 + sum(m <= s for m in MERGES)


def pe_inverse(pe, B, p, s, h):
    S, bk = B.sem, B.bank[4 * h:4 * h + 4]
    r = hs(h)
    if s:
        pe.wait_ge(S(f"inv_dve{h}"), STEPS * p + s)
        if 2 <= s <= 4:
            pe.wait_ge(S(f"inv_act{h}"), 6 * p + s - 1)

    def four(b, lhsT, rhs):
        for c in range(NCH):
            mm = pe.matmul(bk[b][:, c * CH:(c + 1) * CH], lhsT(c), rhs(c), start=True, stop=True)
        return mm

    L, Lp, Up, Ti, Tt = [(lambda t: (lambda c: t[:, c, :]))(t) for t in (B.Lm[h], B.Lp[h], B.Up[h], B.Ti[h], B.Tt[h])]
    bh = lambda c: B.p["bh"][r, c * CH:(c + 1) * CH]
    kh = lambda c: B.p["kh"][r, c * CH:(c + 1) * CH]
    both = lambda c: B.ar[r, c].rearrange("p q t -> p (q t)")
    if s == 0:
        four(0, lambda c: B.ar[r, c, 0, :], bh)
        for c in range(NCH):
            pe.matmul(bk[1 + c // 2][:, c % 2 * 256:c % 2 * 256 + 256], bh(c), both(c), start=True, stop=True)
        for c in range(2):
            mm = pe.matmul(bk[3][:, c * 256:c * 256 + 256], kh(c), both(c), start=True, stop=True)
    if s == 1:
        for c in range(2, 4):
            mm = pe.matmul(bk[0][:, c % 2 * 256:c % 2 * 256 + 256], kh(c), both(c), start=True, stop=True)
    if s in SQUARE:
        mm = four(1, Up, Lp)
        if s < 3:
            mm = four(2, Lp, Up)
    if s in (2, 3, 4):
        mm = four(0, Lp, Tt)
    if s in (5, 7, 9):
        for c in range(NCH):
            mm = pe.transpose(bk[1][:, c * CH:(c + 1) * CH], Tt(c), B.ident[:])
        mm.then_inc(S(f"inv_mm{h}"), 1)
        mm = four(2, L, Tt)
    if s in (6, 8, 10):
        pe.wait_ge(S(f"inv_act{h}"), 6 * p + 4 + (s - 6) // 2)
        mm = four(0, Ti, Up)
    if s == 11:
        bs, ks, a = B.p["bh"][r, SEQ:T], B.p["kh"][r, SEQ:T], B.ars[r].rearrange("p q t -> p (q t)")
        pe.matmul(bk[1][0:NS, 0:NS], B.ars[r, 0, :], bs, start=True, stop=True)
        pe.matmul(bk[1][0:NS, 32:96], bs, a, start=True, stop=True)
        mm = pe.matmul(bk[1][0:NS, 96:160], ks, a, start=True, stop=True)
    if s == 12:
        mm = pe.matmul(bk[1][0:NS, 0:NS], B.sUR[h][:, 0, :], B.sL[h][:], start=True, stop=True)
    if s == 13:
        mm = pe.matmul(bk[1][0:NS, 0:NS], B.sL2[h][:], B.sTt[h][:], start=True, stop=True)
    mm.then_inc(S(f"inv_mm{h}"), 1)


def dve_inverse(dve, B, p, s, h):
    S, bk = B.sem, B.bank[4 * h:4 * h + 4]
    dve.wait_ge(S(f"inv_mm{h}"), products(p, s))
    quad = lambda b: bk[b][:].rearrange("p (c t) -> p c t", c=NCH)
    pairs = lambda b: bk[b][:].rearrange("p (c q t) -> p c q t", c=2, q=2)
    m4 = lambda m: m[:].unsqueeze(1).to_broadcast([128, NCH, CH])
    up = B.up2[:].unsqueeze(1).to_broadcast([128, 2, 2, CH])
    Lm, UR, KR, Lp, Up, Tt = B.Lm[h], B.UR[h], B.KR[h], B.Lp[h], B.Up[h], B.Tt[h]
    if s == 0:
        dve.tensor_tensor(Lm[:], quad(0), m4(B.low), ALU.mult)
        dve.tensor_tensor(UR[:, 0:2], pairs(1), up, ALU.mult)
        dve.tensor_tensor(UR[:, 2:4], pairs(2), up, ALU.mult)
        dve.tensor_tensor(KR[:, 0:2], pairs(3), up, ALU.mult)
        dve.drain()
        dve.tensor_tensor(Lp[:], Lm[:], m4(B.bm[16]), ALU.mult)
        dve.tensor_tensor(Up[:], UR[:, :, 0, :], m4(B.bm[16]), ALU.mult)
        dve.drain()
        ins = dve.tensor_tensor(Tt[:], Up[:], m4(B.ident), ALU.add)
    if s == 1:
        ins = dve.tensor_tensor(KR[:, 2:4], pairs(0), up, ALU.mult)
    if s in (2, 3, 4, 6, 8, 10):
        ins = dve.tensor_tensor(Tt[:], quad(0), Tt[:], ALU.add)
    if s in (5, 7, 9):
        ins = dve.tensor_tensor(Up[:], quad(2), m4(B.offu[MERGES[s]]), ALU.mult)
    if s == 11:
        dve.tensor_tensor(B.sL[h][:], bk[1][0:NS, 0:NS], B.s_low[:], ALU.mult)
        dve.tensor_tensor(B.sUR[h][:], bk[1][0:NS, 32:96].rearrange("p (q t) -> p q t", q=2), B.s_up2[:], ALU.mult)
        dve.tensor_tensor(B.sKR[h][:], bk[1][0:NS, 96:160].rearrange("p (q t) -> p q t", q=2), B.s_up2[:], ALU.mult)
        dve.drain()
        ins = dve.tensor_tensor(B.sTt[h][:], B.sUR[h][:, 0, :], B.ident[0:NS, 0:NS], ALU.add)
    if s == 12:
        ins = dve.tensor_copy(B.sL2[h][:], bk[1][0:NS, 0:NS])
    if s == 13:
        ins = dve.tensor_tensor(B.sTt[h][:], bk[1][0:NS, 0:NS], B.sTt[h][:], ALU.add)
    ins.then_inc(S(f"inv_dve{h}"), 1)


def pe_scan(pe, B, p, q):
    S = B.sem
    n = (NCH + 1) * p + q
    prompt = q < NCH
    for h in range(2):
        bk, r = B.bank[4 * h:4 * h + 4], hs(h)
        if q == 0:
            pe.wait_ge(S(f"inv_dve{h}"), STEPS * (p + 1))
        if prompt:
            mm = pe.matmul(bk[1][:, 0:HD], B.KR[h][:, q, 0, :], B.tok[0][:, q, r], start=True, stop=q == 0)
        else:
            mm = pe.matmul(bk[1][0:NS, 0:HD], B.sKR[h][:, 0, :], B.toks[0][:, r], start=True, stop=False)
        if q:
            pe.wait_ge(S(f"seq_st{h}"), n)
        if q and prompt:
            mm = pe.matmul(bk[1][:, 0:HD], B.ar[r, q, 0, :], B.ST[r, :], start=False, stop=True)
        if not prompt:
            for b in range(DB):
                mm = pe.matmul(bk[1][0:NS, 0:HD], B.axs[r, b, :], B.STs[r, b, :], start=False, stop=b == DB - 1)
        mm.then_inc(S(f"x_mm{h}"), 1)
    for h in range(2):
        bk, r = B.bank[4 * h:4 * h + 4], hs(h)
        if prompt:
            pe.matmul(bk[3][r, 0:HD], B.tok[2][:, q, r], B.tok[0][:, q, r], start=True, stop=False)
            y = bk[0][r, q * CH:(q + 1) * CH]
            if q:
                pe.matmul(y, B.ST[r, :], B.ar[r, q, 1, :], start=True, stop=False)
            pe.matmul(y, B.tok[0][:, q, r], B.KR[h][:, q, 1, :], start=q == 0, stop=False)
        else:
            pe.matmul(bk[3][r, :], B.toks[2][:, r], B.vx[:, h].rearrange("p b i -> p (b i)"), start=True, stop=False)
    for h in range(2):
        bk = B.bank[4 * h:4 * h + 4]
        pe.wait_ge(S(f"x_ev{h}"), n + 1)
        if prompt:
            mm = pe.matmul(bk[2][:, 0:HD], B.Tt[h][:, q, :], B.X[h][:], start=True, stop=True)
        else:
            mm = pe.matmul(bk[2][0:NS, 0:HD], B.sTt[h][:], B.X[h][0:NS, :], start=True, stop=True)
        mm.then_inc(S(f"sa_mm{h}"), 1)
    for h in range(2):
        bk, r = B.bank[4 * h:4 * h + 4], hs(h)
        pe.wait_ge(S(f"sa_ev{h}"), n + 1)
        if prompt:
            pe.matmul(bk[3][r, 0:HD], B.tok[1][:, q, r], B.SA[h][:], start=False, stop=True).then_inc(S(f"y_mm{h}"), 1)
        else:
            y = bk[2][r, 0:NS]
            pe.matmul(y, B.SA[h][0:NS, :], B.sUR[h][:, 1, :], start=True, stop=False)
            pe.matmul(y, B.toks[0][:, r], B.sKR[h][:, 1, :], start=False, stop=False)
            for b in range(DB):
                pe.matmul(y, B.STs[r, b, :], B.rxs[r, b, :], start=False, stop=b == DB - 1)
            pe.wait_ge(S(f"sax{h}"), p + 1)
            pe.matmul(bk[3][r, :], B.toks[1][:, r], B.sax[h][:].rearrange("p b i -> p (b i)"), start=False, stop=True)\
                .then_inc(S(f"y_mm{h}"), 2)
    if prompt:
        for h in range(2):
            bk, r = B.bank[4 * h:4 * h + 4], hs(h)
            pe.matmul(bk[0][r, q * CH:(q + 1) * CH], B.SA[h][:], B.UR[h][:, q, 1, :], start=False, stop=True).then_inc(S(f"y_mm{h}"), 1)


def dve_scan(dve, B, p, q):
    S = B.sem
    n = (NCH + 1) * p + q
    for h in range(2):
        r = hs(h)
        if q == NCH:
            dve.wait_ge(S(f"sa_ev{h}"), n + 1)
            dve.tensor_tensor(B.sax[h][:], B.SA[h][0:NS, :].unsqueeze(1).to_broadcast([NS, DB, HD]),
                              B.row_sel[:].unsqueeze(2).to_broadcast([NS, DB, HD]), ALU.mult).then_inc(S(f"sax{h}"), 1)
    for h in range(2):
        r, d = hs(h), B.bank[4 * h + 3]
        dve.wait_ge(S(f"y_mm{h}"), 2 * n + 1)
        if q == NCH:
            dve.tensor_tensor(B.STs[r], d[r, :].rearrange("p (b i) -> p b i", b=DB), B.STs[r], ALU.add)
        elif q:
            dve.tensor_tensor(B.ST[r, :], d[r, 0:HD], B.ST[r, :], ALU.add)
        else:
            ins = dve.tensor_scalar(B.ST[r, :], d[r, 0:HD], B.fac[r, 0:1], None, ALU.mult)
        if q:
            dve.drain()
        if q == NCH:
            ins = dve.tensor_tensor(B.STs[r], B.STs[r], B.facs[r, :].unsqueeze(2).to_broadcast([HD, DB, HD]), ALU.mult)
        elif q:
            ins = dve.tensor_scalar(B.ST[r, :], B.ST[r, :], B.fac[r, q:q + 1], None, ALU.mult)
        ins.then_inc(S(f"seq_st{h}"), 1)


def act_pair(act, B, p):
    S, bank, P = B.sem, B.bank, B.p
    act.wait_ge(S("st_in_tr"), p + 1)
    act.activation(B.STs[:].rearrange("p b i -> p (b i)"), bank[6][:], ACT.Copy).then_inc(S("st_in"), 1)
    for i, (dst, b) in enumerate([("lw", "w0"), ("a", "a0"), ("g", None)]):
        act.wait_ge(S("lora_mm"), 3 * p + i + 1)
        if dst == "g" and p >= 1:
            act.wait_ge(S("pair_done"), p)
        for h in range(2):
            if b:
                ins = act.activation(P[dst][:, half(h)], bank[2 * i + h][:, 0:HALF], ACT.Sigmoid, bias=vec(B, b)[:, p:p + 1])
            else:
                ins = act.activation(P[dst][:, half(h)], bank[2 * i + h][:, 0:HALF], ACT.Copy)
        ins.then_inc(S("lora_ev"), 1)
    act.wait_ge(S("cum_ready"), p + 1)
    act.activation(P["e1"][:], P["t1"][:], ACT.Exp)
    act.activation(P["e2"][:], P["cum"][:], ACT.Exp)
    act.activation(P["lw"][:], P["cum"][:], ACT.Exp, scale=-1.0)
    act.activation(B.fac[:], B.fac[:], ACT.Exp)
    act.activation(B.facs[:], P["cum"][:, SEQ + DS - 1:T:DS], ACT.Exp).then_inc(S("exps_ready"), 1)
    act.wait_ge(S("kkmax_ready"), p + 1)
    act.activation(P["t2"][:], P["t2"][:], ACT.Sqrt).then_inc(S("kk_rt"), 1)
    act.wait_ge(S("tok_tr"), p + 1)
    for i in range(3):
        act.activation(B.tok[i][:].rearrange("p c t -> p (c t)"), bank[i][:], ACT.Copy)
        ins = act.activation(B.toks[i][:], bank[3][0:NS, i * 128:(i + 1) * 128], ACT.Copy)
    ins.then_inc(S("tok_ev"), 1)
    for s in SQUARE:
        for h in range(2):
            act.wait_ge(S(f"inv_mm{h}"), products(p, s))
            ins = act.activation(B.Lp[h][:].rearrange("p c t -> p (c t)"), bank[4 * h + 1][:], ACT.Copy)
            if s < 3:
                ins = act.activation(B.Up[h][:].rearrange("p c t -> p (c t)"), bank[4 * h + 2][:], ACT.Copy)
            ins.then_inc(S(f"inv_act{h}"), 1)
    for m in range(3):
        for h in range(2):
            act.wait_ge(S(f"inv_mm{h}"), products(p, 5 + 2 * m) - 1)
            act.activation(B.Ti[h][:].rearrange("p c t -> p (c t)"), bank[4 * h + 1][:], ACT.Copy).then_inc(S(f"inv_act{h}"), 1)
    for q in range(NCH + 1):
        n = (NCH + 1) * p + q
        rows = 128 if q < NCH else NS
        for h in range(2):
            act.wait_ge(S(f"x_mm{h}"), n + 1)
            if q:
                act.wait_ge(S(f"sa_mm{h}"), n)
            act.activation(B.X[h][0:rows, :], bank[4 * h + 1][0:rows, 0:HD], ACT.Copy).then_inc(S(f"x_ev{h}"), 1)
        for h in range(2):
            act.wait_ge(S(f"sa_mm{h}"), n + 1)
            if q:
                act.wait_ge(S(f"y_mm{h}"), 2 * n)
            act.activation(B.SA[h][0:rows, :], bank[4 * h + 2][0:rows, 0:HD], ACT.Copy).then_inc(S(f"sa_ev{h}"), 1)
    for h in range(2):
        act.wait_ge(S(f"y_mm{h}"), 2 * (NCH + 1) * (p + 1))
        act.activation(P["e1"][hs(h), 0:SEQ], bank[4 * h][hs(h), :], ACT.Copy)
        ins = act.activation(P["e1"][hs(h), SEQ:T], bank[4 * h + 2][hs(h), 0:NS], ACT.Copy)
    ins.then_inc(S("y_ev"), 1)
    act.wait_ge(S("st_out_tr"), p + 1)
    if p >= 1:
        act.wait_ge(S("state_stored"), 64 * p)
    act.activation(B.stout[:, 0, :], bank[3][0:HD, 0:128], ACT.Copy)
    act.activation(B.stout[:, 1:5, :].rearrange("p b j -> p (b j)"), bank[7][0:HD, :], ACT.Copy)
    act.activation(B.stout[:, 5:9, :].rearrange("p b j -> p (b j)"), bank[2][0:HD, :], ACT.Copy).then_inc(S("st_out_ev"), 1)
    act.wait_ge(S("head_means"), 2 * p + 2)
    for h in range(2):
        ins = act.activation(P["t1"][:, half(h)], bank[1 + 4 * h][:, 0:HALF], ACT.Sqrt, bias=B.eps_lnx[:, 0:1])
    ins.then_inc(S("var_rt"), 1)


def dve_pair(dve, B, p):
    S, bank, P = B.sem, B.bank, B.p
    r, k, v = (B.rkv[i][:, p, :] for i in range(3))
    col = lambda name: vec(B, name)[:, p:p + 1]
    if p == 0:
        dve.wait_ge(S("rkv_ev"), 56)
    dve.tensor_scalar(P["kk"][:], k, col("k_k"), None, ALU.mult)
    dve.wait_ge(S("lora_ev"), 3 * p + 1)
    dve.tensor_scalar(P["lw"][:], P["lw"][:], -float(2.718281828459045 ** -0.5), None, ALU.mult)
    dve.drain()
    dve.tensor_tensor(P["t2"][:], P["kk"][:], P["kk"][:], ALU.mult).then_inc(S("kksq_ready"), 1)
    dve.tensor_tensor_scan(P["cum"][:], B.seg_start[:], P["lw"][:], 0.0, ALU.mult, ALU.add)
    dve.drain()
    dve.tensor_copy(B.mid[:], P["cum"][:, CH // 2 - 1:SEQ:CH])
    dve.drain()
    pc = P["cum"][:, 0:SEQ].rearrange("p (c t) -> p c t", c=NCH)
    dve.tensor_tensor(pc, pc, B.mid[:].unsqueeze(2).to_broadcast([128, NCH, CH]), ALU.subtract)
    dve.drain()
    dve.tensor_tensor(B.fac[:, 0:NCH - 1], P["cum"][:, CH - 1:SEQ - CH:CH], B.mid[:, 1:NCH], ALU.add)
    dve.tensor_copy(B.fac[:, NCH - 1:NCH], P["cum"][:, SEQ - 1:SEQ])
    dve.tensor_tensor(P["t1"][:], P["cum"][:], P["lw"][:], ALU.subtract).then_inc(S("cum_ready"), 1)
    dve.wait_ge(S("lora_ev"), 3 * p + 2)
    dve.tensor_scalar(P["km"][:], P["a"][:], -1.0, col("k_a"), ALU.add, ALU.mult)
    dve.drain()
    dve.scalar_tensor_tensor(out=P["km"][:], in0=P["km"][:], scalar=1.0, in1=k, op0=ALU.add, op1=ALU.mult)
    dve.drain()
    dve.scalar_tensor_tensor(out=P["bonus"][:], in0=r, scalar=col("r_k"), in1=P["km"][:], op0=ALU.mult, op1=ALU.mult)\
       .then_inc(S("rk_ready"), 1)
    dve.wait_ge(S("head_sums"), 2 * p + 1)
    for h in range(2):
        ins = dve.tensor_scalar(P["t2"][:, half(h)], bank[6 + h][:, 0:HALF], 1e-24, None, ALU.max)
    ins.then_inc(S("kkmax_ready"), 1)
    dve.wait_ge(S("head_sums"), 2 * p + 2)
    for h in range(2):
        dve.tensor_tensor(P["bonus"][:, half(h)], bank[h][:, 0:HALF], v[:, half(h)], ALU.mult)
    dve.wait_ge(S("exps_ready"), p + 1)
    dve.tensor_tensor(B.ar[:, :, 1, :], r[:, 0:SEQ].rearrange("p (c t) -> p c t", c=NCH),
                      P["e2"][:, 0:SEQ].rearrange("p (c t) -> p c t", c=NCH), ALU.mult)
    dve.tensor_tensor(B.ars[:, 1, :], r[:, SEQ:T], P["e2"][:, SEQ:T], ALU.mult)
    dve.tensor_tensor(P["kh"][:], P["km"][:], P["lw"][:], ALU.mult)
    dve.wait_ge(S("kk_rt"), p + 1)
    dve.reciprocal(P["t2"][:], P["t2"][:])
    dve.drain()
    dve.tensor_tensor(P["kk"][:], P["kk"][:], P["t2"][:], ALU.mult)
    dve.drain()
    dve.scalar_tensor_tensor(out=B.ar[:, :, 0, :], in0=P["kk"][:, 0:SEQ].rearrange("p (c t) -> p c t", c=NCH), scalar=-1.0,
                             in1=P["e1"][:, 0:SEQ].rearrange("p (c t) -> p c t", c=NCH), op0=ALU.mult, op1=ALU.mult)
    dve.scalar_tensor_tensor(out=B.ars[:, 0, :], in0=P["kk"][:, SEQ:T], scalar=-1.0, in1=P["e1"][:, SEQ:T],
                             op0=ALU.mult, op1=ALU.mult)
    dve.tensor_tensor(P["bh"][:], P["kk"][:], P["a"][:], ALU.mult)
    dve.drain()
    dve.tensor_tensor(B.axs[:], B.seg_sel[:], B.ars[:, 0, :].unsqueeze(1).to_broadcast([128, DB, NS]), ALU.mult)
    dve.tensor_tensor(B.rxs[:], B.seg_sel[:], B.ars[:, 1, :].unsqueeze(1).to_broadcast([128, DB, NS]), ALU.mult)
    dve.tensor_tensor(P["bh"][:], P["bh"][:], P["lw"][:], ALU.mult).then_inc(S("grams_ready"), 1)
    dve.wait_ge(S("tok_ev"), p + 1)
    for h in range(2):
        dve.tensor_tensor(B.vx[:, h], B.toks[0][:, hs(h)].unsqueeze(1).to_broadcast([NS, DB, HD]),
                          B.row_sel[:].unsqueeze(2).to_broadcast([NS, DB, HD]), ALU.mult)
    for s in range(STEPS):
        for h in range(2):
            dve_inverse(dve, B, p, s, h)
    for q in range(NCH + 1):
        dve_scan(dve, B, p, q)
    y = P["e1"]
    dve.wait_ge(S("head_means"), 2 * p + 1)
    for h in range(2):
        dve.tensor_tensor(y[:, half(h)], y[:, half(h)], bank[1 + 4 * h][:, 0:HALF], ALU.subtract)
    dve.drain()
    dve.tensor_tensor(P["t2"][:], y[:], y[:], ALU.mult).then_inc(S("ysq_ready"), 1)
    dve.wait_ge(S("var_rt"), p + 1)
    dve.reciprocal(P["t1"][:], P["t1"][:])
    dve.drain()
    dve.tensor_tensor(y[:], y[:], P["t1"][:], ALU.mult)
    dve.drain()
    dve.tensor_scalar(y[:], y[:], col("lnx_w"), col("lnx_b"), ALU.mult, ALU.add)
    dve.drain()
    dve.tensor_tensor(y[:], y[:], P["bonus"][:], ALU.add)
    dve.drain()
    dve.tensor_tensor(r, y[:], P["g"][:], ALU.mult).then_inc(S("pair_done"), 1)


TT = [(i, 128 if i < 4 else NS) for i in range(5)]
C = 96
OVER = (2 * T - 1) // C
SLOTS = E_N + OVER + (E_N + OVER) % 2
ZPARTS = -(-SLOTS * C // 128)


def cols(i):
    return slice(i * 128, min((i + 1) * 128, T))


def allocate_moe(nc, B, sb):
    B.x_slots = nc.dram_tensor("x_slots", [SLOTS * C, D], F32, kind="Internal").ap()
    B.y_slots = nc.dram_tensor("y_slots", [SLOTS * C, D], F32, kind="Internal").ap()
    st = ExitStack()
    B.wr = sb(st, "wr", [128, KT, 20])
    B.br = sb(st, "br", [128, 20])
    B.lg = sb(st, "lg", [128, 5, 20])
    B.rt = {n: sb(st, f"rt_{n}", [128, 5, w]) for n, w in
            dict(gmax=1, eg=4, sum=1, rem=1, gm=4, sel=16, ing=4, v1=1, v2=1, o1=4, o2=4, in2=4, ew=1, w1=1, w2=1, eqt=4,
                 m1=16, m2=16, m=16, before=16, place=16, t16=16, over=16, pos=2).items()}
    B.pos = sb(st, "pos", [128, 5, 2], I32)
    B.cnt = {n: sb(st, f"cnt_{n}", [128, 16]) for n in ("count", "extra", "a", "b", "t", "base")}
    B.row_ok = sb(st, "row_ok", [128, 1])
    B.cmp = sb(st, "cmp", [128, SLOTS, 16])
    B.slot_ef = sb(st, "slot_ef", [128, SLOTS])
    B.slot_e = sb(st, "slot_e", [128, SLOTS], I32)
    B.pairs_f = sb(st, "pairs_f", [128, 1])
    B.ga = [sb(st, f"ga{i}", [128, D]) for i in range(4)]
    B.xs = [sb(st, f"xs{i}", [C, D]) for i in range(2)]
    B.ys = [sb(st, f"ys{i}", [C, D]) for i in range(2)]
    B.xsT = sb(st, "xsT", [128, KT, C])
    B.act = sb(st, "act", [128, 4, C])
    B.wg = [sb(st, f"wg{i}", [128, KT, FF]) for i in range(2)]
    B.wu = [sb(st, f"wu{i}", [128, KT, FF]) for i in range(2)]
    B.wd = [sb(st, f"wd{i}", [128, 4, D]) for i in range(2)]
    B.wo = [sb(st, f"wo{i}", [128, KT, 128]) for i in range(4)]
    B.htok = B.ga + [B.ys[0]]
    st.close()


def before(regs, l):
    return 0 if l == 0 else regs[0] + 1


def sp_out_proj(sp, B, n, src):
    S = B.sem
    for m in range(KT):
        g = n * KT + m
        if g >= 4:
            sp.wait_ge(S("out_mm"), 2 * (g - 3))
        for part, rows in src(m):
            sp.dma_start(B.wo[g % 4][part] if part else B.wo[g % 4][:], rows).then_inc(S(f"wo_loaded{g % 4}"), 16)


def pe_out_proj(pe, B, n, x, dmas):
    S = B.sem
    for m in range(KT):
        g = n * KT + m
        pe.wait_ge(S(f"wo_loaded{g % 4}"), dmas[g])
        for h in range(2):
            q = 2 * g + h
            if q % 16 >= 8:
                pe.wait_ge(S("out_ev"), q - 7)
            for k in range(KT):
                mm = pe.matmul(B.bank[q % 8][:, 0:HALF], B.wo[g % 4][:, k, :], x[:, k, half(h)], start=k == 0, stop=k == KT - 1)
            mm.then_inc(S("out_mm"), 1)


def add_gated(dve, B, ps, h, gate, m):
    dst = B.xT[:, m, half(h)]
    w = HALF if h == 0 else HALF - NS
    if h:
        dve.tensor_tensor(B.tmp_s[:, m % 2].rearrange("p (b s) -> p b s", s=DS), ps[:, w:HALF].rearrange("p (b s) -> p b s", s=DS),
                          gate[:, m, 1:NC].unsqueeze(2).to_broadcast([128, DB, DS]), ALU.mult)
        dve.drain()
        dve.tensor_tensor(dst[:, w:HALF], dst[:, w:HALF], B.tmp_s[:, m % 2], ALU.add)
    return dve.scalar_tensor_tensor(out=dst[:, 0:w], in0=ps[:, 0:w], scalar=gate[:, m, 0:1], in1=dst[:, 0:w], op0=ALU.mult, op1=ALU.add)


def dve_out_proj(dve, B, n, gate):
    S = B.sem
    for q in range(16 * n, 16 * n + 16):
        dve.wait_ge(S("out_mm"), q + 1)
        add_gated(dve, B, B.bank[q % 8], q % 2, gate, q % 16 // 2).then_inc(S("out_ev"), 1)


def pool_zero_slots(pool, B):
    S = B.sem
    pool.wait_ge(S("last_ev"), 1)
    for rows in (B.x_slots, B.y_slots):
        for q in range(ZPARTS):
            n = min(128, SLOTS * C - q * 128)
            dst = rows[q * 128:q * 128 + n].rearrange("p (a c) -> p a c", c=256)
            pool.dma_start(dst, B.zeros[0:n].unsqueeze(1).to_broadcast([n, D // 256, 256])).then_inc(S("slots_zero"), 16)


def pool_moe(pool, B, l, regs):
    S = B.sem
    pool.wait_ge(S("slots_zero"), 32 * ZPARTS)
    pool.wait_ge(S("route_step"), 4 * l + 4)
    regs.append(pool.value_load(B.pairs[l][0:1, 0:1], min_val=E_N // 2 - 1, max_val=SLOTS // 2 - 1))
    for t, rows in TT:
        pool.wait_ge(S("h_ev"), 10 * l + 2 * t + 2)
        for j in range(2):
            pool.indirect_dma_start(out=B.x_slots, out_offset=bass.IndirectOffsetOnAxis(ap=B.pos[0:rows, t, j:j + 1], axis=0),
                                    in_=B.htok[t][0:rows, :], in_offset=None).then_inc(S("scattered"), 16)
    pool.wait_ge(S("ys_complete"), l + 1)
    pool.wait_ge(S("scattered"), 160 * (l + 1))
    for t, rows in TT:
        if t >= 2:
            pool.wait_ge(S("y_tr"), 10 * l + 2 * t - 2)
        for j in range(2):
            pool.indirect_dma_start(out=B.ga[2 * (t % 2) + j][0:rows, :], out_offset=None, in_=B.y_slots,
                                    in_offset=bass.IndirectOffsetOnAxis(ap=B.pos[0:rows, t, j:j + 1], axis=0))\
                .then_inc(S(f"gathered{t % 2}"), 16)


def sp_moe(sp, B, io, l, regs):
    S = B.sem
    if l == 0:
        sp.wait_ge(S("out_mm"), 16)
    for src, n, w in [("moe_w_grp", 0, 4), ("moe_w_exp", 4, 16)]:
        sp.dma_start(B.wr[:, :, n:n + w], io[src][l].rearrange("(k p) n -> p k n", p=128)).then_inc(S("router_loaded"), 16)
    for src, n, w in [("moe_b_grp", 0, 4), ("moe_b_exp", 4, 16)]:
        sp.dma_start(B.br[:, n:n + w], io[src][l].rearrange("(a n) -> a n", a=1).to_broadcast([128, w])).then_inc(S("router_loaded"), 16)

    def load_gate_up(i, e):
        pick = lambda name: io[name][l, bass.ds(e, 1)].rearrange("e (k p) n -> p (e k) n", p=128)
        sp.dma_start(B.wg[i][:], pick("moe_w_gate")).then_inc(S(f"wgu_loaded{i}"), 16)
        sp.dma_start(B.wu[i][:], pick("moe_w_up")).then_inc(S(f"wgu_loaded{i}"), 16)

    def load_down(i, e):
        sp.dma_start(B.wd[i][:], io["moe_w_down"][l, bass.ds(e, 1)].rearrange("e (k p) n -> p (e k) n", p=128))\
            .then_inc(S(f"wd_loaded{i}"), 16)

    def load_tokens(i, slot):
        sp.dma_start(B.xs[i][:], B.x_slots.rearrange("(s c) n -> c s n", c=C)[:, bass.ds(slot, 1), :]
                     .rearrange("c s n -> c (s n)")).then_inc(S(f"xs_loaded{i}"), 16)

    for i in range(2):
        load_gate_up(i, i)
        load_down(i, i)
    sp.wait_ge(S("route_step"), 4 * l + 4)
    regs.append(sp.value_load(B.pairs[l][0:1, 0:1], min_val=E_N // 2 - 1, max_val=SLOTS // 2 - 1))
    sp.wait_ge(S("scattered"), 160 * (l + 1))
    for i in range(2):
        load_tokens(i, i)
    with sp.Fori(1, regs[l] + 1) as t:
        for i in range(2):
            slot = 2 * t + i
            last = (t - 1 + before(regs, l)) * 2 + i
            e = sp.value_load(B.slot_e[0:1, bass.ds(slot, 1)], min_val=0, max_val=E_N - 1)
            sp.wait_ge(S("x_tr"), last * 2 + 2)
            load_tokens(i, slot)
            sp.wait_ge(S("up_mm"), last * 4 + 4)
            load_gate_up(i, e)
            sp.wait_ge(S("down_mm"), last * 2 + 2)
            load_down(i, e)
    for i in range(2):
        sp.wait_ge(S(f"ys_stored{i}"), (regs[l] + 1 + before(regs, l)) * 16)
    sp.nop().then_inc(S("ys_complete"), 1)


def pe_moe(pe, B, l, regs):
    S, bank, R = B.sem, B.bank, B.rt
    pe.wait_ge(S("router_loaded"), 64 * (l + 1))
    pe.wait_ge(S("norm_done"), 2 + 3 * l)
    for t, rows in TT:
        for k in range(KT):
            mm = pe.matmul(bank[2][0:rows, t * 20:(t + 1) * 20], B.fT[:, k, cols(t)], B.wr[:, k, :], start=k == 0, stop=k == KT - 1)
    mm.then_inc(S("route_mm"), 1)
    for q in range(10):
        t, rows = TT[q // 2]
        if q >= 7:
            pe.wait_ge(S("h_ev"), 10 * l + q - 6)
        for k in range(4):
            mm = pe.transpose(bank[(q % 7 + 3) % 8][0:rows, k * 128:(k + 1) * 128], B.fT[:, q % 2 * 4 + k, cols(t)], B.ident[:])
        mm.then_inc(S("h_tr"), 1)
    pe.wait_ge(S("route_step"), 4 * l + 3)
    for t, rows in TT:
        c = slice(t * 16, (t + 1) * 16)
        pe.matmul(bank[2][:, c], B.upper[:], R["m"][:, t], start=True, stop=False)
        pe.matmul(bank[2][:, c], B.ones[:], R["before"][:, t], start=False, stop=True)
    for q, m in enumerate([R["before"], R["m"]]):
        mm = pe.matmul(bank[2][:, 80:96], B.ones[:], m[:, 4], start=q == 0, stop=q == 1)
    mm.then_inc(S("route_mm"), 1)
    pe.wait_ge(S("route_step"), 4 * l + 4)
    regs.append(pe.value_load(B.pairs[l][0:1, 0:1], min_val=E_N // 2 - 1, max_val=SLOTS // 2 - 1))

    def turn(i, n):
        pe.wait_ge(S(f"xs_loaded{i}"), n * 16 + 16)
        for h in range(2):
            for k in range(4):
                mm = pe.transpose(bank[6 + h][:, k * C:(k + 1) * C], B.xs[i][:, (4 * h + k) * 128:(4 * h + k + 1) * 128], B.ident[0:C, 0:C])
            mm.then_inc(S("x_tr"), 1)

    def slot(i, t, first, last):
        n = t + before(regs, l)
        s = n * 2 + i
        pe.wait_ge(S("xt_ev"), s * 2 + 2)
        pe.wait_ge(S(f"wgu_loaded{i}"), n * 32 + 32)
        for m in range(4):
            if m >= 2:
                pe.wait_ge(S("act_ready"), s * 4 + (m - 1))
            c = slice(m // 2 * C, (m // 2 + 1) * C)
            for w, b, done in [(B.wg[i], 0, "gate_mm"), (B.wu[i], 1, "up_mm")]:
                for k in range(KT):
                    mm = pe.matmul(bank[m % 2 * 2 + b][:, c], w[:, k, m * 128:(m + 1) * 128], B.xsT[:, k], start=k == 0, stop=k == KT - 1)
                mm.then_inc(S(done), 1)
        if not last:
            turn(1 - i, n + i)
        pe.wait_ge(S("act_ready"), s * 4 + 4)
        pe.wait_ge(S(f"wd_loaded{i}"), n * 16 + 16)
        if not (first and i == 0):
            pe.wait_ge(S("ys_ev"), s * 2)
        for h in range(2):
            for k in range(4):
                mm = pe.matmul(bank[4 + h][0:C, :], B.act[:, k], B.wd[i][:, k, h * 512:(h + 1) * 512], start=k == 0, stop=k == 3)
            mm.then_inc(S("down_mm"), 1)

    turn(0, before(regs, l))
    slots(pe, regs, l, slot)
    for q in range(10):
        t, rows = TT[q // 2]
        if q % 2 == 0:
            pe.wait_ge(S("y_sum"), 5 * l + t + 1)
        if q >= 8:
            pe.wait_ge(S("y_added"), 10 * l + q - 7)
        for k in range(4):
            kk = q % 2 * 4 + k
            mm = pe.transpose(bank[q % 8][:, k * 128:k * 128 + rows], B.ga[t % 2 * 2 + 1][0:rows, kk * 128:(kk + 1) * 128],
                              B.ident[0:rows, 0:rows])
        mm.then_inc(S("y_tr"), 1)


def act_moe(act, B, l, regs):
    S, bank, R = B.sem, B.bank, B.rt

    def keep_tokens(q):
        t, rows = TT[q // 2]
        act.wait_ge(S("h_tr"), 10 * l + q + 1)
        act.activation(B.htok[t][0:rows, q % 2 * 512:q % 2 * 512 + 512], bank[(q % 7 + 3) % 8][0:rows, :], ACT.Copy).then_inc(S("h_ev"), 1)

    act.wait_ge(S("route_step"), 4 * l + 1)
    act.activation(R["eg"][:], R["eg"][:], ACT.Exp).then_inc(S("route_exped"), 1)
    for q in range(8):
        keep_tokens(q)
    act.wait_ge(S("route_step"), 4 * l + 2)
    act.activation(R["ew"][:], R["ew"][:], ACT.Exp).then_inc(S("route_exped"), 1)
    for q in range(8, 10):
        keep_tokens(q)
    act.wait_ge(S("route_step"), 4 * l + 4)
    regs.append(act.value_load(B.pairs[l][0:1, 0:1], min_val=E_N // 2 - 1, max_val=SLOTS // 2 - 1))

    def keep_turned(s):
        act.wait_ge(S("x_tr"), s * 2 + 2)
        act.activation(B.xsT[:, 4:8], bank[7][:, 0:4 * C].rearrange("p (k c) -> p k c", k=4), ACT.Copy).then_inc(S("xt_ev"), 1)

    def slot(i, t, first, last):
        n = t + before(regs, l)
        s = n * 2 + i
        for m in range(4):
            act.wait_ge(S("gate_mm"), s * 4 + (m + 1))
            act.activation(B.act[:, m], bank[m % 2 * 2][:, m // 2 * C:(m // 2 + 1) * C], ACT.Silu).then_inc(S("silu_done"), 1)
        if not last:
            keep_turned(s + 1)
        act.wait_ge(S("down_mm"), s * 2 + 2)
        if not first:
            act.wait_ge(S(f"ys_stored{i}"), n * 16)
        act.activation(B.ys[i][:, 512:1024], bank[5][0:C, :], ACT.Copy).then_inc(S("ys_ev"), 1)
        act.wait_ge(S("ys_ev"), s * 2 + 2)
        act.dma_start(B.y_slots.rearrange("(s c) n -> c s n", c=C)[:, bass.ds(t * 2 + i, 1), :].rearrange("c s n -> c (s n)"), B.ys[i][:])\
            .then_inc(S(f"ys_stored{i}"), 16)

    keep_turned(before(regs, l) * 2)
    slots(act, regs, l, slot)


def slots(eng, regs, l, slot):
    slot(0, 0, True, False)
    slot(1, 0, True, False)
    with eng.Fori(1, regs[l]) as t:
        for i in range(2):
            slot(i, t, False, False)
    slot(0, regs[l], False, False)
    slot(1, regs[l], False, True)


def first_max(dve, R, value, top, out, n):
    dve.tensor_tensor(R["eqt"][:, :, 0:n], value, top[:].to_broadcast([128, 5, n]), ALU.is_equal)
    dve.memset(R["rem"][:], 1.0)
    dve.drain()
    for j in range(n):
        dve.tensor_tensor(out[:, :, j:j + 1], R["eqt"][:, :, j:j + 1], R["rem"][:], ALU.mult)
        dve.drain()
        dve.tensor_tensor(R["rem"][:], R["rem"][:], out[:, :, j:j + 1], ALU.subtract)
        dve.drain()


def dve_moe(dve, B, l, regs):
    S, bank, R, N = B.sem, B.bank, B.rt, B.cnt
    tt, ts = dve.tensor_tensor, dve.tensor_scalar
    ts(B.row_ok[:], B.idx[:, 0:1], 0.0, None, ALU.mult)
    dve.drain()
    dve.memset(B.row_ok[0:NS], 1.0)
    dve.wait_ge(S("router_loaded"), 64 * (l + 1))
    dve.memset(B.lg[:], 0.0)
    dve.drain()
    dve.wait_ge(S("route_mm"), 2 * l + 1)
    tt(B.lg[:, 0:4], bank[2][:, 0:80].rearrange("p (t c) -> p t c", t=4), B.br[:].unsqueeze(1).to_broadcast([128, 4, 20]), ALU.add)
    tt(B.lg[0:NS, 4], bank[2][0:NS, 80:100], B.br[0:NS], ALU.add)
    dve.drain()
    dve.tensor_reduce(R["gmax"][:], B.lg[:, :, 0:4], AX.X, ALU.max)
    dve.drain()
    tt(R["eg"][:], B.lg[:, :, 0:4], R["gmax"][:].to_broadcast([128, 5, 4]), ALU.subtract).then_inc(S("route_step"), 1)
    first_max(dve, R, B.lg[:, :, 0:4], R["gmax"], R["gm"], 4)
    tt(R["sel"][:].rearrange("p t (g e) -> p t g e", g=4), B.lg[:, :, 4:20].rearrange("p t (g e) -> p t g e", g=4),
       R["gm"][:].unsqueeze(3).to_broadcast([128, 5, 4, 4]), ALU.mult)
    dve.drain()
    dve.tensor_reduce(R["ing"][:], R["sel"][:].rearrange("p t (g e) -> p t e g", g=4), AX.X, ALU.add)
    dve.drain()
    dve.tensor_reduce(R["v1"][:], R["ing"][:], AX.X, ALU.max)
    dve.drain()
    first_max(dve, R, R["ing"][:], R["v1"], R["o1"], 4)
    dve.scalar_tensor_tensor(out=R["in2"][:], in0=R["o1"][:], scalar=NEG, in1=R["ing"][:], op0=ALU.mult, op1=ALU.add)
    dve.drain()
    dve.tensor_reduce(R["v2"][:], R["in2"][:], AX.X, ALU.max)
    dve.drain()
    tt(R["ew"][:], R["v2"][:], R["v1"][:], ALU.subtract).then_inc(S("route_step"), 1)
    first_max(dve, R, R["in2"][:], R["v2"], R["o2"], 4)
    for m, o in [("m1", "o1"), ("m2", "o2")]:
        tt(R[m][:].rearrange("p t (g e) -> p t g e", g=4), R["gm"][:].unsqueeze(3).to_broadcast([128, 5, 4, 4]),
           R[o][:].unsqueeze(2).to_broadcast([128, 5, 4, 4]), ALU.mult)
    dve.memset(R["before"][:, 0], 0.0)
    dve.drain()
    tt(R["m"][:], R["m1"][:], R["m2"][:], ALU.add)
    dve.drain()
    ts(R["m"][:, 4], R["m"][:, 4], B.row_ok[:, 0:1], None, ALU.mult)
    for t in range(1, 5):
        tt(R["before"][:, t], R["before"][:, t - 1], R["m"][:, t - 1], ALU.add)
        dve.drain()
    dve.nop().then_inc(S("route_step"), 1)
    dve.wait_ge(S("route_exped"), 2 * l + 1)
    dve.tensor_reduce(R["sum"][:], R["eg"][:], AX.X, ALU.add)
    dve.drain()
    dve.reciprocal(R["sum"][:], R["sum"][:])
    dve.wait_ge(S("route_exped"), 2 * l + 2)
    ts(R["w1"][:], R["ew"][:], 1.0, None, ALU.add)
    dve.drain()
    dve.reciprocal(R["w1"][:], R["w1"][:])
    dve.drain()
    tt(R["w1"][:], R["w1"][:], R["sum"][:], ALU.mult)
    dve.drain()
    tt(R["w2"][:], R["w1"][:], R["ew"][:], ALU.mult)
    dve.wait_ge(S("route_mm"), 2 * l + 2)
    dve.tensor_copy(N["count"][:], bank[2][:, 80:96])
    dve.memset(N["extra"][:], 0.0)
    dve.drain()
    for j in range(1, T // C + 1):
        ts(N["t"][:], N["count"][:], float(j * C), None, ALU.is_gt)
        dve.drain()
        tt(N["extra"][:], N["extra"][:], N["t"][:], ALU.add)
        dve.drain()
    src, dst = N["extra"], N["a"]
    for d in (1, 2, 4, 8):
        tt(dst[:, d:16], src[:, d:16], src[:, 0:16 - d], ALU.add)
        dve.tensor_copy(dst[:, 0:d], src[:, 0:d])
        dve.drain()
        src, dst = dst, N["b"] if dst is N["a"] else N["a"]
    upto = src
    over = upto[:, 15:16]
    dve.tensor_copy(B.slot_ef[:, 0:16], B.idx[:, 0:16])
    n = SLOTS - 16
    tt(B.cmp[:, 0:n], upto[:].unsqueeze(1).to_broadcast([128, n, 16]), B.idx[:, 0:n].unsqueeze(2).to_broadcast([128, n, 16]), ALU.is_le)
    tt(N["base"][:], upto[:], N["extra"][:], ALU.subtract)
    dve.scalar_tensor_tensor(out=N["t"][:], in0=B.idx[:, 0:16], scalar=2.0, in1=over.to_broadcast([128, 16]), op0=ALU.mult, op1=ALU.is_lt)
    dve.drain()
    dve.tensor_reduce(B.slot_ef[:, 16:SLOTS], B.cmp[:, 0:n], AX.X, ALU.add)
    dve.tensor_reduce(B.pairs_f[:], N["t"][:], AX.X, ALU.add)
    ts(N["base"][:], N["base"][:], 15.0, None, ALU.add)
    dve.drain()
    ts(B.slot_ef[:], B.slot_ef[:], float(E_N - 1), None, ALU.min)
    ts(B.pairs_f[:], B.pairs_f[:], float(E_N // 2 - 1), None, ALU.add)
    tt(N["base"][:], N["base"][:], B.idx[:, 0:16], ALU.subtract)
    ts(R["over"][:], bank[2][:, 0:80].rearrange("p (t c) -> p t c", t=5), float(C), None, ALU.is_ge)
    dve.drain()
    dve.tensor_copy(B.slot_e[:], B.slot_ef[:])
    dve.tensor_copy(B.pairs[l][:], B.pairs_f[:])
    tt(R["place"][:], R["over"][:], N["base"][:].unsqueeze(1).to_broadcast([128, 5, 16]), ALU.mult)
    dve.drain()
    tt(R["place"][:], R["place"][:], B.idx[:, 0:16].unsqueeze(1).to_broadcast([128, 5, 16]), ALU.add)
    dve.drain()
    dve.scalar_tensor_tensor(out=R["place"][:], in0=R["place"][:], scalar=float(C), in1=bank[2][:, 0:80].rearrange("p (t c) -> p t c", t=5),
                             op0=ALU.mult, op1=ALU.add)
    dve.drain()
    for j, m in enumerate(["m1", "m2"]):
        tt(R["t16"][:], R["place"][:], R[m][:], ALU.mult)
        dve.drain()
        dve.tensor_reduce(R["pos"][:, :, j:j + 1], R["t16"][:], AX.X, ALU.add)
        dve.drain()
    dve.tensor_copy(B.pos[:], R["pos"][:])
    dve.drain()
    dve.nop().then_inc(S("route_step"), 1)
    regs.append(dve.value_load(B.pairs[l][0:1, 0:1], min_val=E_N // 2 - 1, max_val=SLOTS // 2 - 1))

    def keep_turned(s):
        dve.wait_ge(S("x_tr"), s * 2 + 1)
        dve.tensor_copy(B.xsT[:, 0:4], bank[6][:, 0:4 * C].rearrange("p (k c) -> p k c", k=4)).then_inc(S("xt_ev"), 1)

    def slot(i, t, first, last):
        n = t + before(regs, l)
        s = n * 2 + i
        for m in range(4):
            dve.wait_ge(S("silu_done"), s * 4 + (m + 1))
            dve.wait_ge(S("up_mm"), s * 4 + (m + 1))
            tt(B.act[:, m], bank[m % 2 * 2 + 1][:, m // 2 * C:(m // 2 + 1) * C], B.act[:, m], ALU.mult).then_inc(S("act_ready"), 1)
        if not last:
            keep_turned(s + 1)
        dve.wait_ge(S("down_mm"), s * 2 + 1)
        if not first:
            dve.wait_ge(S(f"ys_stored{i}"), n * 16)
        dve.tensor_copy(B.ys[i][:, 0:512], bank[4][0:C, :]).then_inc(S("ys_ev"), 1)

    keep_turned(before(regs, l) * 2)
    slots(dve, regs, l, slot)
    gate = mod(B, l, 5)
    for t in range(6):
        if t < 5:
            rows = TT[t][1]
            a, b = B.ga[t % 2 * 2][0:rows], B.ga[t % 2 * 2 + 1][0:rows]
            dve.wait_ge(S(f"gathered{t % 2}"), 32 * ((3, 2)[t % 2] * l + t // 2 + 1))
            ts(a, a, R["w1"][0:rows, t, 0:1], None, ALU.mult)
            dve.drain()
            dve.scalar_tensor_tensor(out=b, in0=b, scalar=R["w2"][0:rows, t, 0:1], in1=a, op0=ALU.mult, op1=ALU.add).then_inc(S("y_sum"), 1)
        if t >= 1:
            for h in range(2):
                q = 2 * (t - 1) + h
                dve.wait_ge(S("y_tr"), 10 * l + q + 1)
                ps = bank[q % 8]
                if t - 1 < 4:
                    for k in range(4):
                        dst = B.xT[:, 4 * h + k, cols(t - 1)]
                        ins = dve.scalar_tensor_tensor(out=dst, in0=ps[:, k * 128:(k + 1) * 128], scalar=gate[:, 4 * h + k, 0:1], in1=dst,
                                                       op0=ALU.mult, op1=ALU.add)
                else:
                    for k in range(4):
                        tmp = B.tmp_s[:, k % 2]
                        tt(tmp.rearrange("p (b s) -> p b s", s=DS), ps[:, k * 128:k * 128 + NS].rearrange("p (b s) -> p b s", s=DS),
                           gate[:, 4 * h + k, 1:NC].unsqueeze(2).to_broadcast([128, DB, DS]), ALU.mult)
                        dve.drain()
                        ins = tt(B.xT[:, 4 * h + k, SEQ:T], B.xT[:, 4 * h + k, SEQ:T], tmp, ALU.add)
                ins.then_inc(S("y_added"), 1)
    dve.drain()
    dve.nop().then_inc(S("x_ready"), 1)


NCP, NCS = 31, 15
NCK = DB * NCS
CK = 4 * NCK + 4 * NCP
SK = PAST + NS
TABLE = {}
_at = 0
for _n, _w in [("dist_p", 512), ("dist_c", 4 * NCP), ("row_valid", 4), ("dist_s", 2 * SK), ("dist_cs", 2 * NCK), ("spread", 256),
               ("head_sel", 4), ("slope", 4)]:
    TABLE[_n] = (_at, _at + _w)
    _at += _w
TABLE_W = _at
FAR = 1.0e32


def slope_of(h):
    return 2.0 ** (-8.0 * (h + 1) / NH)


def shape_table():
    import numpy as np
    tab = np.zeros((128, TABLE_W), np.float32)
    p = np.arange(128)

    def put(name, value):
        a, b = TABLE[name]
        tab[:value.shape[0], a:b] = value.reshape(value.shape[0], -1)

    d = p[:, None] - np.arange(512)[None] + 384
    put("dist_p", np.where(d >= 0, d, FAR))
    q = np.arange(4)[None, :, None] * 128 + p[:, None, None]
    d = q - (16 * np.arange(NCP)[None, None] + 31)
    put("dist_c", np.where(d >= 0, d, FAR))
    put("row_valid", (q[:, :, 0] >= 31).astype(np.float32))
    b4, hg, t = p // 32, p % 16 // 4, p % 4
    bq = np.arange(2)[None, :, None]
    past = (PAST + t)[:, None, None] - np.arange(PAST)[None, None] + 0 * bq
    new = np.arange(NS)[None, None]
    own = (new // DS == 4 * bq + b4[:, None, None]) & (new % DS <= t[:, None, None])
    put("dist_s", np.concatenate([past, np.where(own, t[:, None, None] - new % DS, FAR)], 2))
    c = np.arange(NCK)[None, None]
    d = (PAST + t)[:, None, None] - (16 * (c % NCS) + 31)
    put("dist_cs", np.where(c // NCS == 4 * bq + b4[:, None, None], d, FAR))
    tok = np.arange(NS)[:, None, None]
    put("spread", (tok == (4 * bq[0][None] + b4[None, None]) * DS + t[None, None]).astype(np.float32))
    put("head_sel", (hg[:, None] == np.arange(HG)[None]).astype(np.float32))
    put("slope", np.stack([-2.0 ** (-8.0 * (HG * g + hg + 1) / NH) for g in range(G)], 1))
    return tab


def allocate_nsa(nc, B, sb):
    kv = ExitStack()
    B.kvtok = sb(kv, "kvtok", [128, 5, 1536])
    B.kT = sb(kv, "kT", [128, 2, 2, T])
    B.kcT = sb(kv, "kcT", [128, 2, NCK + NCP])
    B.vcs = sb(kv, "vcs", [NCK, G, HD])
    B.vcp = sb(kv, "vcp", [NCP, G, HD])
    B.tab = sb(kv, "tab", [128, TABLE_W])
    B.pages = sb(kv, "pages", [1, 16], I32)
    B.pbr = sb(kv, "pbr", [36, 128])
    B.pbT = sb(kv, "pbT", [128, 36])
    B.posb = sb(kv, "posb", [128, 4])
    B.cw2 = sb(kv, "cw2", [128, 2, 2, HD])
    past = ExitStack()
    B.cs = sb(past, "cs", [128, 8, 16, HD])
    st = ExitStack()
    B.wkv = sb(st, "wkv", [128, KT, 1536])
    st.close()
    st = ExitStack()
    B.cp = sb(st, "cp", [64, G, 16, HD])
    B.kvT = sb(st, "kvT", [128, G, 8, 160])
    B.cw1 = sb(st, "cw1", [128, 16, 256])
    B.hid = sb(st, "hid", [128, 2, CK])
    st.close()
    past.close()
    B.kTs = sb(kv, "kTs", [128, 2, 2, DB, PAST])
    B.vp = sb(kv, "vp", [128, 2, 16, 256])
    B.qT = sb(kv, "qT", [128, KT, T])
    B.gates = sb(kv, "gates", [128, 5, 48])
    B.gs = sb(kv, "gs", [128, 2, G, 3])
    B.gtmp = sb(kv, "gtmp", [128, 2, 48])
    B.qs = sb(kv, "qs", [128, 2, DB, 32])
    st = ExitStack()
    B.kp = sb(st, "kp", [128, 16, 256])
    B.wq = [sb(st, f"wq{i}", [128, KT, 128]) for i in range(2)]
    B.wgt = sb(st, "wgt", [128, KT, 48])
    st.close()
    st = ExitStack()
    B.sc = [sb(st, f"sc{i}", [128, 2, 512]) for i in range(3)]
    B.PT = [sb(st, f"PT{i}", [128, 2, 512]) for i in range(2)]
    B.nm = [sb(st, f"nm{i}", [128, 3]) for i in range(2)]
    B.sm = [sb(st, f"sm{i}", [128, 3]) for i in range(2)]
    B.scc = [sb(st, f"scc{i}", [128, 4, NCP]) for i in range(2)]
    B.nmc = sb(st, "nmc", [128, 4])
    B.smc = sb(st, "smc", [128, 4])
    B.PTc = [sb(st, f"PTc{i}", [NCP, 512]) for i in range(2)]
    st.close()
    kv.close()
    st = ExitStack()
    B.ytok = sb(st, "ytok", [128, 5, D])
    st.close()


def table(B, name, rows=128):
    a, b = TABLE[name]
    return B.tab[0:rows, a:b]


def gslice(g):
    return slice(64 * (g % 2), 64 * (g % 2) + 64), g // 2


def sp_kv(nc, sp, B, io, out):
    S = B.sem
    sp.wait_ge(S("x_ready"), 2)
    for c in range(3):
        sp.dma_start(B.wkv[:, :, c * 512:(c + 1) * 512], io["w_kv"][:, c * 512:(c + 1) * 512].rearrange("(k p) n -> p k n", p=128))\
          .then_inc(S("wkv_loaded"), 16)
    sp.dma_start(B.tab[:], io["table"]).then_inc(S("small_loaded"), 16)
    sp.dma_start(B.pages[:], io["page_table"].rearrange("b n -> (b n)").rearrange("(a n) -> a n", a=1)).then_inc(S("pages_loaded"), 16)
    sp.dma_start(B.pbr[0:32], io["cmp_pos"].rearrange("z (c l) d -> (z c) (l d)", l=2)).then_inc(S("small_loaded"), 16)
    sp.dma_start(B.pbr[32:36], io["cmp_b1"].rearrange("z (m p) -> (z m) p", p=128)).then_inc(S("small_loaded"), 16)
    sp.dma_start(B.cw2[:], io["cmp_w2"].rearrange("z (m p) d -> p z m d", p=128)).then_inc(S("small_loaded"), 16)
    for src, dst in [(io["cache_win_kv"], out["win_sample"][:, 0:PAST])]:
        sp.dma_start(dst.rearrange("b t s g d -> b t (s g d)"), src.rearrange("b t s g d -> b t (s g d)")).then_inc(S("kv_stored"), 16)
    sp.wait_ge(S("pages_loaded"), 16)
    for q in range(16):
        page = sp.value_load(B.pages[0:1, q:q + 1], min_val=0, max_val=NPOOL - 1)
        rows = io["cache_nsa_kv"][bass.ds(page, 1)].rearrange("a (n l) s g d -> (a n) l (s g) d", l=16)
        for c in range(8):
            sp.dma_start(B.cs[8 * q:8 * q + 8, c], rows[:, :, c, :]).then_inc(S("cs_loaded"), 16)
    sp.wait_ge(S("kv_ev"), 15)
    sp.dma_start(out["kv_prompt"].rearrange("b (t p) s g d -> p (b t) (s g d)", p=128), B.kvtok[:, 0:4, 0:1024]).then_inc(S("stored"), 16)
    sp.dma_start(out["win_prompt"].rearrange("b (t p) s g d -> p (b t) (s g d)", p=128), B.kvtok[:, 0:4, 1024:1536]).then_inc(S("kv_stored"), 16)
    sp.dma_start(out["kv_sample"].rearrange("b t s g d -> (b t) (s g d)"), B.kvtok[0:NS, 4, 0:1024]).then_inc(S("kv_stored"), 16)
    for b in range(DB):
        sp.dma_start(out["win_sample"][b, PAST:PAST + DS].rearrange("t s g d -> t (s g d)"), B.kvtok[b * DS:(b + 1) * DS, 4, 1024:1536])\
          .then_inc(S("kv_stored"), 16)
    sp.dma_start(B.cw1[:], io["cmp_w1"][0].rearrange("(c p) h -> p c h", p=128)).then_inc(S("cw1_loaded"), 16)
    sp.wait_ge(S("stored"), 48)
    rows = out["kv_prompt"].rearrange("b (n l) s g d -> (b n) l s g d", l=16)
    for z in range(2):
        for g in range(G):
            sp.dma_start(B.cp[32 * z:32 * z + 32, g], rows[:, :, z, g, :]).then_inc(S("cs_loaded"), 16)
    sp.wait_ge(S("hid_mm"), 1)
    sp.dma_start(B.cw1[:], io["cmp_w1"][1].rearrange("(c p) h -> p c h", p=128)).then_inc(S("cw1_loaded"), 16)
    sp.wait_ge(S("cmp_done"), 1)
    def load_past(tile, s, br, done):
        for q in range(16):
            if br:
                row = io["cache_win_kv"][q // 2:q // 2 + 1, q % 2 * 128:q % 2 * 128 + 128, s]
            else:
                page = sp.value_load(B.pages[0:1, q:q + 1], min_val=0, max_val=NPOOL - 1)
                row = io["cache_nsa_kv"][bass.ds(page, 1), :, 2 + s]
            sp.dma_start(tile[:, q, :], row.rearrange("a t g d -> t (a g d)")).then_inc(S(done), 16)

    w_q = io["nsa_w_qg"][0, :, 0:D].rearrange("(k p) (gp g2 hg d) -> p k gp g2 hg d", p=128, gp=2, g2=2, hg=HG)

    def load_wq(j):
        for g2 in range(2):
            sp.dma_start(B.wq[j % 2][:, :, g2 * HD:(g2 + 1) * HD], w_q[:, :, j // 4, g2, j % 4, :]).then_inc(S(f"wq_loaded{j % 2}"), 16)

    load_past(B.kp, 0, 0, "kp_loaded")
    load_wq(0)
    load_wq(1)
    sp.wait_ge(S("kts_tr"), 8)
    load_past(B.kp, 0, 1, "kp_loaded")
    sp.dma_start(B.wgt[:], io["nsa_w_qg"][0, :, D:D + 48].rearrange("(k p) n -> p k n", p=128)).then_inc(S("wgt_loaded"), 16)
    for j in range(2, KT):
        sp.wait_ge(S("q_mm"), 2 * (j - 1))
        load_wq(j)
    for br in range(2):
        load_past(B.vp[:, br], 1, br, "vp_loaded")


def pe_kv(pe, B):
    S, bank, ident = B.sem, B.bank, B.ident
    pe.wait_ge(S("wkv_loaded"), 48)
    pe.wait_ge(S("norm_done"), 3)
    for n in range(15):
        t, c = n // 3, n % 3
        rows = TT[t][1]
        if n >= 8:
            pe.wait_ge(S("kv_ev"), n - 7)
        for k in range(KT):
            mm = pe.matmul(bank[n % 8][0:rows, :], B.fT[:, k, cols(t)], B.wkv[:, k, c * 512:(c + 1) * 512], start=k == 0, stop=k == KT - 1)
        mm.then_inc(S("kv_mm"), 1)
    pe.wait_ge(S("kv_ev"), 15)
    for n in range(4):
        br, gp = n // 2, n % 2
        at = (2 + 2 * br) * 256 + gp * 128
        for t in range(4):
            mm = pe.transpose(bank[n][:, t * 128:(t + 1) * 128], B.kvtok[:, t, at:at + 128], ident[:])
        mm.then_inc(S("kt_tr"), 1)
    for n in range(4):
        at = (2 + 2 * (n // 2)) * 256 + n % 2 * 128
        pe.transpose(bank[4][:, n * NS:(n + 1) * NS], B.kvtok[0:NS, 4, at:at + 128], ident[0:NS, 0:NS])
    pe.wait_ge(S("small_loaded"), 64)
    pe.transpose(bank[4][:, 128:164], B.pbr[:], ident[0:36, 0:36]).then_inc(S("kt_tr"), 1)
    pe.wait_ge(S("kt_ev"), 5)
    pe.wait_ge(S("cs_loaded"), 16 * 136)
    for z in range(2):
        for n in range(16):
            a = 16 * z + n
            if a >= 8:
                pe.wait_ge(S("kvt_ev"), a - 7)
            if z and n == 0:
                pe.wait_ge(S("cmp_ev"), 1)
                pe.wait_ge(S("hid_ev"), 4)
            for q in range(2):
                g, lp = (2 * n + q) // 8, (2 * n + q) % 8
                cz = slice(32 * z, 32 * z + 32)
                pe.transpose(bank[n % 8][:, q * 160:q * 160 + 128], B.cs[:, 4 * z + g, 2 * lp:2 * lp + 2].rearrange("p l d -> p (l d)"), ident[:])
                mm = pe.transpose(bank[n % 8][:, q * 160 + 128:q * 160 + 160], B.cp[cz, g, 2 * lp:2 * lp + 2].rearrange("p l d -> p (l d)"),
                                  ident[cz, cz])
            mm.then_inc(S("kvt_tr"), 1)
        pe.wait_ge(S("kvt_ev"), 16 * (z + 1))
        pe.wait_ge(S("cw1_loaded"), 16 * (z + 1))
        for m in range(2):
            for c in range(16):
                mm = pe.matmul(bank[4][:, m:m + 1], B.cw1[:, c, m * 128:(m + 1) * 128], B.pbT[:, z * 16 + c:z * 16 + c + 1],
                               start=c == 0, stop=c == 15)
        mm.then_inc(S("pos_mm"), 1)
        for m in range(2):
            for part in range(2):
                for c in range(16):
                    r, lp = c // 8, c % 8
                    v = B.kvT[:, :, lp, 0:128].rearrange("p g (b n) -> p g b n", b=DB)[:, :, :, r:r + NCS] if part == 0 else \
                        B.kvT[:, :, lp, 128 + r:128 + r + NCP]
                    o = bank[2 * m + part][:, 0:4 * NCK].rearrange("p (g b n) -> p g b n", g=G, b=DB) if part == 0 else \
                        bank[2 * m + part][:, 0:4 * NCP].rearrange("p (g n) -> p g n", g=G)
                    mm = pe.matmul(o, B.cw1[:, c, m * 128:(m + 1) * 128], v, start=c == 0, stop=c == 15)
        mm.then_inc(S("hid_mm"), 1)
        pe.wait_ge(S("hid_ev"), 4 * (z + 1))
        for g in range(G):
            r, gp = gslice(g)
            for part, w in [(0, NCK), (1, NCP)]:
                at = g * NCK if part == 0 else 4 * NCK + g * NCP
                for m in range(2):
                    if z == 0:
                        o = bank[5][r, gp * 151 + part * NCK:gp * 151 + part * NCK + w]
                        mm = pe.matmul(o, B.cw2[:, z, m, :], B.hid[:, m, at:at + w], start=m == 0, stop=m == 1)
                    else:
                        mm = pe.matmul(bank[5 + part][0:w, g * HD:(g + 1) * HD], B.hid[:, m, at:at + w], B.cw2[:, z, m, :],
                                       start=m == 0, stop=m == 1)
        mm.then_inc(S("cmp_mm"), 1)
    pe.wait_ge(S("cmp_ev"), 2)
    for br in range(2):
        pe.wait_ge(S("kp_loaded"), 256 * (br + 1))
        for n in range(8):
            gp, bp = n // 4, n % 4
            if 8 * br + n >= 8:
                pe.wait_ge(S("kts_ev"), 8 * br + n - 7)
            for q in range(4):
                mm = pe.transpose(bank[n][:, q * 128:(q + 1) * 128], B.kp[:, 4 * bp + q, gp * 128:(gp + 1) * 128], ident[:])
            mm.then_inc(S("kts_tr"), 1)
    pe.wait_ge(S("norm_done"), 4)
    for j in range(KT):
        pe.wait_ge(S(f"wq_loaded{j % 2}"), 32 * (j // 2 + 1))
        for h in range(2):
            n = 2 * j + h
            if n >= 8:
                pe.wait_ge(S("q_ev"), n - 7)
            else:
                pe.wait_ge(S("kts_ev"), 9 + n)
            for k in range(KT):
                mm = pe.matmul(bank[n % 8][:, 0:HALF], B.wq[j % 2][:, k, :], B.fT[:, k, half(h)], start=k == 0, stop=k == KT - 1)
            mm.then_inc(S("q_mm"), 1)
    pe.wait_ge(S("wgt_loaded"), 16)
    pe.wait_ge(S("q_ev"), 16)
    for t, rows in TT:
        for k in range(KT):
            mm = pe.matmul(bank[0][0:rows, t * 48:(t + 1) * 48], B.fT[:, k, cols(t)], B.wgt[:, k, :], start=k == 0, stop=k == KT - 1)
    mm.then_inc(S("gates_mm"), 1)
    pe.wait_ge(S("gates_ready"), 1)
    for bq in range(2):
        a = TABLE["spread"][0] + bq * 128
        mm = pe.matmul(bank[1][:, bq * 48:(bq + 1) * 48], B.tab[0:NS, a:a + 128], B.gates[0:NS, 4, :], start=True, stop=True)
    mm.then_inc(S("gates_mm"), 1)
    pe_attend(pe, B)


UNITS = [(h, i) for h in range(NH) for i in range(4)]
SUNITS = [(bq, g) for bq in range(2) for g in range(G)]

NU = len(UNITS)


def unit(h):
    g = h // HG
    r, gp = gslice(g)
    return g, r, gp, gp * 4 + h % HG


def pe_attend(pe, B):
    S, bank, ident = B.sem, B.bank, B.ident
    U = len(UNITS)
    pe.wait_ge(S("gs_ready"), 1)

    def scores(u):
        h, i = UNITS[u]
        g, r, gp, j = unit(h)
        if u >= 2:
            pe.wait_ge(S("sc_ready"), u - 1)
        for br in range(2):
            mm = pe.matmul(bank[2 * (u % 2) + br][:, 0:128 * (i + 1)], B.qT[r, j, i * 128:(i + 1) * 128], B.kT[r, br, gp, 0:128 * (i + 1)],
                           start=True, stop=True)
        mm.then_inc(S("sc_mm"), 1)

    def cmp_scores(h):
        g, r, gp, j = unit(h)
        if h >= 1:
            pe.wait_ge(S("ptc_ev"), h)
        for i in range(4):
            mm = pe.matmul(bank[6][:, i * NCP:(i + 1) * NCP], B.qT[r, j, i * 128:(i + 1) * 128], B.kcT[r, gp, NCK:NCK + NCP],
                           start=True, stop=True)
        mm.then_inc(S("scc_mm"), 1)

    def cmp_turn(h):
        pe.wait_ge(S("pc_ready"), h + 1)
        for i in range(4):
            mm = pe.transpose(bank[6][0:NCP, i * 128:(i + 1) * 128], B.scc[h % 2][:, i, :], ident[:])
        mm.then_inc(S("ptc_tr"), 1)

    def turn(u):
        h, i = UNITS[u]
        pe.wait_ge(S("p_ready"), u + 1)
        if u >= 1:
            pe.wait_ge(S("pt_ev"), u)
        for br in range(2):
            for kt in range(i + 1):
                mm = pe.transpose(bank[4 + br][:, kt * 128:(kt + 1) * 128], B.sc[u % 3][:, br, kt * 128:(kt + 1) * 128], ident[:])
        mm.then_inc(S("pt_tr"), 1)

    def values(u):
        h, i = UNITS[u]
        g, r, gp, j = unit(h)
        pe.wait_ge(S("pt_ev"), u + 1)
        if i == 0:
            pe.wait_ge(S("ptc_ev"), h + 1)
            if h >= 1:
                pe.wait_ge(S("o_ev"), h)
        o = bank[7][r, i * 128:(i + 1) * 128]
        pe.matmul(o, B.vcp[:, g, :], B.PTc[h % 2][:, i * 128:(i + 1) * 128], start=True, stop=False)
        for br in range(2):
            for kt in range(i + 1):
                v = (3 + 2 * br) * 256 + g * HD
                mm = pe.matmul(o, B.kvtok[:, kt, v:v + HD], B.PT[u % 2][:, br, kt * 128:(kt + 1) * 128], start=False,
                               stop=br == 1 and kt == i)
        mm.then_inc(S("pv_mm"), 1)

    for s in range(U + 3):
        if s < U:
            scores(s)
            if UNITS[s][1] == 0:
                cmp_scores(UNITS[s][0])
        if s >= 2 and s - 2 < U:
            turn(s - 2)
            if UNITS[s - 2][1] == 0:
                cmp_turn(UNITS[s - 2][0])
        if s >= 3:
            values(s - 3)
    pe.wait_ge(S("o_ev"), NH)
    pe.wait_ge(S("vp_loaded"), 512)

    def s_scores(u):
        bq, g = SUNITS[u]
        r, gp = gslice(g)
        if u >= 1:
            pe.wait_ge(S("sc_ready"), NU + u)
        for br in range(2):
            b_ = bank[2 * (u % 2) + br]
            for b in range(4):
                pe.matmul(b_[32 * b:32 * b + 32, 0:PAST], B.qs[r, gp, 4 * bq + b, :], B.kTs[r, br, gp, 4 * bq + b, :], start=True, stop=True)
            qall = B.qs[r, gp, 4 * bq:4 * bq + 4, :].rearrange("p b c -> p (b c)")
            pe.matmul(b_[:, PAST:SK], qall, B.kT[r, br, gp, SEQ:T], start=True, stop=True)
        pe.matmul(bank[6][:, 0:NCK], qall, B.kcT[r, gp, 0:NCK], start=True, stop=True).then_inc(S("sc_mm"), 1)

    def s_turn(u):
        pe.wait_ge(S("p_ready"), NU + u + 1)
        if u >= 1:
            pe.wait_ge(S("pt_ev"), NU + u)
        P = s_probs(B, u)
        for br in range(2):
            for kt in range(2):
                pe.transpose(bank[4 + br][:, kt * 128:(kt + 1) * 128], P[br][:, kt * 128:(kt + 1) * 128], ident[:])
            mm = pe.transpose(bank[4 + br][0:NS, 256:384], P[br][:, PAST:SK], ident[:])
        mm = pe.transpose(bank[4][0:NCK, 384:512], P[2], ident[:])
        mm.then_inc(S("pt_tr"), 1)

    def s_values(u):
        bq, g = SUNITS[u]
        r, gp = gslice(g)
        pe.wait_ge(S("pt_ev"), NU + u + 1)
        if u >= 1:
            pe.wait_ge(S("so_ev"), u)
        PT = B.PT[u % 2]
        for b in range(4):
            c = slice(32 * b, 32 * b + 32)
            o = bank[7][r, c]
            pe.matmul(o, B.vcs[:, g, :], PT[0:NCK, 0, 384:512][:, c], start=True, stop=False)
            for br in range(2):
                for kt in range(2):
                    pe.matmul(o, B.vp[:, br, 2 * (4 * bq + b) + kt, g * HD:(g + 1) * HD], PT[:, br, kt * 128:(kt + 1) * 128][:, c],
                              start=False, stop=False)
                v = (3 + 2 * br) * 256 + g * HD
                mm = pe.matmul(o, B.kvtok[0:NS, 4, v:v + HD], PT[0:NS, br, 256:384][:, c], start=False, stop=br == 1)
        mm.then_inc(S("pv_mm"), 1)

    U = len(SUNITS)
    for s in range(U + 3):
        if s < U:
            s_scores(s)
        if s >= 2 and s - 2 < U:
            s_turn(s - 2)
        if s >= 3:
            s_values(s - 3)


def s_probs(B, u):
    v = B.sc[u % 3][:].rearrange("p a b -> p (a b)")
    return [v[:, 0:SK], v[:, SK:2 * SK], v[:, 2 * SK:2 * SK + NCK]]


def act_kv(act, B):
    S, bank = B.sem, B.bank
    for n in range(15):
        act.wait_ge(S("kv_mm"), n + 1)
        rows = TT[n // 3][1]
        act.activation(B.kvtok[0:rows, n // 3, n % 3 * 512:n % 3 * 512 + 512], bank[n % 8][0:rows, :], ACT.Copy).then_inc(S("kv_ev"), 1)
    act_scale(act, B, 3, mod(B, 1, 0))
    for z in range(2):
        act.wait_ge(S("hid_mm"), z + 1)
        act.wait_ge(S("posb_ready"), z + 1)
        if z:
            act.wait_ge(S("cmp_mm"), 1)
        for m in range(2):
            bias = B.posb[:, 2 * z + m:2 * z + m + 1]
            act.activation(B.hid[:, m, 0:4 * NCK], bank[2 * m][:, 0:4 * NCK], ACT.Gelu_apprx_tanh, bias=bias).then_inc(S("hid_ev"), 1)
            act.activation(B.hid[:, m, 4 * NCK:CK], bank[2 * m + 1][:, 0:4 * NCP], ACT.Gelu_apprx_tanh, bias=bias).then_inc(S("hid_ev"), 1)
    for n in range(16):
        act.wait_ge(S("q_mm"), n + 1)
        if n == 0:
            act.wait_ge(S("cmp_done"), 1)
        act.activation(B.qT[:, n // 2, half(n % 2)], bank[n % 8][:, 0:HALF], ACT.Copy, scale=HD ** -0.5).then_inc(S("q_ev"), 1)
    act.wait_ge(S("gates_mm"), 1)
    act.activation(B.gates[:, 0:4].rearrange("p t c -> p (t c)"), bank[0][:, 0:192], ACT.Sigmoid)
    act.activation(B.gates[0:NS, 4], bank[0][0:NS, 192:240], ACT.Sigmoid).then_inc(S("gates_ready"), 1)
    U = len(UNITS)
    for s in range(U + 2):
        if s % 4 == 3 and s > 4:
            act_store_head(act, B, s // 4 - 1)
        if s < U:
            h, i = UNITS[s]
            x = s % 2
            act.wait_ge(S("sc_ready"), s + 1)
            for br in range(2):
                v = B.sc[s % 3][:, br, 0:128 * (i + 1)]
                ins = act.activation(v, v, ACT.Exp, bias=B.nm[x][:, br:br + 1], accum_out=B.sm[x][:, br:br + 1])
            ins.then_inc(S("exp_done"), 1)
            if i == 0:
                act.wait_ge(S("scc_ready"), h + 1)
                act.activation(B.scc[h % 2][:], B.scc[h % 2][:], ACT.Exp).then_inc(S("expc_done"), 1)
        if s >= 2:
            h, i = UNITS[s - 2]
            x = s % 2
            act.wait_ge(S("pt_tr"), s - 1)
            if s >= 4:
                act.wait_ge(S("pv_mm"), s - 3)
            for br in range(2):
                ins = act.activation(B.PT[x][:, br, 0:128 * (i + 1)], bank[4 + br][:, 0:128 * (i + 1)], ACT.Copy)
            ins.then_inc(S("pt_ev"), 1)
            if i == 0:
                act.wait_ge(S("ptc_tr"), h + 1)
                act.activation(B.PTc[h % 2][:], bank[6][0:NCP, :], ACT.Copy).then_inc(S("ptc_ev"), 1)
    act_store_head(act, B, NH - 1)
    U = len(SUNITS)
    for s in range(U + 2):
        if s < U:
            x = s % 2
            act.wait_ge(S("sc_ready"), NU + s + 1)
            for q, col in [(0, 1), (1, 2), (2, 0)]:
                v = s_probs(B, s)[q]
                ins = act.activation(v, v, ACT.Exp, bias=B.nm[x][:, col:col + 1], accum_out=B.sm[x][:, col:col + 1])
            ins.then_inc(S("exp_done"), 1)
        if s >= 2:
            act.wait_ge(S("pt_tr"), NU + s - 1)
            if s >= 4:
                act.wait_ge(S("pv_mm"), NU + s - 3)
            PT = B.PT[s % 2]
            for br in range(2):
                act.activation(PT[:, br, 0:256], bank[4 + br][:, 0:256], ACT.Copy)
                ins = act.activation(PT[0:NS, br, 256:384], bank[4 + br][0:NS, 256:384], ACT.Copy)
            act.activation(PT[0:NCK, 0, 384:512], bank[4][0:NCK, 384:512], ACT.Copy).then_inc(S("pt_ev"), 1)


def act_store_head(act, B, h):
    S = B.sem
    g, r, gp, j = unit(h)
    act.wait_ge(S("pv_mm"), 4 * (h + 1))
    act.activation(B.fT[r, j, 0:SEQ], B.bank[7][r, :], ACT.Copy).then_inc(S("o_ev"), 1)


def dve_kv(dve, B):
    S, bank = B.sem, B.bank
    for n in range(5):
        dve.wait_ge(S("kt_tr"), n + 1)
        if n < 4:
            ins = dve.tensor_copy(B.kT[:, n // 2, n % 2, 0:SEQ], bank[n][:])
        else:
            dve.tensor_copy(B.kT[:, :, :, SEQ:T], bank[4][:, 0:128].rearrange("p (a b n) -> p a b n", a=2, b=2))
            ins = dve.tensor_copy(B.pbT[:], bank[4][:, 128:164])
        ins.then_inc(S("kt_ev"), 1)
    dve.drain()
    dve_norm(dve, B, None, 3, "g_mix1", mod(B, 1, 0), mod(B, 1, 1))
    for z in range(2):
        for n in range(16):
            dve.wait_ge(S("kvt_tr"), 16 * z + n + 1)
            if z and n == 0:
                dve.wait_ge(S("hid_mm"), 1)
            g, lp = 2 * n // 8, 2 * n % 8
            dve.tensor_copy(B.kvT[:, g, lp:lp + 2, :], bank[n % 8][:, 0:320].rearrange("p (q c) -> p q c", q=2)).then_inc(S("kvt_ev"), 1)
        dve.wait_ge(S("pos_mm"), z + 1)
        dve.tensor_tensor(B.posb[:, 2 * z:2 * z + 2], bank[4][:, 0:2], B.pbT[:, 32 + 2 * z:34 + 2 * z], ALU.add).then_inc(S("posb_ready"), 1)
        dve.wait_ge(S("cmp_mm"), z + 1)
        if z == 0:
            ins = dve.tensor_copy(B.kcT[:].rearrange("p a c -> p (a c)"), bank[5][:, 0:302])
        else:
            dve.tensor_copy(B.vcs[:].rearrange("p g d -> p (g d)"), bank[5][0:NCK, 0:256])
            ins = dve.tensor_copy(B.vcp[:].rearrange("p g d -> p (g d)"), bank[6][0:NCP, 0:256])
        ins.then_inc(S("cmp_ev"), 1)
    dve.drain()
    dve.nop().then_inc(S("cmp_done"), 1)
    for n in range(16):
        dve.wait_ge(S("kts_tr"), n + 1)
        gp, bp = n % 8 // 4, n % 4
        dve.tensor_copy(B.kTs[:, n // 8, gp, 2 * bp:2 * bp + 2, :].rearrange("p b t -> p (b t)"), bank[n % 8][:]).then_inc(S("kts_ev"), 1)
    dve.memset(B.qs[:], 0.0)
    dve.drain()
    dve.wait_ge(S("q_ev"), 16)
    for gp in range(2):
        dve.tensor_copy(B.qs[:, gp, :, 0:16].rearrange("p b (h t) -> p b h t", h=HG),
                        B.qT[:, 4 * gp:4 * gp + 4, SEQ:T].rearrange("p h (b t) -> p b h t", b=DB))
    dve.wait_ge(S("gates_mm"), 2)
    sel = table(B, "head_sel").unsqueeze(1).unsqueeze(3).to_broadcast([128, G, HG, 3])
    for bq in range(2):
        dve.tensor_tensor(B.gtmp[:, bq].rearrange("p (g h c) -> p g h c", g=G, h=HG),
                          bank[1][:, bq * 48:(bq + 1) * 48].rearrange("p (g h c) -> p g h c", g=G, h=HG), sel, ALU.mult)
    dve.drain()
    for bq in range(2):
        ins = dve.tensor_reduce(B.gs[:, bq], B.gtmp[:, bq].rearrange("p (g h c) -> p g c h", g=G, h=HG), AX.X, ALU.add)
    ins.then_inc(S("gs_ready"), 1)
    dve_attend(dve, B)


def dve_attend(dve, B):
    S, bank = B.sem, B.bank
    U = len(UNITS)
    a0 = TABLE["dist_p"][0]
    for s in range(U + 1):
        if s < U:
            h, i = UNITS[s]
            x, nk = s % 2, 128 * (i + 1)
            dve.wait_ge(S("sc_mm"), s + 1)
            if s >= 3:
                dve.wait_ge(S("pt_tr"), s - 2)
            for br in range(2):
                dve.scalar_tensor_tensor(out=B.sc[s % 3][:, br, 0:nk], in0=B.tab[:, a0 + 384 - 128 * i:a0 + 512], scalar=-slope_of(h),
                                         in1=bank[2 * x + br][:, 0:nk], op0=ALU.mult, op1=ALU.add)
            dve.drain()
            dve.tensor_reduce(B.nm[x][:, 0:2], B.sc[s % 3][:, :, 0:nk], AX.X, ALU.max, negate=True).then_inc(S("sc_ready"), 1)
            if i == 0:
                C = B.scc[h % 2]
                dve.wait_ge(S("scc_mm"), h + 1)
                if h >= 2:
                    dve.wait_ge(S("ptc_tr"), h - 1)
                dve.scalar_tensor_tensor(out=C[:], in0=table(B, "dist_c").rearrange("p (i n) -> p i n", i=4), scalar=-slope_of(h),
                                         in1=bank[6][:, 0:4 * NCP].rearrange("p (i n) -> p i n", i=4), op0=ALU.mult, op1=ALU.add)
                dve.drain()
                dve.tensor_reduce(B.nmc[:], C[:], AX.X, ALU.max)
                dve.drain()
                dve.tensor_tensor(C[:], C[:], B.nmc[:].unsqueeze(2).to_broadcast([128, 4, NCP]), ALU.subtract).then_inc(S("scc_ready"), 1)
        if s >= 1:
            h, i = UNITS[s - 1]
            x, nk = (s - 1) % 2, 128 * (i + 1)
            dve.wait_ge(S("exp_done"), s)
            dve.reciprocal(B.sm[x][:, 0:2], B.sm[x][:, 0:2])
            dve.drain()
            dve.tensor_tensor(B.sm[x][:, 0:2], B.sm[x][:, 0:2], B.gates[:, i, 3 * h + 1:3 * h + 3], ALU.mult)
            dve.drain()
            for br in range(2):
                v = B.sc[(s - 1) % 3][:, br, 0:nk]
                ins = dve.tensor_scalar(v, v, B.sm[x][:, br:br + 1], None, ALU.mult)
            ins.then_inc(S("p_ready"), 1)
            if i == 0:
                C = B.scc[h % 2]
                dve.wait_ge(S("expc_done"), h + 1)
                dve.tensor_reduce(B.smc[:], C[:], AX.X, ALU.add)
                dve.drain()
                dve.reciprocal(B.smc[:], B.smc[:])
                dve.drain()
                dve.tensor_tensor(B.smc[:], B.smc[:], table(B, "row_valid"), ALU.mult)
                dve.drain()
                dve.tensor_tensor(B.smc[:], B.smc[:], B.gates[:, 0:4, 3 * h], ALU.mult)
                dve.drain()
                dve.tensor_tensor(C[:], C[:], B.smc[:].unsqueeze(2).to_broadcast([128, 4, NCP]), ALU.mult).then_inc(S("pc_ready"), 1)
    U = len(SUNITS)
    ds = table(B, "dist_s").rearrange("p (q k) -> p q k", q=2)
    dcs = table(B, "dist_cs").rearrange("p (q k) -> p q k", q=2)
    dve.wait_ge(S("pt_tr"), len(UNITS))
    for s in range(U + 3):
        if s < U:
            bq, g = SUNITS[s]
            x = s % 2
            sl = table(B, "slope")[:, g:g + 1]
            P = s_probs(B, s)
            dve.wait_ge(S("sc_mm"), NU + s + 1)
            if s >= 3:
                dve.wait_ge(S("pt_tr"), NU + s - 2)
            for q, d, src in [(0, ds, bank[2 * x]), (1, ds, bank[2 * x + 1]), (2, dcs, bank[6])]:
                w = SK if q < 2 else NCK
                dve.scalar_tensor_tensor(out=P[q], in0=d[:, bq], scalar=sl, in1=src[:, 0:w], op0=ALU.mult, op1=ALU.add)
            dve.drain()
            for q, col in [(0, 1), (1, 2), (2, 0)]:
                ins = dve.tensor_reduce(B.nm[x][:, col:col + 1], P[q], AX.X, ALU.max, negate=True)
            ins.then_inc(S("sc_ready"), 1)
        if s >= 1 and s - 1 < U:
            bq, g = SUNITS[s - 1]
            x = (s - 1) % 2
            dve.wait_ge(S("exp_done"), NU + s)
            dve.reciprocal(B.sm[x][:], B.sm[x][:])
            dve.drain()
            dve.tensor_tensor(B.sm[x][:], B.sm[x][:], B.gs[:, bq, g, :], ALU.mult)
            dve.drain()
            for q, col in [(0, 1), (1, 2), (2, 0)]:
                v = s_probs(B, s - 1)[q]
                ins = dve.tensor_scalar(v, v, B.sm[x][:, col:col + 1], None, ALU.mult)
            ins.then_inc(S("p_ready"), 1)
        if s >= 3:
            bq, g = SUNITS[s - 3]
            r, gp = gslice(g)
            dve.wait_ge(S("pv_mm"), NU + s - 2)
            dst = B.fT[r, 4 * gp:4 * gp + 4, SEQ + 16 * bq:SEQ + 16 * bq + 16].rearrange("p h (b t) -> p b h t", b=4)
            src = bank[7][r, 0:128].rearrange("p (b c) -> p b c", b=4)[:, :, 0:16].rearrange("p b (h t) -> p b h t", h=HG)
            dve.tensor_copy(dst, src).then_inc(S("so_ev"), 1)


def sp_rest(nc, sp, B, io, out):
    S = B.sem
    regs = []
    sp.wait_ge(S("pair_done"), PAIRS)
    sp.wait_ge(S("state_stored"), 64 * PAIRS)
    sp.wait_ge(S("stored"), 32)
    w_o = io["rwkv_w_o"][0].rearrange("(k p) n -> p k n", p=128)
    sp_out_proj(sp, B, 0, lambda m: [(None, w_o[:, :, m * 128:(m + 1) * 128])])
    sp_moe(sp, B, io, 0, regs)
    sp_kv(nc, sp, B, io, out)
    sp.wait_ge(S("so_ev"), len(SUNITS))
    sp.wait_ge(S("kv_stored"), 16 * 11)
    w_o1 = io["nsa_w_o"][0].rearrange("(gp g2 hg d) n -> g2 d gp hg n", gp=2, g2=2, hg=HG)

    def rows(m):
        for g2 in range(2):
            for gp in range(2):
                yield (slice(64 * g2, 64 * g2 + 64), slice(4 * gp, 4 * gp + 4)), w_o1[g2, :, gp, :, m * 128:(m + 1) * 128]

    sp_out_proj(sp, B, 1, rows)
    sp_moe(sp, B, io, 1, regs)
    sp.wait_ge(S("y_ev_out"), 10)
    sp.dma_start(out["y_prompt"].rearrange("b (t p) d -> p (b t) d", p=128), B.ytok[:, 0:4, :]).then_inc(S("stored"), 16)
    sp.dma_start(out["y_sample"].rearrange("b s d -> (b s) d"), B.ytok[0:NS, 4, :]).then_inc(S("stored"), 16)
    sp.wait_ge(S("stored"), 80)


def pe_rest(nc, pe, B, io, out):
    S = B.sem
    regs = []
    pe.wait_ge(S("pair_done"), PAIRS)
    pe_out_proj(pe, B, 0, B.rkv[0], [16 * (m // 4 + 1) for m in range(KT)])
    pe_norm_sum(pe, B, 1)
    pe_moe(pe, B, 0, regs)
    pe_norm_sum(pe, B, 2)
    pe_kv(pe, B)
    pe.wait_ge(S("so_ev"), len(SUNITS))
    pe.wait_ge(S("o_ev"), NH)
    pe_out_proj(pe, B, 1, B.fT, [0] * KT + [32 + 64 * (m // 4 + 1) for m in range(KT)])
    pe_norm_sum(pe, B, 3)
    pe_moe(pe, B, 1, regs)
    pe_norm_sum(pe, B, 4)
    pe.wait_ge(S("norm_done"), 6)
    for n in range(10):
        t, h = n // 2, n % 2
        rows = TT[t][1]
        if n >= 8:
            pe.wait_ge(S("y_ev_out"), n - 7)
        for q in range(4):
            mm = pe.transpose(B.bank[n % 8][0:rows, q * 128:(q + 1) * 128], B.fT[:, 4 * h + q, cols(t)], B.ident[:])
        mm.then_inc(S("y_tr"), 1)


def act_rest(nc, act, B, io, out):
    S = B.sem
    regs = []
    act_norm(act, B, 1)
    act_scale(act, B, 1, mod(B, 0, 3))
    act_moe(act, B, 0, regs)
    act_norm(act, B, 2)
    act_scale(act, B, 2, mod(B, 2, 0))
    act_kv(act, B)
    act_norm(act, B, 3)
    act_scale(act, B, 4, mod(B, 1, 3))
    act_moe(act, B, 1, regs)
    act_norm(act, B, 4)
    for n in range(10):
        act.wait_ge(S("y_tr"), 20 + n + 1)
        rows = TT[n // 2][1]
        act.activation(B.ytok[0:rows, n // 2, n % 2 * 512:n % 2 * 512 + 512], B.bank[n % 8][0:rows, :], ACT.Copy).then_inc(S("y_ev_out"), 1)


def dve_rest(nc, dve, B, io, out):
    S = B.sem
    regs = []
    dve.drain()
    dve_out_proj(dve, B, 0, mod(B, 0, 2))
    dve.drain()
    dve.nop().then_inc(S("x_ready"), 1)
    dve_norm(dve, B, 1, 1, "g_ffn0", mod(B, 0, 3), mod(B, 0, 4))
    dve_moe(dve, B, 0, regs)
    dve_norm(dve, B, 2, 2, "g_kv", mod(B, 2, 0), mod(B, 2, 1))
    dve_kv(dve, B)
    dve.drain()
    dve_out_proj(dve, B, 1, mod(B, 1, 2))
    dve.drain()
    dve.nop().then_inc(S("x_ready"), 1)
    dve_norm(dve, B, 3, 4, "g_ffn1", mod(B, 1, 3), mod(B, 1, 4))
    dve_moe(dve, B, 1, regs)
    dve_norm(dve, B, 4, None, "g_f", None, None)


_OUTS = [("y_prompt", (1, SEQ, D)), ("y_sample", (DB, DS, D)), ("kv_prompt", (1, SEQ, 4, G, HD)), ("kv_sample", (DB, DS, 4, G, HD)),
         ("win_prompt", (1, SEQ, 2, G, HD)), ("win_sample", (DB, PAST + DS, 2, G, HD)), ("wkv_prompt", (1, 1, NH, HD, HD)),
         ("wkv_sample", (1, DB, NH, HD, HD)), ("shift_prompt", (1, 1, D)), ("shift_sample", (1, DB, D))]
_UNUSED = ("rwkv_v0", "rwkv_v1", "rwkv_v2")


def kernel(**inputs):
    import numpy as _np
    import concourse.bacc as _bacc
    from concourse import mybir as _mybir
    from concourse.bass_utils import run_bass_kernel_spmd as _run

    nc = _bacc.Bacc("TRN2", target_bir_lowering=False, num_devices=1)
    arrays, io, out = {}, {}, {}
    for name, value in inputs.items():
        if name in _UNUSED:
            continue
        a = _np.ascontiguousarray(value)
        arrays[f"in_{name}_dram"] = a
        io[name] = nc.dram_tensor(f"in_{name}_dram", a.shape, _mybir.dt.from_np(a.dtype), kind="ExternalInput").ap()
    arrays["in_table_dram"] = shape_table()
    io["table"] = nc.dram_tensor("in_table_dram", (128, TABLE_W), _mybir.dt.float32, kind="ExternalInput").ap()
    for name, shape in _OUTS:
        out[name] = nc.dram_tensor(f"out_{name}_dram", shape, _mybir.dt.float32, kind="ExternalOutput").ap()
    program(nc, io, out)
    r = _run(nc, [arrays], core_ids=[0])
    return tuple(r.results[0][f"out_{name}_dram"] for name, _ in _OUTS)
```
